# Optimizing a Trainium2 kernel written in Bass

```python
import math
import jax, jax.numpy as jnp
from jax import lax
import numpy as np

D_MODEL = 1024
BATCH = 1
SEQ = 512
DEPTH = 2
DEC_BATCH = 8
DEC_SEQ = 16
PAST_LEN = 256

CHUNK = 64
Q_BLOCK = 128
N_A = DEPTH // 2
N_B = DEPTH - N_A
SB_HEADS = 16
SB_HEAD_DIM = D_MODEL // SB_HEADS
SB_WIDTH = SB_HEADS * SB_HEAD_DIM
DA_HEADS = 8
DA_HEAD_DIM = D_MODEL // (2 * DA_HEADS)
DA_V_DIM = 2 * DA_HEAD_DIM
DA_WIDTH = DA_HEADS * DA_V_DIM
DA_QK_WIDTH = DA_HEADS * 2 * DA_HEAD_DIM
ROT_DIM = DA_HEAD_DIM // 4
ROPE_THETA = 500000.0
NORM_EPS = 1e-6
MASK_VALUE = -1e30

kernel_name = "yoco_stickbreak_diffattn_stream_step"

def _rmsnorm(x, g):
    xf = x.astype(jnp.float32)
    y = xf * lax.rsqrt(jnp.mean(xf * xf, axis=-1, keepdims=True) + NORM_EPS)
    return (y * g.astype(jnp.float32)).astype(x.dtype)

def _adaln(c, w, b):
    return jnp.dot(jax.nn.silu(c), w) + b

def _rotary(x, pos):
    half = ROT_DIM // 2
    inv = ROPE_THETA ** (-jnp.arange(0, ROT_DIM, 2, dtype=jnp.float32) / ROT_DIM)
    ang = pos.astype(jnp.float32)[:, None] * inv[None, :]
    cos = jnp.cos(ang)[:, None, None, :]
    sin = jnp.sin(ang)[:, None, None, :]
    xr = x[..., :ROT_DIM].astype(jnp.float32)
    x1, x2 = xr[..., :half], xr[..., half:]
    rot = jnp.concatenate([x1 * cos - x2 * sin, x2 * cos + x1 * sin], axis=-1)
    return jnp.concatenate([rot.astype(x.dtype), x[..., ROT_DIM:]], axis=-1)

def _sweep(fn, q, q_pos):
    b, t = q.shape[0], q.shape[1]
    if t > Q_BLOCK and t % Q_BLOCK == 0:
        n = t // Q_BLOCK
        qb = jnp.moveaxis(q.reshape((b, n, Q_BLOCK) + q.shape[2:]), 1, 0)
        pb = q_pos.reshape(n, Q_BLOCK)
        out = lax.map(lambda a: fn(a[0], a[1]), (qb, pb))
        out = jnp.moveaxis(out, 0, 1)
        return out.reshape((b, t) + out.shape[3:])
    return fn(q, q_pos)

def _sb_block(q, q_pos, k, v, k_pos):
    z = jnp.einsum('bqhd,bkhd->bhqk', q, k, preferred_element_type=jnp.float32) * (SB_HEAD_DIM ** -0.5)
    mask = k_pos[None, :] < q_pos[:, None]
    log_beta = jax.nn.log_sigmoid(z)
    log_stay = jnp.where(mask, jax.nn.log_sigmoid(-z), 0.0)
    later = lax.cumsum(log_stay, axis=3, reverse=True) - log_stay
    a = jnp.where(mask, jnp.exp(log_beta + later), 0.0)
    return jnp.einsum('bhqk,bkhd->bqhd', a, v.astype(jnp.float32)).astype(v.dtype)

def _diff_block(q, q_pos, k, v, k_pos, lam):
    s = jnp.einsum('bqhcd,bkhcd->bhcqk', q, k, preferred_element_type=jnp.float32) * (DA_HEAD_DIM ** -0.5)
    mask = (k_pos[None, :] // CHUNK) <= (q_pos[:, None] // CHUNK)
    s = jnp.where(mask, s, MASK_VALUE)
    p = jax.nn.softmax(s, axis=-1)
    w = p[:, :, 0] - lam * p[:, :, 1]
    return jnp.einsum('bhqk,bkhe->bqhe', w, v.astype(jnp.float32))

def _trunk(x, c, q_pos, k_pos, caches, p):
    b, t, _ = x.shape
    new_ak, new_av = [], []
    for i in range(N_A):
        shift, scale, gate = jnp.split(_adaln(c, p['mod_w_a'][i], p['mod_b_a'][i]), 3, axis=-1)
        h = _rmsnorm(x, p['ln_pre_a'][i]) * (1.0 + scale[:, None, :]) + shift[:, None, :]
        q, k, v, g = jnp.split(jnp.dot(h, p['w_in_a'][i]), 4, axis=-1)
        q = q.reshape(b, t, SB_HEADS, SB_HEAD_DIM)
        k = k.reshape(b, t, SB_HEADS, SB_HEAD_DIM)
        v = v.reshape(b, t, SB_HEADS, SB_HEAD_DIM)
        new_ak.append(k)
        new_av.append(v)
        if caches is None:
            k_all, v_all = k, v
        else:
            k_all = jnp.concatenate([caches[0][i], k], axis=1)
            v_all = jnp.concatenate([caches[1][i], v], axis=1)
        o = _sweep(lambda qb, pb: _sb_block(qb, pb, k_all, v_all, k_pos), q, q_pos)
        y = jnp.dot(o.reshape(b, t, SB_WIDTH) * jax.nn.silu(g), p['w_out_a'][i])
        x = x + gate[:, None, :] * _rmsnorm(y, p['ln_post_a'][i])
    kv_shift, kv_scale = jnp.split(_adaln(c, p['mod_w_kv'], p['mod_b_kv']), 2, axis=-1)
    h = _rmsnorm(x, p['ln_kv']) * (1.0 + kv_scale[:, None, :]) + kv_shift[:, None, :]
    kb, vb = jnp.split(jnp.dot(h, p['w_kv_b']), 2, axis=-1)
    kb = _rotary(kb.reshape(b, t, DA_HEADS, 2, DA_HEAD_DIM), q_pos)
    vb = vb.reshape(b, t, DA_HEADS, DA_V_DIM)
    if caches is None:
        kb_all, vb_all = kb, vb
    else:
        kb_all = jnp.concatenate([caches[2], kb], axis=1)
        vb_all = jnp.concatenate([caches[3], vb], axis=1)
    for j in range(N_B):
        lambda_init = 0.8 - 0.6 * math.exp(-0.3 * (N_A + j))
        shift, scale, gate = jnp.split(_adaln(c, p['mod_w_b'][j], p['mod_b_b'][j]), 3, axis=-1)
        h = _rmsnorm(x, p['ln_pre_b'][j]) * (1.0 + scale[:, None, :]) + shift[:, None, :]
        q, g = jnp.split(jnp.dot(h, p['w_in_b'][j]), [DA_QK_WIDTH], axis=-1)
        q = _rotary(q.reshape(b, t, DA_HEADS, 2, DA_HEAD_DIM), q_pos)
        f32 = jnp.float32
        lam = (jnp.exp(jnp.sum(p['lambda_q1'][j].astype(f32) * p['lambda_k1'][j].astype(f32)))
               - jnp.exp(jnp.sum(p['lambda_q2'][j].astype(f32) * p['lambda_k2'][j].astype(f32)))
               + lambda_init)
        o = _sweep(lambda qb, pb: _diff_block(qb, pb, kb_all, vb_all, k_pos, lam), q, q_pos)
        o = (_rmsnorm(o, p['subln_b'][j]) * (1.0 - lambda_init)).astype(x.dtype)
        y = jnp.dot(o.reshape(b, t, DA_WIDTH) * jax.nn.silu(g), p['w_out_b'][j])
        x = x + gate[:, None, :] * _rmsnorm(y, p['ln_post_b'][j])
    return x, jnp.stack(new_ak, axis=0), jnp.stack(new_av, axis=0), kb, vb

def setup_inputs(seed: int = 0) -> dict:
    key = jax.random.key(seed)
    ks = jax.random.split(key, 32)
    f32 = jnp.float32
    D = D_MODEL
    sd = D ** -0.5

    def nrm(k, shape, s=1.0):
        return jax.random.normal(k, shape, f32) * s

    def gain(k, shape):
        return 1.0 + 0.05 * jax.random.normal(k, shape, f32)

    return {
        "x_prompt": nrm(ks[0], (BATCH, SEQ, D)),
        "x_sample": nrm(ks[1], (DEC_BATCH, DEC_SEQ, D)),
        "c_prompt": nrm(ks[2], (BATCH, D)),
        "c_sample": nrm(ks[3], (DEC_BATCH, D)),
        "cache_a_k": nrm(ks[4], (N_A, DEC_BATCH, PAST_LEN, SB_HEADS, SB_HEAD_DIM)),
        "cache_a_v": nrm(ks[5], (N_A, DEC_BATCH, PAST_LEN, SB_HEADS, SB_HEAD_DIM)),
        "cache_b_k": nrm(ks[6], (DEC_BATCH, PAST_LEN, DA_HEADS, 2, DA_HEAD_DIM)),
        "cache_b_v": nrm(ks[7], (DEC_BATCH, PAST_LEN, DA_HEADS, DA_V_DIM)),
        "ln_pre_a": gain(ks[8], (N_A, D)),
        "ln_post_a": gain(ks[9], (N_A, D)),
        "mod_w_a": nrm(ks[10], (N_A, D, 3 * D), sd),
        "mod_b_a": nrm(ks[11], (N_A, 3 * D), 0.02),
        "w_in_a": nrm(ks[12], (N_A, D, 4 * SB_WIDTH), sd),
        "w_out_a": nrm(ks[13], (N_A, SB_WIDTH, D), SB_WIDTH ** -0.5),
        "ln_kv": gain(ks[14], (D,)),
        "mod_w_kv": nrm(ks[15], (D, 2 * D), sd),
        "mod_b_kv": nrm(ks[16], (2 * D,), 0.02),
        "w_kv_b": nrm(ks[17], (D, DA_QK_WIDTH + DA_WIDTH), sd),
        "ln_pre_b": gain(ks[18], (N_B, D)),
        "ln_post_b": gain(ks[19], (N_B, D)),
        "mod_w_b": nrm(ks[20], (N_B, D, 3 * D), sd),
        "mod_b_b": nrm(ks[21], (N_B, 3 * D), 0.02),
        "w_in_b": nrm(ks[22], (N_B, D, DA_QK_WIDTH + DA_WIDTH), sd),
        "w_out_b": nrm(ks[23], (N_B, DA_WIDTH, D), DA_WIDTH ** -0.5),
        "lambda_q1": nrm(ks[24], (N_B, DA_HEAD_DIM), 0.1),
        "lambda_k1": nrm(ks[25], (N_B, DA_HEAD_DIM), 0.1),
        "lambda_q2": nrm(ks[26], (N_B, DA_HEAD_DIM), 0.1),
        "lambda_k2": nrm(ks[27], (N_B, DA_HEAD_DIM), 0.1),
        "subln_b": gain(ks[28], (N_B, DA_V_DIM)),
    }

def reference(x_prompt, x_sample, c_prompt, c_sample, cache_a_k, cache_a_v, cache_b_k, cache_b_v,
              ln_pre_a, ln_post_a, mod_w_a, mod_b_a, w_in_a, w_out_a,
              ln_kv, mod_w_kv, mod_b_kv, w_kv_b,
              ln_pre_b, ln_post_b, mod_w_b, mod_b_b, w_in_b, w_out_b,
              lambda_q1, lambda_k1, lambda_q2, lambda_k2, subln_b):
    params = {
        'ln_pre_a': ln_pre_a, 'ln_post_a': ln_post_a, 'mod_w_a': mod_w_a, 'mod_b_a': mod_b_a,
        'w_in_a': w_in_a, 'w_out_a': w_out_a,
        'ln_kv': ln_kv, 'mod_w_kv': mod_w_kv, 'mod_b_kv': mod_b_kv, 'w_kv_b': w_kv_b,
        'ln_pre_b': ln_pre_b, 'ln_post_b': ln_post_b, 'mod_w_b': mod_w_b, 'mod_b_b': mod_b_b,
        'w_in_b': w_in_b, 'w_out_b': w_out_b,
        'lambda_q1': lambda_q1, 'lambda_k1': lambda_k1, 'lambda_q2': lambda_q2, 'lambda_k2': lambda_k2,
        'subln_b': subln_b,
    }
    pos_p = jnp.arange(x_prompt.shape[1], dtype=jnp.int32)
    y_prompt, a_k_p, a_v_p, b_k_p, b_v_p = _trunk(x_prompt, c_prompt, pos_p, pos_p, None, params)
    past = cache_b_k.shape[1]
    t_new = x_sample.shape[1]
    q_pos_s = past + jnp.arange(t_new, dtype=jnp.int32)
    k_pos_s = jnp.arange(past + t_new, dtype=jnp.int32)
    y_sample, a_k_s, a_v_s, b_k_s, b_v_s = _trunk(
        x_sample, c_sample, q_pos_s, k_pos_s, (cache_a_k, cache_a_v, cache_b_k, cache_b_v), params)
    return (y_prompt, y_sample, a_k_p, a_v_p, b_k_p, b_v_p, a_k_s, a_v_s, b_k_s, b_v_s)


_drawn_inputs = setup_inputs


def setup_inputs(seed=0):
    import zlib

    import numpy as np

    out = dict(_drawn_inputs(seed))
    spreads = {}
    factors = {'mod_b_kv': 2.701, 'lambda_q1': 5.746, 'lambda_k1': 8.0}
    for name, (base, spread) in spreads.items():
        noise = np.random.default_rng([zlib.crc32(name.encode()), seed]).standard_normal(out[name].shape)
        drawn = base * np.exp(spread * noise) if base else spread * noise
        out[name] = __import__('jax').numpy.asarray(drawn.astype(out[name].dtype))
    for name, factor in factors.items():
        out[name] = (out[name] * factor).astype(out[name].dtype)
    return out
```

```python
import math
from contextlib import ExitStack

import numpy as np
import concourse.bass as bass
from concourse import mybir
from concourse.alu_op_type import AluOpType as ALU

F32 = mybir.dt.float32
BF16 = mybir.dt.bfloat16
ACT = mybir.ActivationFunctionType
AX = mybir.AxisListType

P = 128
D = 1024
KT = D // P
SEQ = 512
NT = SEQ // P
NSEQ = 8
NEW = 16
TT = NT + 1
TOK = TT * P
PAST = 256
PK = PAST // P
KEYS = PAST + NEW
PAIRS = 8
HD = 64
NC = 512
ROWS = 1 + NSEQ
SCALE = HD ** -0.5
EPS = 1e-6
NEG = -1e30
ROT = HD // 4
HALF = ROT // 2
LAMBDA_INIT = 0.8 - 0.6 * math.exp(-0.3)
HEAD = 8
UNITS = [(h, i) for i in (3, 2, 1, 0) for h in (0, 1)]
KB = 256

C_ID, C_SEL, C_EXP, C_EXS, C_COS, C_SIN, C_M0, C_M1 = 0, 128, 137, 265, 393, 433, 473, 474
C_PAIR = 475
C_N = C_PAIR + 2 * P


def constant_table():
    t = np.zeros((P, C_N), np.float32)
    p = np.arange(P)
    t[p, C_ID + p] = 1.0
    for r in range(ROWS):
        t[p % 32 == r, C_SEL + r] = 1.0
    t[p % 32 == 0, C_EXP:C_EXP + P] = 1.0
    for s in range(NSEQ):
        t[p % 32 == 1 + s, C_EXS + NEW * s:C_EXS + NEW * (s + 1)] = 1.0
    inv = np.float32(500000.0) ** (-np.arange(0, ROT, 2, dtype=np.float32) / np.float32(ROT))
    for i in range(TT):
        pos = (P * i + p) if i < NT else PAST + p % NEW
        ang = pos.astype(np.float32)[:, None] * inv[None, :].astype(np.float32)
        t[:, C_COS + HALF * i:C_COS + HALF * (i + 1)] = np.cos(ang)
        t[:, C_SIN + HALF * i:C_SIN + HALF * (i + 1)] = np.sin(ang)
    comp = (p // NEW) % 2
    t[:, C_M0] = comp == 0
    t[:, C_M1] = comp == 1
    for g in range(2):
        t[p, C_PAIR + P * g + NEW * (4 * g + p // 32) + p % NEW] = 1.0
    return t


def mask_table():
    q, k = np.arange(P)[:, None], np.arange(P)[None, :]
    return np.concatenate([
        np.where(k < q, 0.0, NEG), np.where(k // HD <= q // HD, 0.0, NEG),
        np.where(np.arange(NEW)[None, :] < q % NEW, 0.0, NEG), np.eye(P)], axis=1).astype(np.float32)


class Ring:

    def __init__(self, banks, done):
        self.banks, self.done, self.uses = banks, done, []

    def add(self, engine):
        self.uses.append((engine, 1 + sum(e == engine for e, _ in self.uses)))
        return len(self.uses) - 1

    def bank(self, n):
        return self.banks[n % len(self.banks)]

    def wait_free(self, eng, n):
        if n >= len(self.banks):
            e, v = self.uses[n - len(self.banks)]
            eng.wait_ge(self.done[e], v)

    def wait_all(self, eng, n):
        for e in self.done:
            v = sum(x == e for x, _ in self.uses[:n])
            if v:
                eng.wait_ge(self.done[e], v)


def build(nc, i, o):
    ctx = ExitStack()
    with ctx:
        def sb(name, shape, dt=F32):
            return ctx.enter_context(nc.sbuf_tensor(name, shape, dt))

        def sem(name):
            return ctx.enter_context(nc.semaphore(name))

        arena = sb("arena", [P, 188 * KB])
        at = [0]

        def region(kb):
            a = arena[:, at[0] * KB:(at[0] + kb) * KB]
            at[0] += kb
            return a

        X, RA, RB, RC, RD, RE, RF = (region(20) for _ in range(7))
        W = [region(16) for _ in range(2)]
        RH = region(16)

        def tok(r):
            return r.rearrange("p (t n) -> p t n", t=TT)

        def feat(r):
            return r.rearrange("p (k n) -> p k n", k=KT)

        def sub(r, a, n):
            return r[:, int(a * KB):int(a * KB) + n]

        x = tok(X)
        wk = [w.rearrange("p (k n) -> p k n", k=KT) for w in W]
        G = [sb(f"gate_{l}", [P, 2, D]) for l in "ab"]
        modT = sb("modT", [P, 6, KT, ROWS])
        const = sb("const", [P, C_N])
        ident = const[:, C_ID:C_ID + P]
        maskf = sub(RF, 0, 2 * P + NEW + P)
        maskb = sb("maskb", [P, 2 * P + NEW + P], BF16)
        mask_sb, mask_da = maskb[:, 0:P], maskb[:, P:2 * P]
        mask_new, identb = maskb[:, 2 * P:2 * P + NEW], maskb[:, 2 * P + NEW:]
        lnT = sb("lnT", [P, 3, KT])
        biasT = sb("biasT", [P, 6, KT])
        ss = sb("ss", [P, 2 * TT])
        rstd = sb("rstd", [P, 2 * TT])
        small = sb("small", [P, 64])
        neglam = sb("neglam", [P, 1])
        sgn = sb("sgn", [P, 1])
        subS = sb("subS", [P, P])
        gbias, lnpost = sub(RH, 0, D), sub(RH, 4, D)
        msum = [sub(RH, 8 + 2 * b, NC) for b in range(2)]
        cT = sub(RH, 12, KT * 32).rearrange("p (k r) -> p k r", k=KT)
        cin = sub(RH, 13, KT * ROWS).rearrange("p (k r) -> p k r", k=KT)
        lamv = sub(RH, 14, 4 * HD).rearrange("p (a d) -> p a d", a=4)
        junk = [sub(RH, 2 * b, NC) for b in range(2)]
        ytmp = sub(RH, 4, 2 * D).rearrange("p (b n) -> p b n", b=2)
        ps = [ctx.enter_context(nc.psum_tensor(f"bank{b}", [P, NC], F32)) for b in range(8)]

        xh = tok(RF)
        hT = feat(RE)
        kT, qT, gT, v, knat = feat(RA), feat(RB), feat(RC), tok(RD), tok(RF)
        xh2, hkv, hb = tok(RC), feat(RE), feat(RF)
        kbT, qbT, kbn, gs, vb, qbn, obuf, ogT = feat(RA), feat(RB), tok(RC), tok(RC), tok(RD), tok(RE), tok(RE), feat(RA)
        AT = sub(RE, 0, 2 * NT * NC).rearrange("p (h j q) -> p h j q", h=2, j=NT)
        vst = sub(RE, 16, NT * P).rearrange("p (j n) -> p j n", j=NT)
        beta = sub(RF, 0, 4 * NC).rearrange("p (b n) -> p b n", b=4)
        stay = sub(RF, 8, 4 * NC).rearrange("p (b n) -> p b n", b=4)
        ex = sub(RF, 16, 2 * NC).rearrange("p (b n) -> p b n", b=2)
        qz = sub(RH, 0, 2 * NC).rearrange("p (h n) -> p h n", h=2)
        pr = sub(RF, 0, 4 * NC).rearrange("p (b c n) -> p b c n", b=2, c=2)
        wT = sub(RF, 8, 2 * NC).rearrange("p (b n) -> p b n", b=2)
        kc = [sub(RH, 4, PK * D), sub(RE, 0, PK * D)]
        kc = [a.rearrange("p (k n) -> p k n", k=PK) for a in kc]
        ktc = [sub(RF, 8.5 * b, PAIRS * KEYS).rearrange("p (k n) -> p k n", k=PAIRS) for b in range(2)]
        vc = [sub(RD, 8 * b, PK * D).rearrange("p (k n) -> p k n", k=PK) for b in range(2)]
        vnew = [sub(RD, 16, D), sub(RE, 8, D)]
        qb = sub(RF, 17, PAIRS * 32).rearrange("p (k n) -> p k n", k=PAIRS)
        sbeta, sstay, sex = (sub(RE, 12 + 2.25 * b, 2 * KEYS).rearrange("p (g n) -> p g n", g=2) for b in range(3))
        sAT = sub(RH, 12, 2 * 3 * P).rearrange("p (g k n) -> p g k n", g=2, k=3)
        kcb = [sub(RH, 4, PK * D), sub(RD, 0, PK * D)]
        kcb = [a.rearrange("p (k n) -> p k n", k=PK) for a in kcb]
        vcb = sub(RD, 8, PK * D).rearrange("p (k n) -> p k n", k=PK)
        vnewb = sub(RD, 16, D)
        spr = sub(RH, 12, 2 * KEYS).rearrange("p (g n) -> p g n", g=2)
        cmat = sub(RH, 14.5, 2 * P).rearrange("p (g n) -> p g n", g=2)
        qbb = sub(RF, 17, PAIRS * 32).rearrange("p (k n) -> p k n", k=PAIRS)
        WTW = P + NEW
        swT = sub(RF, 18, 3 * WTW).rearrange("p (k n) -> p k n", k=3)
        osb = sub(RH, 0, 2 * P)
        sq = sub(RF, 0, 2 * D).rearrange("p (b n) -> p b n", b=2)

        caches = {
            "ak": i["cache_a_k"].rearrange("a s (k p) h d -> (a s) p k (h d)", p=P),
            "av": i["cache_a_v"].rearrange("a s (k p) h d -> (a s) p k (h d)", p=P),
            "bk": i["cache_b_k"].rearrange("s (k p) h c d -> s p k (h c d)", p=P),
            "bv": i["cache_b_v"].rearrange("s (k p) h d -> s p k (h d)", p=P),
        }
        out_p = {
            "y": o["y_p"].rearrange("b (t p) n -> p (b t) n", p=P),
            "ak": o["ak_p"].rearrange("a b (t p) h d -> p (a b t) (h d)", p=P),
            "av": o["av_p"].rearrange("a b (t p) h d -> p (a b t) (h d)", p=P),
            "bk": o["bk_p"].rearrange("b (t p) h c d -> p (b t) (h c d)", p=P),
            "bv": o["bv_p"].rearrange("b (t p) h d -> p (b t) (h d)", p=P),
        }
        out_s = {
            "y": o["y_s"].rearrange("s q n -> (s q) n"),
            "ak": o["ak_s"].rearrange("a s q h d -> (a s q) (h d)"),
            "av": o["av_s"].rearrange("a s q h d -> (a s q) (h d)"),
            "bk": o["bk_s"].rearrange("s q h c d -> (s q) (h c d)"),
            "bv": o["bv_s"].rearrange("s q h d -> (s q) (h d)"),
        }
        av_rows = o["av_s"].rearrange("a s q h d -> (a s) q (h d)")
        bv_rows = o["bv_s"].rearrange("s q h d -> s q (h d)")
        o_scratch = i["o_scratch"]

        def cols(w, c):
            return w.rearrange("(k p) n -> p k n", p=P)[:, :, NC * c:NC * (c + 1)]

        wa, woa, wkv, wb, wob = (i["w_in_a"][0], i["w_out_a"][0], i["w_kv_b"], i["w_in_b"][0], i["w_out_b"][0])
        mods = [("a", i["mod_w_a"][0], c) for c in range(6)] + [("kv", i["mod_w_kv"], c) for c in range(4)] \
            + [("b", i["mod_w_b"][0], c) for c in range(6)]
        steps = [("mod", n) for n in range(4)]
        rest = list(range(4, 16))
        for n, (kind, c) in enumerate([("k", 2), ("k", 3), ("v", 4), ("v", 5), ("q", 0), ("q", 1), ("g", 6), ("g", 7)]):
            steps.append(("a" + kind, c))
            steps += [("mod", rest.pop(0)) for _ in range(2 if n < 4 else 1)]
        steps += [("ya", 0), ("ya", 1)]
        steps += [("bk", 0), ("bk", 1), ("bv", 2), ("bv", 3), ("bq", 0), ("bq", 1), ("bg", 2), ("bg", 3)]
        steps += [("yb", 0), ("yb", 1)]
        dram = {"ak": wa, "av": wa, "aq": wa, "ag": wa, "ya": woa, "bk": wkv, "bv": wkv, "bq": wb, "bg": wb, "yb": wob}
        chunk = {s: n for n, s in enumerate(steps)}

        s_const, s_mask, s_x, s_c, s_vec = sem("const_in"), sem("mask_in"), sem("x_in"), sem("c_in"), sem("vectors_in")
        s_maskb = sem("masks_cast")
        s_silu_c, s_cz, s_lam, s_lamx = sem("silu_c"), sem("c_zeroed"), sem("lambda_steps"), sem("lambda_exp")
        s_gb = sem("gate_vectors_in")
        s_w = [sem("weights_in0"), sem("weights_in1")]
        s_macc, s_msum, s_mout, s_mdone = sem("mod_partial"), sem("mod_partial_read"), sem("mod_out"), sem("mod_read")
        s_dve = sem("dve_chain")
        s_ss, s_var, s_sqrt, s_xh = sem("squares_summed"), sem("variance"), sem("sqrt_done"), sem("normed_ready")
        s_tr, s_trA, s_trV = sem("transposed"), sem("transposed_read_act"), sem("transposed_read_dve")
        s_pj, s_pjA, s_pjV = sem("projected"), sem("projected_read_act"), sem("projected_read_dve")
        s_rot, s_gsub = sem("rotated"), sem("gate_subln")
        s_stored = {n: sem("stored_" + n) for n in ("ak", "av", "bk", "bv")}
        s_y, s_ysq, s_yv, s_ysr, s_yt, s_x2 = (sem("y_ready"), sem("y_squares"), sem("y_var"), sem("y_sqrt"),
                                              sem("y_scaled"), sem("x_updated"))
        a_qz, a_vst, a_z, a_sig, a_ex, a_mul, a_t, a_at, a_av, a_og = (sem("a_" + n) for n in (
            "q_staged", "v_staged", "z_ready", "sigmoids", "scanned", "a_ready", "t_ready", "at_ready", "o_ready", "o_gated"))
        (c_k, c_v, c_vn, c_kt, c_ktr, c_q, c_z, c_sig, c_ex, c_mul, c_t, c_at, c_av, c_og) = (sem("c_" + n) for n in (
            "k_in", "v_in", "vnew_in", "k_transposed", "k_read", "q_staged", "z_ready", "sigmoids", "scanned",
            "a_ready", "t_ready", "at_ready", "o_ready", "o_gated"))
        c_k = [c_k, sem("c_k_in1")]
        c_v = [c_v, sem("c_v_in1")]
        c_vn = [c_vn, sem("c_vnew_in1")]
        b_qz, b_s, b_mx, b_nb, b_p, b_rc, b_c1, b_w, b_t, b_wt, b_o, b_or = (sem("b_" + n) for n in (
            "q_staged", "s_ready", "max", "neg_max", "p_ready", "reciprocal", "coefficient", "w_ready", "t_ready",
            "wt_ready", "o_ready", "o_read"))
        (d_v, d_vn, d_kt, d_ktr, d_q, d_s, d_mx, d_nb, d_p, d_rc, d_rs, d_cm, d_wt, d_wtr, d_o, d_or, d_out) = (
            sem("d_" + n) for n in ("v_in", "vnew_in", "k_transposed", "k_read", "q_staged", "s_ready", "max",
                                    "neg_max", "p_ready", "reciprocal", "row_scale", "combiner", "wt_ready", "wt_read",
                                    "o_ready", "o_read", "o_out"))
        d_left = sem("d_o_left")
        d_k = [sem("d_k_in0"), sem("d_k_in1")]
        s_osq, s_oss, s_ov, s_osr, s_or, s_og = (sem("o_" + n) for n in ("squares", "sums", "var", "sqrt", "rstd", "gated"))
        s_oin, s_out = sem("o_sample_in"), sem("y_stored")
        s_zero = sem("zeroed")

        proj = Ring([0, 1, 2, 3], {"act": s_pjA, "dve": s_pjV})
        jobs = {}
        for kind, c in steps:
            if kind[0] not in "ab" or kind in ("mod",):
                continue
            if kind in ("aq", "ag"):
                subs = [("T", f, h) for f in range(4) for h in range(2)]
            else:
                subs = [("N", t) for t in range(TT)]
            for job in subs:
                e = "act" if kind[1] == "g" or len(proj.uses) % 2 == 0 else "dve"
                jobs.setdefault((kind, c), []).append((proj.add(e), e, job))
        pj_end = {}
        for key, js in jobs.items():
            pj_end[key] = js[-1][0] + 1
        trans = Ring([6, 7], {"act": s_trA, "dve": s_trV})
        tr_of = {}
        for stage in ("xa", "ka", "xb", "kb", "qb", "og"):
            tr_of[stage] = []
            for g in range(KT + 2):
                e = "dve" if g >= KT or g % 2 else "act"
                tr_of[stage].append((trans.add(e), e))

        def tr_end(stage):
            return tr_of[stage][-1][0] + 1

        def tr_src(n, g):
            return [(t, g) for t in range(NT)] if g < KT else [(NT, 4 * (g - KT) + a) for a in range(4)]

        def tr_dst(dst, g):
            return dst[:, g, 0:SEQ] if g < KT else dst[:, 4 * (g - KT):4 * (g - KT) + 4, SEQ:TOK]

        def tr_bank(n, g):
            b = ps[trans.bank(n)]
            return b[:, :] if g < KT else b[:, :].rearrange("p (a n) -> p a n", a=4)

        def proj_dst(kind, c, job, bank):
            if job[0] == "T":
                _, f, h = job
                dst = {"aq": qT, "ag": gT}[kind]
                return dst[:, 4 * (c % 2) + f, 320 * h:320 * (h + 1)], bank[:, 0:320]
            dst = {"ak": knat, "av": v, "bk": kbn, "bv": vb, "bq": qbn, "bg": gs}[kind]
            return dst[:, job[1], NC * (c % 2):NC * (c % 2 + 1)], bank[:, :]

        def mod_outs(n):
            return sum(1 if mods[m][2] < 4 else 2 for m in range(n))

        def wait_used(eng, n):
            kind, c = steps[n]
            if kind == "mod":
                eng.wait_ge(s_macc, c + 1)
            elif kind[0] == "y":
                eng.wait_ge(s_y, TT * (1 + (kind == "yb")))
            else:
                eng.wait_ge(s_pj, pj_end[(kind, c)])

        block = ctx.enter_context(nc.Block())

        @block.sync
        def _(sp):
            sp.dma_start(cin, i["cT"]).then_inc(s_c, 16)
            sp.dma_start(const[:, :], i["consts"]).then_inc(s_const, 16)

            def load(n):
                kind, c = steps[n]
                if n >= 2:
                    wait_used(sp, n - 2)
                src = cols(mods[c][1], mods[c][2]) if kind == "mod" else cols(dram[kind], c)
                sp.dma_start(wk[n % 2], src).then_inc(s_w[n % 2], 16)

            load(0)
            sp.dma_start(x[:, 0:NT, :], i["x_prompt"].rearrange("b (t p) n -> p (b t) n", p=P)).then_inc(s_x, 16)
            sp.dma_start(x[:, NT, :], i["x_sample"].rearrange("s q n -> (s q) n")).then_inc(s_x, 16)
            load(1)
            sp.dma_start(lnT[:, :, :], i["lnT"]).then_inc(s_vec, 16)
            sp.dma_start(biasT[:, :, :], i["biasT"]).then_inc(s_vec, 16)
            sp.dma_start(maskf, i["masks"]).then_inc(s_mask, 16)
            sp.dma_start(lamv, i["lam"].partition_broadcast(P)).then_inc(s_vec, 16)
            sp.dma_start(subS[:, :], i["subln_b"].rearrange("a n -> (a n)").partition_broadcast(P)).then_inc(s_vec, 16)
            sp.dma_start(gbias, i["mod_b_a"][0, 2 * D:3 * D].partition_broadcast(P)).then_inc(s_gb, 16)
            sp.dma_start(lnpost, i["ln_post_a"][0].partition_broadcast(P)).then_inc(s_gb, 16)
            for n in range(2, chunk[("ya", 0)]):
                load(n)
                if steps[n] == ("mod", 8):
                    sp.wait_ge(s_mdone, mod_outs(6))
                    sp.dma_start(gbias, i["mod_b_b"][0, 2 * D:3 * D].partition_broadcast(P)).then_inc(s_gb, 16)
                    sp.dma_start(lnpost, i["ln_post_b"][0].partition_broadcast(P)).then_inc(s_gb, 16)
            load(chunk[("ya", 0)])
            load(chunk[("ya", 1)])

            sp.wait_ge(s_mdone, mod_outs(16))

            def cache_a(it, b):
                s = it * 2 + b
                sp.wait_ge(c_kt, s * 4 + (HEAD - 4))
                sp.dma_start(kc[b], caches["ak"][s]).then_inc(c_k[b], 16)
                sp.wait_ge(c_av, s * 2 + (HEAD - 2))
                sp.dma_start(vc[b], caches["av"][s]).then_inc(c_v[b], 16)
                sp.dma_start(vnew[b][0:NEW, :], av_rows[s]).then_inc(c_vn[b], 16)

            sp.wait_ge(a_av, HEAD + PAIRS)
            sp.wait_ge(a_at, HEAD + 8 * PAIRS)
            sp.wait_ge(s_stored["ak"], 32)
            sp.wait_ge(s_stored["av"], 32)
            with sp.Fori(0, NSEQ // 2) as it:
                for b in range(2):
                    cache_a(it, b)
            for n in range(chunk[("bk", 0)], len(steps)):
                load(n)
            sp.wait_ge(b_o, HEAD + NT * PAIRS)
            sp.wait_ge(s_stored["bk"], 32)
            sp.wait_ge(s_stored["bv"], 32)

            def cache_b(it, b):
                s = it * 2 + b
                sp.wait_ge(d_kt, s * 4 + (HEAD - 4))
                sp.dma_start(kcb[b], caches["bk"][s]).then_inc(d_k[b], 16)
                sp.wait_ge(d_o, s + HEAD)
                sp.dma_start(vcb, caches["bv"][s]).then_inc(d_v, 16)
                sp.dma_start(vnewb[0:NEW, :], bv_rows[s]).then_inc(d_vn, 16)

            with sp.Fori(0, NSEQ // 2) as it:
                for b in range(2):
                    cache_b(it, b)
            sp.wait_ge(d_out, 16 * 4 * NSEQ)
            sp.dma_start(obuf[:, NT, :].rearrange("p (g j n) -> p g j n", g=2, j=4),
                         o_scratch.rearrange("s q g j n -> (s q) g j n")).then_inc(s_oin, 16)
            for t in range(TT):
                sp.wait_ge(s_x2, TT + t + 1)
                if t < NT:
                    sp.dma_start(out_p["y"][:, t, :], x[:, t, :]).then_inc(s_out, 16)
                else:
                    sp.dma_start(out_s["y"], x[:, t, :]).then_inc(s_out, 16)
            sp.wait_ge(s_out, 16 * TT)
            sp.wait_ge(s_stored["bk"], 32)
            sp.wait_ge(s_stored["bv"], 32)

        @block.gpsimd
        def _(pool):
            for s in (a_qz, a_vst, c_q, b_qz, d_q, d_left):
                pool.sem_inc(s, HEAD)

            def store(name, src, ring, n):
                ring.wait_all(pool, n)
                pool.dma_start(out_p[name], src[:, 0:NT, :]).then_inc(s_stored[name], 16)
                pool.dma_start(out_s[name], src[:, NT, :]).then_inc(s_stored[name], 16)

            store("ak", knat, proj, pj_end[("ak", 3)])
            store("av", v, proj, pj_end[("av", 5)])
            proj.wait_all(pool, pj_end[("ag", 7)])
            trans.wait_all(pool, tr_end("ka"))
            pool.wait_ge(s_mdone, mod_outs(16))
            pool.wait_ge(s_stored["ak"], 32)
            pool.wait_ge(s_stored["av"], 32)
            nc.gpsimd.memset(qz[HD:P, 0, :], 0.0).then_inc(s_zero, 1)
            pool.wait_ge(s_zero, 1)
            nc.gpsimd.memset(qz[0:HD, 1, :], 0.0).then_inc(s_zero, 1)
            pool.wait_ge(s_zero, 2)
            with pool.Fori(0, PAIRS) as p:
                pool.wait_ge(a_z, p * 8 + HEAD)
                nc.gpsimd.tensor_copy(qz[0:HD, 0, :], qT[0:HD, p, 0:SEQ]).then_inc(a_qz, 1)
                pool.wait_ge(a_qz, p * 2 + (HEAD + 1))
                nc.gpsimd.tensor_copy(qz[HD:P, 1, :], qT[HD:P, p, 0:SEQ]).then_inc(a_qz, 1)
                pool.wait_ge(a_qz, p * 2 + (HEAD + 2))
                pool.wait_ge(a_av, p + HEAD)
                nc.gpsimd.tensor_copy(vst, v[:, 0:NT, bass.ts(p, P)]).then_inc(a_vst, 1)
                pool.wait_ge(a_vst, p + (HEAD + 1))
            pool.wait_ge(a_av, HEAD + PAIRS)
            pool.wait_ge(a_at, HEAD + 8 * PAIRS)
            pool.wait_ge(a_mul, HEAD + 8 * PAIRS)
            nc.gpsimd.memset(qb, 0.0).then_inc(s_zero, 1)
            pool.wait_ge(s_zero, 3)

            def stage_new(s, b, kt_src, q_src, kt_dst, q_dst, done, z_done):
                pool.wait_ge(z_done, s * 2 + HEAD)
                new = bass.ds(s * NEW + SEQ, NEW)
                copies = [(kt_dst[b][:, :, PAST:KEYS], kt_src[:, :, new]), (q_dst[0:HD, :, 0:NEW], q_src[0:HD, :, new]),
                          (q_dst[HD:P, :, NEW:32], q_src[HD:P, :, new])]
                for n, (dst, src) in enumerate(copies):
                    nc.gpsimd.tensor_copy(dst, src).then_inc(done, 1)
                    pool.wait_ge(done, s * 3 + (HEAD + n + 1))

            with pool.Fori(0, NSEQ // 2) as it:
                for b in range(2):
                    stage_new(it * 2 + b, b, kT, qT, ktc, qb, c_q, c_z)
            pool.wait_ge(s_rot, 1)
            store("bk", kbn, proj, pj_end[("bk", 1)])
            store("bv", vb, proj, pj_end[("bv", 3)])
            for t in range(TT):
                proj.wait_all(pool, pj_end[("bg", 3)])
                pool.wait_ge(s_vec, 64)
                g3 = gs[:, t, :].rearrange("p (h e) -> p h e", h=PAIRS)
                if t == 0:
                    nc.gpsimd.tensor_scalar(subS[:, :], subS[:, :], 1.0 - LAMBDA_INIT, None, ALU.mult).then_inc(s_gsub, 1)
                    pool.wait_ge(s_gsub, 1)
                nc.gpsimd.tensor_tensor(g3, g3, subS[:, :].unsqueeze(1).to_broadcast([P, PAIRS, P]), ALU.mult).then_inc(s_gsub, 1)
            pool.wait_ge(s_gsub, 1 + TT)
            trans.wait_all(pool, tr_end("qb"))
            nc.gpsimd.memset(qz[HD:P, 0, :], 0.0).then_inc(s_zero, 1)
            pool.wait_ge(s_zero, 4)
            nc.gpsimd.memset(qz[0:HD, 1, :], 0.0).then_inc(s_zero, 1)
            pool.wait_ge(s_zero, 5)
            with pool.Fori(0, PAIRS) as p:
                pool.wait_ge(b_s, p * NT + HEAD)
                nc.gpsimd.tensor_copy(qz[0:HD, 0, :], qbT[0:HD, p, 0:SEQ]).then_inc(b_qz, 1)
                pool.wait_ge(b_qz, p * 2 + (HEAD + 1))
                nc.gpsimd.tensor_copy(qz[HD:P, 1, :], qbT[HD:P, p, 0:SEQ]).then_inc(b_qz, 1)
                pool.wait_ge(b_qz, p * 2 + (HEAD + 2))
            pool.wait_ge(b_o, HEAD + NT * PAIRS)
            nc.gpsimd.memset(qbb, 0.0).then_inc(s_zero, 1)
            pool.wait_ge(s_zero, 6)
            nc.gpsimd.memset(swT[:, :, P:WTW], 0.0).then_inc(s_zero, 1)
            pool.wait_ge(s_zero, 7)

            def out_b(s):
                pool.wait_ge(d_or, s + HEAD + 1)
                for j in range(4):
                    pool.dma_start(o_scratch[s][:, :, j, :],
                                   osb[32 * j:32 * j + NEW, :].rearrange("p (g n) -> p g n", g=2)).then_inc(d_out, 16)
                pool.wait_ge(d_out, s * 64 + 64)
                pool.sem_inc(d_left, 1)

            with pool.Fori(0, NSEQ // 2) as it:
                for b in range(2):
                    stage_new(it * 2 + b, b, kbT, qbT, ktc, qbb, d_q, d_s)
                    out_b(it * 2 + b)

        @block.scalar
        def _(act):
            for s in (a_sig, a_at, c_sig, c_ktr, c_at, b_p, b_wt, b_or, d_p, d_ktr, d_wtr, d_or):
                act.sem_inc(s, HEAD)
            act.wait_ge(s_c, 16)
            act.wait_ge(s_cz, 1)
            nc.scalar.activation(cT[:, :, 0:ROWS], cin, ACT.Silu).then_inc(s_silu_c, 1)
            act.wait_ge(s_lam, 1)
            nc.scalar.activation(small[:, 2:4], small[:, 0:2], ACT.Exp).then_inc(s_lamx, 1)

            def square_sums(src, stage):
                for t in range(TT):
                    nc.scalar.activation(xh_of[stage][:, t, :], src[:, t, :], ACT.Square,
                                         accum_out=ss[:, TT * stage + t:TT * stage + t + 1]).then_inc(s_ss, 1)
                act.wait_ge(s_var, stage + 1)
                nc.scalar.activation(ss[:, TT * stage:TT * (stage + 1)], ss[:, TT * stage:TT * (stage + 1)],
                                     ACT.Sqrt).then_inc(s_sqrt, 1)

            xh_of = [xh, xh2]
            act.wait_ge(s_x, 32)
            act.wait_ge(s_maskb, 1)
            square_sums(x, 0)

            def affine(dst, kt, bank, vs):
                nc.scalar.activation(dst, bank, ACT.Identity, bias=modT[:, vs, kt, 0:1], scale=modT[:, vs + 1, kt, 0:1])\
                    .then_inc(s_trA, 1)

            act.wait_ge(s_mdone, 4)
            for g, (n, e) in enumerate(tr_of["xa"]):
                if e == "act":
                    act.wait_ge(s_tr, n + 1)
                    affine(hT[:, g, 0:SEQ], g, tr_bank(n, g), 0)

            def read_proj(kind, c):
                for n, e, job in jobs[(kind, c)]:
                    if e != "act":
                        continue
                    act.wait_ge(s_pj, n + 1)
                    bank = ps[proj.bank(n)]
                    func = ACT.Silu if kind[1] == "g" else ACT.Copy
                    dst, src = proj_dst(kind, c, job, bank)
                    nc.scalar.activation(dst, src, func).then_inc(s_pjA, 1)

            def read_transposes(stage, dst):
                for g, (n, e) in enumerate(tr_of[stage]):
                    if e == "act":
                        act.wait_ge(s_tr, n + 1)
                        nc.scalar.activation(tr_dst(dst, g), tr_bank(n, g), ACT.Copy).then_inc(s_trA, 1)

            read_proj("ak", 2)
            read_proj("ak", 3)
            read_proj("av", 4)
            read_transposes("ka", kT)
            for key in (("av", 5), ("aq", 0), ("aq", 1), ("ag", 6), ("ag", 7)):
                read_proj(*key)

            trans.wait_all(act, tr_end("ka"))
            act.wait_ge(s_stored["ak"], 32)
            act.wait_ge(s_stored["av"], 32)
            with act.Fori(0, PAIRS) as p:
                def sig(u):
                    w = P * (UNITS[u][1] + 1)
                    act.wait_ge(a_z, p * 8 + (HEAD + u + 1))
                    act.wait_ge(a_t, p * 8 + (HEAD + u + 1 - 4))
                    nc.scalar.activation(beta[:, u % 4, 0:w], ps[u % 4][:, 0:w], ACT.Sigmoid, scale=SCALE)
                    nc.scalar.activation(stay[:, u % 4, 0:w], ps[u % 4][:, 0:w], ACT.Sigmoid, scale=-SCALE).then_inc(a_sig, 1)

                def read_t(u):
                    h, q = UNITS[u]
                    act.wait_ge(a_t, p * 8 + (HEAD + u + 1))
                    if u == 0:
                        act.wait_ge(a_av, p + HEAD)
                    nc.scalar.activation(AT[:, h, 0:q + 1, P * q:P * (q + 1)],
                                         ps[4 + u % 2][:, 0:P * (q + 1)].rearrange("p (j n) -> p j n", j=q + 1),
                                         ACT.Copy).then_inc(a_at, 1)
                for u in range(8):
                    sig(u)
                    if u >= 2:
                        read_t(u - 2)
                read_t(6)
                read_t(7)

            def read_k(ready, done, s, b):
                for c in range(4):
                    act.wait_ge(ready, s * 4 + (HEAD + c + 1))
                    nc.scalar.activation(ktc[b][:, 2 * c:2 * c + 2, 0:PAST],
                                         ps[c % 2][:, :].rearrange("p (a n) -> p a n", a=2), ACT.Copy).then_inc(done, 1)

            act.wait_ge(a_av, HEAD + PAIRS)
            act.wait_ge(a_mul, HEAD + 8 * PAIRS)
            act.wait_ge(a_at, HEAD + 8 * PAIRS)
            read_k(c_kt, c_ktr, 0, 0)

            def sample_a(it, b, last):
                s = it * 2 + b
                for g in range(2):
                    act.wait_ge(c_z, s * 2 + (HEAD + g + 1))
                    act.wait_ge(c_t, s * 2 + (HEAD + g + 1 - 2))
                    nc.scalar.activation(sbeta[:, g, :], ps[2 + g][:, 0:KEYS], ACT.Sigmoid, scale=SCALE)
                    nc.scalar.activation(sstay[:, g, :], ps[2 + g][:, 0:KEYS], ACT.Sigmoid, scale=-SCALE).then_inc(c_sig, 1)
                if not last:
                    read_k(c_kt, c_ktr, s + 1, 1 - b)
                for g in range(2):
                    act.wait_ge(c_t, s * 2 + (HEAD + g + 1))
                    act.wait_ge(c_av, s * 2 + (HEAD + g + 1 - 2))
                    nc.scalar.activation(sAT[:, g, 0:2, :], ps[4 + g][:, 0:2 * P].rearrange("p (k n) -> p k n", k=2), ACT.Copy)
                    nc.scalar.activation(sAT[0:NEW, g, 2, :], ps[4 + g][0:NEW, 2 * P:3 * P], ACT.Copy).then_inc(c_at, 1)

            with act.Fori(0, NSEQ // 2 - 1) as it:
                for b in range(2):
                    sample_a(it, b, False)
            sample_a(NSEQ // 2 - 1, 0, False)
            sample_a(NSEQ // 2 - 1, 1, True)

            def y_squares(layer):
                for t in range(TT):
                    n = layer * TT + t
                    act.wait_ge(s_y, n + 1)
                    for c in range(2):
                        if n or c:
                            act.wait_ge(s_ysq, 2 * n + c)
                        nc.scalar.activation(junk[c], ps[2 * (t % 2) + c][:, :], ACT.Square,
                                             accum_out=small[:, 4 + c:5 + c]).then_inc(s_ysq, 1)
                    act.wait_ge(s_yv, n + 1)
                    nc.scalar.activation(small[:, 8:9], small[:, 7:8], ACT.Sqrt).then_inc(s_ysr, 1)

            y_squares(0)
            act.wait_ge(s_x2, TT)
            act.wait_ge(c_og, HEAD + 16)
            square_sums(x, 1)
            for g, (n, e) in enumerate(tr_of["xb"]):
                if e == "act":
                    act.wait_ge(s_tr, n + 1)
                    nc.scalar.activation(hkv[:, g, 0:SEQ], tr_bank(n, g), ACT.Identity,
                                         bias=modT[:, 2, g, 0:1], scale=modT[:, 3, g, 0:1])
                    affine(hb[:, g, 0:SEQ], g, tr_bank(n, g), 4)
            read_proj("bk", 0)
            read_proj("bk", 1)
            read_proj("bv", 2)
            read_transposes("kb", kbT)
            for key in (("bv", 3), ("bq", 0), ("bq", 1)):
                read_proj(*key)
            act.wait_ge(s_stored["bk"], 32)
            trans.wait_all(act, tr_end("kb"))
            read_proj("bg", 2)
            read_transposes("qb", qbT)
            read_proj("bg", 3)

            trans.wait_all(act, tr_end("qb"))
            with act.Fori(0, PAIRS) as p:
                def exps(u):
                    w = P * (NT - u)
                    act.wait_ge(b_nb, p * NT + (HEAD + u + 1))
                    act.wait_ge(b_t, p * NT + (HEAD + u + 1 - 2))
                    for c in range(2):
                        nc.scalar.activation(pr[:, u % 2, c, 0:w], ps[2 * (u % 2) + c][:, 0:w], ACT.Exp,
                                             bias=small[:, 16 + 4 * u + c:17 + 4 * u + c], scale=SCALE,
                                             accum_out=small[:, 32 + 4 * u + c:33 + 4 * u + c]).then_inc(b_p, 1)

                def read_t(u):
                    w = P * (NT - u)
                    act.wait_ge(b_t, p * NT + (HEAD + u + 1))
                    act.wait_ge(b_o, p * NT + (HEAD + u + 1 - 2))
                    nc.scalar.activation(wT[:, u % 2, 0:w], ps[4 + u % 2][:, 0:w], ACT.Copy).then_inc(b_wt, 1)

                def read_o(u):
                    act.wait_ge(b_o, p * NT + (HEAD + u + 1))
                    nc.scalar.activation(obuf[:, NT - 1 - u, bass.ts(p, P)], ps[6 + u % 2][:, 0:P], ACT.Copy,
                                         scale=small[:, 34 + 4 * u:35 + 4 * u]).then_inc(b_or, 1)
                for u in range(NT):
                    exps(u)
                    if u >= 1:
                        read_t(u - 1)
                    if u >= 2:
                        read_o(u - 2)
                read_t(NT - 1)
                read_o(NT - 2)
                read_o(NT - 1)

            act.wait_ge(b_o, HEAD + NT * PAIRS)
            act.wait_ge(b_w, HEAD + NT * PAIRS)
            read_k(d_kt, d_ktr, 0, 0)

            def sample_b(it, b, last):
                s = it * 2 + b
                for g in range(2):
                    act.wait_ge(d_nb, s * 2 + (HEAD + g + 1))
                    act.wait_ge(d_wt, s + HEAD)
                    nc.scalar.activation(spr[:, g, :], ps[2 + g][:, 0:KEYS], ACT.Exp, bias=small[:, 18 + g:19 + g],
                                         scale=SCALE, accum_out=small[:, 20 + g:21 + g]).then_inc(d_p, 1)
                if not last:
                    read_k(d_kt, d_ktr, s + 1, 1 - b)
                act.wait_ge(d_wt, s + (HEAD + 1))
                act.wait_ge(d_o, s + HEAD)
                nc.scalar.activation(swT[:, 0:2, 0:P], ps[4][:, 0:2 * P].rearrange("p (k n) -> p k n", k=2), ACT.Copy)
                nc.scalar.activation(swT[0:NEW, 2, 0:P], ps[4][0:NEW, 2 * P:3 * P], ACT.Copy).then_inc(d_wtr, 1)
                act.wait_ge(d_o, s + (HEAD + 1))
                act.wait_ge(d_left, s + HEAD)
                nc.scalar.activation(osb, ps[5][:, 0:2 * P], ACT.Copy).then_inc(d_or, 1)

            with act.Fori(0, NSEQ // 2 - 1) as it:
                for b in range(2):
                    sample_b(it, b, False)
            sample_b(NSEQ // 2 - 1, 0, False)
            sample_b(NSEQ // 2 - 1, 1, True)

            act.wait_ge(s_oin, 16)
            for t in range(TT):
                if t >= 2:
                    act.wait_ge(s_oss, t - 1)
                nc.scalar.activation(sq[:, t % 2, :], obuf[:, t, :], ACT.Square).then_inc(s_osq, 1)
            act.wait_ge(s_ov, 1)
            nc.scalar.activation(small[:, 0:40], small[:, 0:40], ACT.Sqrt).then_inc(s_osr, 1)
            read_transposes("og", ogT)
            y_squares(1)

        @block.vector
        def _(dve):
            chain = [0]

            def link(ins):
                chain[0] += 1
                ins.then_inc(s_dve, 1)
                dve.wait_ge(s_dve, chain[0])

            for s in (a_ex, a_mul, a_og, c_ex, c_mul, c_og, b_mx, b_nb, b_rc, b_c1, b_w, d_mx, d_nb, d_rc, d_rs, d_cm):
                dve.sem_inc(s, HEAD)
            nc.vector.memset(cT[:, :, ROWS:32], 0.0).then_inc(s_cz, 1)
            dve.wait_ge(s_mask, 16)
            nc.vector.tensor_copy(maskb[:, :], maskf).then_inc(s_maskb, 1)

            def norm(stage, src, dst):
                a, b = TT * stage, TT * (stage + 1)
                dve.wait_ge(s_ss, b)
                nc.vector.tensor_scalar(ss[:, a:b], ss[:, a:b], 1.0 / D, EPS, ALU.mult, ALU.add).then_inc(s_var, 1)
                dve.wait_ge(s_sqrt, stage + 1)
                link(nc.vector.reciprocal(rstd[:, a:b], ss[:, a:b]))
                for t in range(TT):
                    nc.vector.tensor_scalar(dst[:, t, :], src[:, t, :], rstd[:, a + t:a + t + 1], None, ALU.mult)\
                        .then_inc(s_xh, 1)

            def mod(n):
                group, _, c = mods[n]
                dve.wait_ge(s_macc, n + 1)
                if n >= 2:
                    dve.wait_ge(s_mout, mod_outs(n - 1))
                nc.vector.tensor_copy(msum[n % 2], ps[4][:, :]).then_inc(s_msum, 1)
                if c < 4:
                    vi = {"a": 0, "kv": 2, "b": 4}[group] + c // 2
                    dst = modT[:, vi, 4 * (c % 2):4 * (c % 2) + 4, :]
                    bias = biasT[:, vi, 4 * (c % 2):4 * (c % 2) + 4].unsqueeze(2).to_broadcast([P, 4, ROWS])
                    dve.wait_ge(s_mout, mod_outs(n + 1))
                    dve.wait_ge(s_vec, 64)
                    src = ps[5][:, 0:4 * ROWS].rearrange("p (k r) -> p k r", k=4)
                    if vi % 2 == 0:
                        nc.vector.tensor_tensor(dst, src, bias, ALU.add).then_inc(s_mdone, 1)
                    else:
                        link(nc.vector.tensor_tensor(dst, src, bias, ALU.add))
                        ln = lnT[:, vi // 2, 4 * (c % 2):4 * (c % 2) + 4].unsqueeze(2).to_broadcast([P, 4, ROWS])
                        link(nc.vector.tensor_scalar(dst, dst, 1.0, None, ALU.add))
                        nc.vector.tensor_tensor(dst, dst, ln, ALU.mult).then_inc(s_mdone, 1)
                else:
                    layer = 0 if group == "a" else 1
                    half = slice(NC * (c - 4), NC * (c - 3))
                    dve.wait_ge(s_gb, 32 * (layer + 1))
                    for r in range(2):
                        dve.wait_ge(s_mout, mod_outs(n) + r + 1)
                        dst = G[layer][:, r, half]
                        link(nc.vector.tensor_tensor(dst, ps[5][:, :], gbias[:, half], ALU.add))
                        nc.vector.tensor_tensor(dst, dst, lnpost[:, half], ALU.mult).then_inc(s_mdone, 1)

            dve.wait_ge(s_vec, 64)
            link(nc.vector.tensor_tensor(lamv[:, 0:3:2, :], lamv[:, 0:3:2, :], lamv[:, 1:4:2, :], ALU.mult))
            nc.vector.tensor_reduce(small[:, 0:2], lamv[:, 0:3:2, :], AX.X, ALU.add).then_inc(s_lam, 1)
            dve.wait_ge(s_lamx, 1)
            link(nc.vector.tensor_tensor(small[:, 10:11], small[:, 3:4], small[:, 2:3], ALU.subtract))
            link(nc.vector.tensor_scalar(neglam[:, :], small[:, 10:11], -LAMBDA_INIT, None, ALU.add))
            dve.wait_ge(s_const, 16)
            link(nc.vector.scalar_tensor_tensor(sgn[:, :], const[:, C_M1:C_M1 + 1], neglam[:, 0:1],
                                                const[:, C_M0:C_M0 + 1], ALU.mult, ALU.add))
            mod(0)
            dve.wait_ge(s_x, 32)
            norm(0, x, xh)
            for n in range(1, 4):
                mod(n)

            def sample_affine(dst, n, g, vs, done):
                k = slice(4 * (g - KT), 4 * (g - KT) + 4)
                d = dst[:, k, SEQ:TOK].rearrange("p k (s q) -> p k s q", s=NSEQ)
                src = ps[trans.bank(n)][:, :].rearrange("p (k s q) -> p k s q", k=4, q=NEW)
                sc, sh = (modT[:, vs + a, k, 1:ROWS].unsqueeze(3).to_broadcast([P, 4, NSEQ, NEW]) for a in (1, 0))
                link(nc.vector.tensor_tensor(d, src, sc, ALU.mult))
                ins = nc.vector.tensor_tensor(d, d, sh, ALU.add)
                if done:
                    ins.then_inc(s_trV, 1)

            def prompt_affine(dst, n, g, vs):
                return nc.vector.tensor_scalar(dst[:, g, 0:SEQ], tr_bank(n, g), modT[:, vs + 1, g, 0:1],
                                               modT[:, vs, g, 0:1], ALU.mult, ALU.add)

            for g, (n, e) in enumerate(tr_of["xa"]):
                if e == "dve":
                    dve.wait_ge(s_tr, n + 1)
                    dve.wait_ge(s_mdone, 4)
                    if g < KT:
                        prompt_affine(hT, n, g, 0).then_inc(s_trV, 1)
                    else:
                        sample_affine(hT, n, g, 0, True)

            def read_proj(kind, c):
                for n, e, job in jobs[(kind, c)]:
                    if e == "dve":
                        dve.wait_ge(s_pj, n + 1)
                        dst, src = proj_dst(kind, c, job, ps[proj.bank(n)])
                        nc.vector.tensor_copy(dst, src).then_inc(s_pjV, 1)

            def read_transposes(stage, dst):
                for g, (n, e) in enumerate(tr_of[stage]):
                    if e == "dve":
                        dve.wait_ge(s_tr, n + 1)
                        nc.vector.tensor_copy(tr_dst(dst, g), tr_bank(n, g)).then_inc(s_trV, 1)

            for at_, st in enumerate(steps):
                if st[0] == "mod" and st[1] >= 4:
                    mod(st[1])
                elif st[0][0] == "a":
                    read_proj(*st)
                    if st == ("av", 4):
                        read_transposes("ka", kT)

            dve.wait_ge(s_stored["ak"], 32)
            dve.wait_ge(s_stored["av"], 32)
            with dve.Fori(0, PAIRS) as p:
                def scan(u):
                    w = P * (UNITS[u][1] + 1)
                    dve.wait_ge(a_sig, p * 8 + (HEAD + u + 1))
                    dve.wait_ge(a_mul, p * 8 + (HEAD + u + 1 - 2))
                    st = stay[:, u % 4, w - 1:0:-1]
                    nc.vector.tensor_tensor_scan(ex[:, u % 2, 0:w - 1][:, ::-1], st, st, 1.0, ALU.mult, ALU.bypass)\
                        .then_inc(a_ex, 1)

                def mul(u):
                    w = P * (UNITS[u][1] + 1)
                    dve.wait_ge(a_ex, p * 8 + (HEAD + u + 1))
                    b = beta[:, u % 4, 0:w - 1]
                    nc.vector.tensor_tensor(b, b, ex[:, u % 2, 0:w - 1], ALU.mult).then_inc(a_mul, 1)
                for u in range(8):
                    scan(u)
                    if u >= 1:
                        mul(u - 1)
                mul(7)
                dve.wait_ge(a_av, p + (HEAD + 1))
                g = gT[:, p, 0:SEQ]
                nc.vector.tensor_tensor(g, ps[6][:, :], g, ALU.mult).then_inc(a_og, 1)

            def sample_a(it, b):
                s = it * 2 + b
                for g in range(2):
                    dve.wait_ge(c_sig, s * 2 + (HEAD + g + 1))
                    dve.wait_ge(c_mul, s * 2 + (HEAD + g + 1 - 2))
                    st = sstay[:, g, KEYS - 1:0:-1]
                    nc.vector.tensor_tensor_scan(sex[:, g, 0:KEYS - 1][:, ::-1], st, st, 1.0, ALU.mult, ALU.bypass)\
                        .then_inc(c_ex, 1)
                    dve.wait_ge(c_ex, s * 2 + (HEAD + g + 1))
                    bt = sbeta[:, g, 0:KEYS - 1]
                    nc.vector.tensor_tensor(bt, bt, sex[:, g, 0:KEYS - 1], ALU.mult).then_inc(c_mul, 1)
                for g in range(2):
                    dve.wait_ge(c_av, s * 2 + (HEAD + g + 1))
                    for h in range(2):
                        rows = slice(HD * h, HD * (h + 1))
                        dst = gT[rows, 4 * g:4 * g + 4, bass.ds(s * NEW + SEQ, NEW)]
                        src = bass.AP(ps[6 + g][rows, 0:1].tensor, 0, [[1, 1]]) if False else diag(ps[6 + g], rows, NEW * h)
                        ins = nc.vector.tensor_tensor(dst, src, dst, ALU.mult)
                    ins.then_inc(c_og, 1)

            def diag(bank, rows, off):
                v5 = bank[rows, 0:NC].rearrange("p (a n) -> p a n", a=4)
                a = v5[:, :, off:off + NEW]
                ap = [list(x_) for x_ in a.ap]
                ap[-2][0] = P + 32
                return bass.AP(a.tensor, a.offset, ap)

            with dve.Fori(0, NSEQ // 2) as it:
                for b in range(2):
                    sample_a(it, b)

            def residual(layer):
                for t in range(TT):
                    n = layer * TT + t
                    dve.wait_ge(s_ysq, 2 * n + 2)
                    link(nc.vector.tensor_tensor(small[:, 6:7], small[:, 4:5], small[:, 5:6], ALU.add))
                    nc.vector.tensor_scalar(small[:, 7:8], small[:, 6:7], 1.0 / D, EPS, ALU.mult, ALU.add).then_inc(s_yv, 1)
                    dve.wait_ge(s_ysr, n + 1)
                    link(nc.vector.reciprocal(small[:, 9:10], small[:, 8:9]))
                    for c in range(2):
                        half = slice(NC * c, NC * (c + 1))
                        ins = nc.vector.scalar_tensor_tensor(ytmp[:, t % 2, half], ps[2 * (t % 2) + c][:, :], small[:, 9:10],
                                                             G[layer][:, int(t == NT), half], ALU.mult, ALU.mult)
                        ins.then_inc(s_yt, 1)
                    dve.wait_ge(s_yt, 2 * n + 2)
                    nc.vector.tensor_tensor(x[:, t, :], x[:, t, :], ytmp[:, t % 2, :], ALU.add).then_inc(s_x2, 1)

            residual(0)
            norm(1, x, xh2)
            for g, (n, e) in enumerate(tr_of["xb"]):
                if e == "dve":
                    dve.wait_ge(s_tr, n + 1)
                    if g < KT:
                        prompt_affine(hkv, n, g, 2)
                        prompt_affine(hb, n, g, 4).then_inc(s_trV, 1)
                    else:
                        sample_affine(hkv, n, g, 2, False)
                        sample_affine(hb, n, g, 4, True)

            def rotate(a, tmp):
                h4 = a.rearrange("p t (k d) -> p t k d", d=HD)
                x1, x2 = h4[:, :, :, 0:HALF], h4[:, :, :, HALF:ROT]
                cs, sn = (const[:, c0:c0 + TT * HALF].rearrange("p (t d) -> p t d", t=TT).unsqueeze(2)
                          .to_broadcast([P, TT, 2 * PAIRS, HALF]) for c0 in (C_COS, C_SIN))
                tm = [tmp[:, TT * P * n_:TT * P * (n_ + 1)].rearrange("p (t k d) -> p t k d", t=TT, k=2 * PAIRS) for n_ in range(4)]
                nc.vector.tensor_tensor(tm[0], x1, cs, ALU.mult)
                nc.vector.tensor_tensor(tm[1], x2, sn, ALU.mult)
                nc.vector.tensor_tensor(tm[2], x2, cs, ALU.mult)
                link(nc.vector.tensor_tensor(tm[3], x1, sn, ALU.mult))
                nc.vector.tensor_tensor(x1, tm[0], tm[1], ALU.subtract)
                nc.vector.tensor_tensor(x2, tm[2], tm[3], ALU.add).then_inc(s_rot, 1)

            read_proj("bk", 0)
            read_proj("bk", 1)
            proj.wait_all(dve, pj_end[("bk", 1)])
            rotate(kbn, RH)
            read_proj("bv", 2)
            read_transposes("kb", kbT)
            read_proj("bv", 3)
            read_proj("bq", 0)
            read_proj("bq", 1)
            proj.wait_all(dve, pj_end[("bq", 1)])
            dve.wait_ge(s_rot, 1)
            rotate(qbn, RH)
            read_transposes("qb", qbT)

            with dve.Fori(0, PAIRS) as p:
                def maxes(u):
                    w = P * (NT - u)
                    mx, nb = small[:, 12:14], small[:, 16 + 4 * u:18 + 4 * u]
                    dve.wait_ge(b_s, p * NT + (HEAD + u + 1))
                    dve.wait_ge(b_nb, p * NT + (HEAD + u))
                    for c in range(2):
                        ins = nc.vector.tensor_reduce(small[:, 12 + c:13 + c], ps[2 * (u % 2) + c][:, 0:w], AX.X, ALU.max)
                    ins.then_inc(b_mx, 1)
                    dve.wait_ge(b_mx, p * NT + (HEAD + u + 1))
                    nc.vector.tensor_scalar(nb, mx, -SCALE, None, ALU.mult).then_inc(b_nb, 1)

                def combine(u):
                    w = P * (NT - u)
                    l, r, c1 = 32 + 4 * u, 34 + 4 * u, 48 + u
                    dve.wait_ge(b_p, p * (2 * NT) + (HEAD + 2 * u + 2))
                    dve.wait_ge(b_or, p * NT + (HEAD + u + 1 - NT))
                    nc.vector.reciprocal(small[:, r:r + 2], small[:, l:l + 2]).then_inc(b_rc, 1)
                    dve.wait_ge(b_rc, p * NT + (HEAD + u + 1))
                    nc.vector.scalar_tensor_tensor(small[:, c1:c1 + 1], small[:, l:l + 1], small[:, r + 1:r + 2], neglam[:, :],
                                                   ALU.mult, ALU.mult).then_inc(b_c1, 1)
                    dve.wait_ge(b_c1, p * NT + (HEAD + u + 1))
                    nc.vector.scalar_tensor_tensor(pr[:, u % 2, 0, 0:w], pr[:, u % 2, 1, 0:w], small[:, c1:c1 + 1],
                                                   pr[:, u % 2, 0, 0:w], ALU.mult, ALU.add).then_inc(b_w, 1)
                for u in range(NT):
                    maxes(u)
                    if u >= 1:
                        combine(u - 1)
                combine(NT - 1)

            dve.wait_ge(b_or, HEAD + NT * PAIRS)

            def sample_b(it, b):
                s = it * 2 + b
                for g in range(2):
                    dve.wait_ge(d_s, s * 2 + (HEAD + g + 1))
                    nc.vector.tensor_reduce(small[:, 16 + g:17 + g], ps[2 + g][:, 0:KEYS], AX.X, ALU.max).then_inc(d_mx, 1)
                    dve.wait_ge(d_mx, s * 2 + (HEAD + g + 1))
                    nc.vector.tensor_scalar(small[:, 18 + g:19 + g], small[:, 16 + g:17 + g], -SCALE, None, ALU.mult)\
                        .then_inc(d_nb, 1)
                for g in range(2):
                    dve.wait_ge(d_p, s * 2 + (HEAD + g + 1))
                    nc.vector.reciprocal(small[:, 22 + g:23 + g], small[:, 20 + g:21 + g]).then_inc(d_rc, 1)
                    dve.wait_ge(d_rc, s * 2 + (HEAD + g + 1))
                    nc.vector.tensor_tensor(small[:, 24 + g:25 + g], small[:, 22 + g:23 + g], sgn[:, :], ALU.mult).then_inc(d_rs, 1)
                    dve.wait_ge(d_rs, s * 2 + (HEAD + g + 1))
                    nc.vector.tensor_scalar(cmat[:, g, :], const[:, C_PAIR + P * g:C_PAIR + P * (g + 1)],
                                            small[:, 24 + g:25 + g], None, ALU.mult).then_inc(d_cm, 1)

            with dve.Fori(0, NSEQ // 2) as it:
                for b in range(2):
                    sample_b(it, b)

            for t in range(TT):
                dve.wait_ge(s_osq, t + 1)
                nc.vector.tensor_reduce(small[:, 8 * t:8 * t + 8], sq[:, t % 2, :].rearrange("p (h e) -> p h e", h=PAIRS),
                                        AX.X, ALU.add).then_inc(s_oss, 1)
            dve.wait_ge(s_oss, TT)
            nc.vector.tensor_scalar(small[:, 0:40], small[:, 0:40], 1.0 / P, EPS, ALU.mult, ALU.add).then_inc(s_ov, 1)
            dve.wait_ge(s_osr, 1)
            link(nc.vector.reciprocal(small[:, 0:40], small[:, 0:40]))
            dve.wait_ge(s_gsub, 1 + TT)
            for t in range(TT):
                o3 = obuf[:, t, :].rearrange("p (h e) -> p h e", h=PAIRS)
                link(nc.vector.tensor_tensor(o3, o3, small[:, 8 * t:8 * t + 8].unsqueeze(2).to_broadcast([P, PAIRS, P]), ALU.mult))
                nc.vector.tensor_tensor(obuf[:, t, :], obuf[:, t, :], gs[:, t, :], ALU.mult).then_inc(s_og, 1)
            read_transposes("og", ogT)
            residual(1)

        @block.tensor
        def _(pe):
            for s in (a_z, a_t, a_av, c_kt, c_z, c_t, c_av, b_s, b_t, b_o, d_kt, d_s, d_wt, d_o):
                pe.sem_inc(s, HEAD)
            mm, tp = nc.tensor.matmul, nc.tensor.transpose

            def weights(n):
                pe.wait_ge(s_w[n % 2], 16 * (n // 2 + 1))
                return wk[n % 2]

            def mod(n):
                group, _, c = mods[n]
                w = weights(chunk[("mod", n)])
                pe.wait_ge(s_silu_c, 1)
                if n:
                    pe.wait_ge(s_msum, n)
                for kk in range(2):
                    for j in range(4):
                        last = mm(ps[4][32 * j:32 * j + 32, :], cT[:, 2 * j + kk, :], w[:, 2 * j + kk, :],
                                  start=kk == 0, stop=kk == 1)
                last.then_inc(s_macc, 1)
                pe.wait_ge(s_msum, n + 1)
                if n:
                    pe.wait_ge(s_mdone, mod_outs(n))
                m = msum[n % 2]
                if c < 4:
                    pe.wait_ge(s_const, 16)
                    for f in range(4):
                        last = mm(ps[5][:, ROWS * f:ROWS * (f + 1)], m[:, P * f:P * (f + 1)],
                                  const[:, C_SEL:C_SEL + ROWS], start=True, stop=True)
                    last.then_inc(s_mout, 1)
                else:
                    for r, c0 in enumerate((C_EXP, C_EXS)):
                        if r:
                            pe.wait_ge(s_mdone, mod_outs(n) + 1)
                        mm(ps[5][:, :], const[:, c0:c0 + P], m, start=True, stop=True).then_inc(s_mout, 1)

            def transposes(stage, src, ready):
                for g, (n, e) in enumerate(tr_of[stage]):
                    trans.wait_free(pe, n)
                    for b, (t, k) in enumerate(tr_src(n, g)):
                        ready(g, t)
                        last = tp(ps[trans.bank(n)][:, P * b:P * (b + 1)], src[:, t, P * k:P * (k + 1)], ident)
                    last.then_inc(s_tr, 1)

            def project(kind, c, h):
                n0 = chunk[(kind, c)]
                w = weights(n0)
                js = jobs[(kind, c)]
                for n, e, job in js:
                    proj.wait_free(pe, n)
                    for k in range(KT):
                        if job[0] == "T":
                            _, f, half = job
                            last = mm(ps[proj.bank(n)][:, 0:320], w[:, k, P * f:P * (f + 1)],
                                      h[:, k, 320 * half:320 * (half + 1)], start=k == 0, stop=k == KT - 1)
                        else:
                            t = job[1]
                            last = mm(ps[proj.bank(n)][:, :], h[:, k, P * t:P * (t + 1)], w[:, k, :],
                                      start=k == 0, stop=k == KT - 1)
                    last.then_inc(s_pj, 1)

            for n in range(4):
                mod(n)
            transposes("xa", xh, lambda g, t: pe.wait_ge(s_xh, t + 1))
            trans.wait_all(pe, tr_end("xa"))
            for kind, c in steps[4:]:
                if kind == "mod":
                    mod(c)
                elif kind[0] == "a":
                    project(kind, c, hT)
                    if (kind, c) == ("av", 4):
                        proj.wait_all(pe, pj_end[("ak", 3)])
                        transposes("ka", knat, lambda g, t: None)
                else:
                    break

            proj.wait_all(pe, pj_end[("ag", 7)])
            trans.wait_all(pe, tr_end("ka"))
            pe.wait_ge(s_mdone, mod_outs(16))
            pe.wait_ge(s_zero, 2)
            pe.wait_ge(s_maskb, 1)
            with pe.Fori(0, PAIRS) as p:
                def scores(u):
                    h, q = UNITS[u]
                    w = P * (q + 1)
                    if u < 2:
                        pe.wait_ge(a_qz, p * 2 + (HEAD + u + 1))
                    pe.wait_ge(a_sig, p * 8 + (HEAD + u + 1 - 4))
                    mm(ps[u % 4][:, 0:w], qz[:, h, P * q:P * (q + 1)], kT[:, p, 0:w], start=True, stop=True)
                    mm(ps[u % 4][:, P * q:w], identb, mask_sb, start=False, stop=True, skip_group_check=True).then_inc(a_z, 1)

                def turn(u):
                    h, q = UNITS[u]
                    pe.wait_ge(a_mul, p * 8 + (HEAD + u + 1))
                    pe.wait_ge(a_at, p * 8 + (HEAD + u + 1 - 2))
                    for j in range(q + 1):
                        last = tp(ps[4 + u % 2][:, P * j:P * (j + 1)], beta[:, u % 4, P * j:P * (j + 1)], ident)
                    last.then_inc(a_t, 1)
                for u in range(8):
                    scores(u)
                    if u >= 3:
                        turn(u - 3)
                for u in range(5, 8):
                    turn(u)
                pe.wait_ge(a_at, p * 8 + (HEAD + 8))
                pe.wait_ge(a_vst, p + (HEAD + 1))
                pe.wait_ge(a_og, p + HEAD)
                for j in range(NT):
                    for h in range(2):
                        last = mm(ps[6][HD * h:HD * (h + 1), P * j:SEQ], vst[:, j, HD * h:HD * (h + 1)],
                                  AT[:, h, j, P * j:SEQ], start=j == 0, stop=True, skip_group_check=True)
                last.then_inc(a_av, 1)

            def turn_k(kcs, k_in, ready, done, s, it, b):
                pe.wait_ge(k_in[b], it * 16 + 16)
                for c in range(4):
                    pe.wait_ge(done, s * 4 + (HEAD + c + 1 - 2))
                    for a in range(2):
                        for k in range(PK):
                            last = tp(ps[c % 2][:, PAST * a + P * k:PAST * a + P * (k + 1)],
                                      kcs[b][:, k, P * (2 * c + a):P * (2 * c + a + 1)], ident)
                    last.then_inc(ready, 1)

            def sample_scores(s, b, g, q, k_read, staged, ready, free, add_mask):
                if g == 0:
                    pe.wait_ge(k_read, s * 4 + (HEAD + 4))
                    pe.wait_ge(staged, s * 3 + (HEAD + 3))
                pe.wait_ge(free, s * 2 + (HEAD + g + 1 - 2))
                for j in range(4):
                    last = mm(ps[2 + g][32 * j:32 * j + 32, 0:KEYS], q[:, 4 * g + j, :], ktc[b][:, 4 * g + j, :],
                              start=True, stop=True, skip_group_check=True)
                if add_mask:
                    last = mm(ps[2 + g][:, PAST:KEYS], identb, mask_new, start=False, stop=True, skip_group_check=True)
                last.then_inc(ready, 1)

            def sample_a(it, b, last_one):
                s = it * 2 + b
                for g in range(2):
                    sample_scores(s, b, g, qb, c_ktr, c_q, c_z, c_sig, True)
                if not last_one:
                    turn_k(kc, c_k, c_kt, c_ktr, s + 1, it + b, 1 - b)
                for g in range(2):
                    pe.wait_ge(c_mul, s * 2 + (HEAD + g + 1))
                    pe.wait_ge(c_at, s * 2 + (HEAD + g + 1 - 2))
                    for k in range(3):
                        w = P if k < 2 else NEW
                        last = tp(ps[4 + g][0:w, P * k:P * (k + 1)], sbeta[:, g, P * k:P * k + w], ident)
                    last.then_inc(c_t, 1)
                pe.wait_ge(c_v[b], it * 16 + 16)
                pe.wait_ge(c_vn[b], it * 16 + 16)
                for g in range(2):
                    pe.wait_ge(c_at, s * 2 + (HEAD + g + 1))
                    pe.wait_ge(c_og, s * 2 + (HEAD + g + 1 - 2))
                    for a in range(4):
                        pair = slice(P * (4 * g + a), P * (4 * g + a + 1))
                        out = ps[6 + g][:, P * a:P * (a + 1)]
                        for k in range(PK):
                            mm(out, vc[b][:, k, pair], sAT[:, g, k, :], start=k == 0, stop=False)
                        last = mm(out, vnew[b][0:NEW, pair], sAT[0:NEW, g, 2, :], start=False, stop=True)
                    last.then_inc(c_av, 1)

            turn_k(kc, c_k, c_kt, c_ktr, 0, 0, 0)
            with pe.Fori(0, NSEQ // 2 - 1) as it:
                for b in range(2):
                    sample_a(it, b, False)
            sample_a(NSEQ // 2 - 1, 0, False)
            sample_a(NSEQ // 2 - 1, 1, True)

            def out_projection(kind, layer, src):
                n0 = chunk[(kind, 0)]
                ws = [weights(n0), weights(n0 + 1)]
                for t in range(TT):
                    if t >= 2:
                        pe.wait_ge(s_x2, layer * TT + t - 1)
                    for c in range(2):
                        for k in range(KT):
                            last = mm(ps[2 * (t % 2) + c][:, :], src[:, k, P * t:P * (t + 1)], ws[c][:, k, :],
                                      start=k == 0, stop=k == KT - 1)
                    last.then_inc(s_y, 1)

            pe.wait_ge(c_og, HEAD + 2 * NSEQ)
            out_projection("ya", 0, gT)
            transposes("xb", xh2, lambda g, t: pe.wait_ge(s_xh, TT + t + 1))
            trans.wait_all(pe, tr_end("xb"))
            for key in (("bk", 0), ("bk", 1), ("bv", 2)):
                project(*key, hkv)
            pe.wait_ge(s_rot, 1)
            transposes("kb", kbn, lambda g, t: None)
            project("bv", 3, hkv)
            project("bq", 0, hb)
            project("bq", 1, hb)
            project("bg", 2, hb)
            pe.wait_ge(s_rot, 2)
            transposes("qb", qbn, lambda g, t: None)
            project("bg", 3, hb)

            proj.wait_all(pe, pj_end[("bg", 3)])
            trans.wait_all(pe, tr_end("qb"))
            pe.wait_ge(s_zero, 5)
            with pe.Fori(0, PAIRS) as p:
                def scores(u):
                    q = NT - 1 - u
                    w = P * (q + 1)
                    if u == 0:
                        pe.wait_ge(b_qz, p * 2 + (HEAD + 2))
                    pe.wait_ge(b_p, p * (2 * NT) + (HEAD + 2 * u + 2 - 4))
                    for c in range(2):
                        mm(ps[2 * (u % 2) + c][:, 0:w], qz[:, c, P * q:P * (q + 1)], kbT[:, p, 0:w], start=True, stop=True)
                        last = mm(ps[2 * (u % 2) + c][:, P * q:w], identb, mask_da, start=False, stop=True, skip_group_check=True)
                    last.then_inc(b_s, 1)

                def turn(u):
                    pe.wait_ge(b_w, p * NT + (HEAD + u + 1))
                    pe.wait_ge(b_wt, p * NT + (HEAD + u + 1 - 2))
                    for j in range(NT - u):
                        last = tp(ps[4 + u % 2][:, P * j:P * (j + 1)], pr[:, u % 2, 0, P * j:P * (j + 1)], ident)
                    last.then_inc(b_t, 1)

                def values(u):
                    pe.wait_ge(b_wt, p * NT + (HEAD + u + 1))
                    pe.wait_ge(b_or, p * NT + (HEAD + u + 1 - 2))
                    for j in range(NT - u):
                        last = mm(ps[6 + u % 2][:, 0:P], wT[:, u % 2, P * j:P * (j + 1)], vb[:, j, bass.ts(p, P)],
                                  start=j == 0, stop=j == NT - 1 - u)
                    last.then_inc(b_o, 1)
                for u in range(NT):
                    scores(u)
                    if u >= 1:
                        turn(u - 1)
                    if u >= 2:
                        values(u - 2)
                turn(NT - 1)
                values(NT - 2)
                values(NT - 1)

            def sample_b(it, b, last_one):
                s = it * 2 + b
                for g in range(2):
                    sample_scores(s, b, g, qbb, d_ktr, d_q, d_s, d_p, False)
                if not last_one:
                    turn_k(kcb, d_k, d_kt, d_ktr, s + 1, it + b, 1 - b)
                pe.wait_ge(d_cm, s * 2 + (HEAD + 2))
                pe.wait_ge(d_wtr, s + HEAD)
                for k in range(3):
                    w = P if k < 2 else NEW
                    for g in range(2):
                        last = mm(ps[4][0:w, P * k:P * (k + 1)], spr[:, g, P * k:P * k + w], cmat[:, g, :],
                                  start=g == 0, stop=g == 1)
                last.then_inc(d_wt, 1)
                pe.wait_ge(d_v, s * 16 + 16)
                pe.wait_ge(d_vn, s * 16 + 16)
                pe.wait_ge(d_wtr, s + (HEAD + 1))
                pe.wait_ge(d_or, s + HEAD)
                for g in range(2):
                    for k in range(3):
                        w = P if k < 2 else NEW
                        for j in range(4):
                            hh = 4 * g + j
                            v_ = vcb[:, k, P * hh:P * (hh + 1)] if k < 2 else vnewb[0:NEW, P * hh:P * (hh + 1)]
                            last = mm(ps[5][32 * j:32 * j + 32, P * g:P * (g + 1)], swT[0:w, k, NEW * hh:NEW * hh + 32], v_,
                                      start=k == 0, stop=k == 2, skip_group_check=True)
                last.then_inc(d_o, 1)

            pe.wait_ge(s_zero, 7)
            turn_k(kcb, d_k, d_kt, d_ktr, 0, 0, 0)
            with pe.Fori(0, NSEQ // 2 - 1) as it:
                for b in range(2):
                    sample_b(it, b, False)
            sample_b(NSEQ // 2 - 1, 0, False)
            sample_b(NSEQ // 2 - 1, 1, True)
            transposes("og", obuf, lambda g, t: pe.wait_ge(s_og, t + 1))
            trans.wait_all(pe, tr_end("og"))
            out_projection("yb", 1, ogT)


_OUTS = [("y_p", (1, SEQ, D)), ("y_s", (NSEQ, NEW, D)), ("ak_p", (1, 1, SEQ, 16, HD)), ("av_p", (1, 1, SEQ, 16, HD)),
         ("bk_p", (1, SEQ, 8, 2, HD)), ("bv_p", (1, SEQ, 8, P)), ("ak_s", (1, NSEQ, NEW, 16, HD)),
         ("av_s", (1, NSEQ, NEW, 16, HD)), ("bk_s", (NSEQ, NEW, 8, 2, HD)), ("bv_s", (NSEQ, NEW, 8, P))]


def kernel(**inputs):
    import concourse.bacc as _bacc
    from concourse.bass_utils import run_bass_kernel_spmd as _run

    a = {k: np.ascontiguousarray(x) for k, x in inputs.items()}

    def columns(rows):
        return np.ascontiguousarray(rows.reshape(-1, KT, P).transpose(2, 0, 1))

    direct = ["x_prompt", "x_sample", "cache_a_k", "cache_a_v", "cache_b_k", "cache_b_v", "mod_w_a", "mod_b_a", "w_in_a",
              "w_out_a", "ln_post_a", "mod_w_kv", "w_kv_b", "ln_post_b", "mod_w_b", "mod_b_b", "w_in_b", "w_out_b", "subln_b"]
    arrays = {n: a[n] for n in direct}
    arrays["cT"] = np.ascontiguousarray(columns(np.concatenate([a["c_prompt"], a["c_sample"]])).transpose(0, 2, 1))
    arrays["lnT"] = columns(np.concatenate([a["ln_pre_a"], a["ln_kv"][None], a["ln_pre_b"]]))
    arrays["biasT"] = columns(np.concatenate([a["mod_b_a"][0, :2 * D], a["mod_b_kv"], a["mod_b_b"][0, :2 * D]]))
    arrays["lam"] = np.concatenate([a["lambda_q1"], a["lambda_k1"], a["lambda_q2"], a["lambda_k2"]])
    arrays["consts"] = constant_table()
    arrays["masks"] = mask_table()
    nc = _bacc.Bacc("TRN2", target_bir_lowering=False, num_devices=1,
                    dynamic_dma_scratch_size=4096)
    ins = {n: nc.dram_tensor(f"in_{n}", x.shape, F32, kind="ExternalInput").ap() for n, x in arrays.items()}
    outs = {n: nc.dram_tensor(f"out_{n}", shape, F32, kind="ExternalOutput").ap() for n, shape in _OUTS}
    ins["o_scratch"] = nc.dram_tensor("o_scratch", (NSEQ, NEW, 2, 4, P), F32, kind="Internal").ap()
    build(nc, ins, outs)
    r = _run(nc, [{f"in_{n}": x for n, x in arrays.items()}], core_ids=[0])
    return tuple(r.results[0][f"out_{n}"] for n, _ in _OUTS)
```

```python
import math
from contextlib import ExitStack

import numpy as np
import concourse.bass as bass
from concourse import mybir
from concourse.alu_op_type import AluOpType as ALU

F32 = mybir.dt.float32
BF16 = mybir.dt.bfloat16
F32R = mybir.dt.float32r
ACT = mybir.ActivationFunctionType
AX = mybir.AxisListType

P = 128
D = 1024
KT = D // P
SEQ = 512
NT = SEQ // P
NSEQ = 8
NEW = 16
TT = NT + 1
TOK = TT * P
PAST = 256
PK = PAST // P
KEYS = PAST + NEW
PAIRS = 8
HD = 64
NC = 512
ROWS = 1 + NSEQ
SCALE = HD ** -0.5
EPS = 1e-6
NEG = -1e30
ROT = HD // 4
HALF = ROT // 2
LAMBDA_INIT = 0.8 - 0.6 * math.exp(-0.3)
HEAD = 8
UNITS = [(h, i) for i in (3, 2, 1, 0) for h in (0, 1)]
KB = 256

C_ID, C_SEL, C_EXP, C_EXS, C_COS, C_SIN, C_M0, C_M1 = 0, 128, 137, 265, 393, 433, 473, 474
C_PAIR = 475
C_N = C_PAIR + 2 * P


def constant_table():
    t = np.zeros((P, C_N), np.float32)
    p = np.arange(P)
    t[p, C_ID + p] = 1.0
    for r in range(ROWS):
        t[p % 32 == r, C_SEL + r] = 1.0
    t[p % 32 == 0, C_EXP:C_EXP + P] = 1.0
    for s in range(NSEQ):
        t[p % 32 == 1 + s, C_EXS + NEW * s:C_EXS + NEW * (s + 1)] = 1.0
    inv = np.float32(500000.0) ** (-np.arange(0, ROT, 2, dtype=np.float32) / np.float32(ROT))
    for i in range(TT):
        pos = (P * i + p) if i < NT else PAST + p % NEW
        ang = pos.astype(np.float32)[:, None] * inv[None, :].astype(np.float32)
        t[:, C_COS + HALF * i:C_COS + HALF * (i + 1)] = np.cos(ang)
        t[:, C_SIN + HALF * i:C_SIN + HALF * (i + 1)] = np.sin(ang)
    comp = (p // NEW) % 2
    t[:, C_M0] = comp == 0
    t[:, C_M1] = comp == 1
    for g in range(2):
        t[p, C_PAIR + P * g + NEW * (4 * g + p // 32) + p % NEW] = 1.0
    return t


def mask_table():
    q, k = np.arange(P)[:, None], np.arange(P)[None, :]
    return np.concatenate([
        np.where(k < q, 0.0, NEG), np.where(k // HD <= q // HD, 0.0, NEG),
        np.where(np.arange(NEW)[None, :] < q % NEW, 0.0, NEG), np.eye(P)], axis=1).astype(np.float32)


def build(nc, i, o):
    ctx = ExitStack()
    with ctx:
        def sb(name, shape, dt=F32):
            return ctx.enter_context(nc.sbuf_tensor(name, shape, dt))

        def sem(name):
            return ctx.enter_context(nc.semaphore(name))

        arena = sb("arena", [P, 141 * KB])
        at = [0]

        def region(kb):
            a = arena[:, at[0] * KB:(at[0] + kb) * KB]
            at[0] += kb
            return a

        X, RA, RB, RC, RD, KN = (region(20) for _ in range(6))
        WR, RH = region(16), region(5)

        def tok(r):
            return r.rearrange("p (t n) -> p t n", t=TT)

        def feat(r):
            return r.rearrange("p (k n) -> p k n", k=KT)

        def sub(r, a, n):
            return r[:, int(a * KB):int(a * KB) + n]

        def cut(r, a, /, **dims):
            names = " ".join(dims)
            return sub(r, a, math.prod(dims.values())).rearrange(f"p ({names}) -> p {names}", **dims)

        hhl = sb("h_parts", [P, 2, KT, TOK], F32R)
        whl = sb("w_parts", [P, 2, 2, 2 * NC], F32R)
        hhi, hlo = hhl[:, 0], hhl[:, 1]

        x = tok(X)
        wraw = [sub(WR, 4 * b, 2 * NC) for b in range(2)]
        mraw = [cut(WR, 8 + 4 * b, k=2, n=NC) for b in range(2)]
        G = [sb(f"gate_{l}", [P, 2, D]) for l in "ab"]
        modT = sb("modT", [P, 6, KT, ROWS])
        const = sb("const", [P, C_N])
        ident = const[:, C_ID:C_ID + P]
        maskf = cut(WR, 12, n=3 * P + NEW)
        maskb = sb("maskb", [P, 2 * P + NEW + P], BF16)
        mask_sb, mask_da = maskb[:, 0:P], maskb[:, P:2 * P]
        mask_new, identb = maskb[:, 2 * P:2 * P + NEW], maskb[:, 2 * P + NEW:]
        lnT = sb("lnT", [P, 3, KT])
        biasT = sb("biasT", [P, 6, KT])
        ss = sb("ss", [P, 2 * TT])
        rstd = sb("rstd", [P, 2 * TT])
        small = sb("small", [P, 64])
        ysq = sb("ysq", [P, 2, TT])
        yvar = sb("yvar", [P, 3, TT])
        neglam = sb("neglam", [P, 1])
        sgn = sb("sgn", [P, 1])
        subs = sb("subs", [P, 1])
        first = [cut(r, 0, k=KT, n=NC) for r in (RA, RB, RC, RD)]
        cT, cin = cut(RH, 0, k=KT, r=32), cut(RH, 1, k=KT, r=ROWS)
        lamv = cut(RH, 1.5, a=4, d=HD)
        gvec = [[sub(X, 8 * l + 4 * b, D) for b in range(2)] for l in range(2)]

        def msum(pos):
            return sub(RH, 3, NC) if pos % 2 == 0 else sub(RC, 16, NC) if pos < 4 else sub(X, 16, NC)

        xh, h32a = tok(KN), feat(RB)
        kT, qT, gT, v, knat, qnat = feat(RA), feat(RB), feat(RC), tok(RD), tok(KN), tok(RC)
        xh2, hkv32, hb32 = tok(RC), feat(RD), feat(RB)
        kbT, qbT, vb, kbn, qbn, obuf = feat(RA), feat(RB), tok(RD), tok(KN), tok(X), tok(X)
        ysb = tok(KN)
        junk = [sub(RH, 2 * b, NC) for b in range(2)]
        qz = cut(WR, 8, b=2, h=2, n=NC)
        AT = cut(KN, 0, h=2, j=NT, q=NC)
        vst = cut(KN, 16, b=2, j=NT, n=P)
        beta, stay, ex = cut(X, 0, b=4, n=NC), cut(X, 8, b=4, n=NC), cut(X, 16, b=2, n=NC)
        pr, wT = cut(KN, 0, b=2, c=2, n=NC), cut(KN, 8, b=2, n=NC)
        kc = [cut(KN, 8 * b, k=PK, n=D) for b in range(2)]
        vc = [cut(RD, 8 * b, k=PK, n=D) for b in range(2)]
        vnew = [sub(KN, 16, D), sub(RD, 16, D)]
        ktc = [cut(X, 8.5 * b, k=PAIRS, n=KEYS) for b in range(2)]
        qb = cut(X, 17, k=PAIRS, n=32)
        sbeta, sstay, sex = (cut(WR, 8 + 2.25 * b, g=2, n=KEYS) for b in range(3))
        sAT = cut(RH, 0, g=2, k=3, n=P)
        kcb = [cut(RD, 8 * b, k=PK, n=D) for b in range(2)]
        vcb = [kbT[:, 4 * b:4 * b + 4, 0:SEQ].rearrange("p (k c) n -> p k c n", c=2) for b in range(2)]
        vnewb = [qbT[:, 2 * b:2 * b + 2, 0:SEQ] for b in range(2)]
        ktcb = [cut(KN, 8.5 * b, k=PAIRS, n=KEYS) for b in range(2)]
        qbb = cut(KN, 17, k=PAIRS, n=32)
        WTW = P + NEW
        swT = cut(KN, 18, k=3, n=WTW)
        gate0 = G[0][:, :, :].rearrange("p a n -> p (a n)")
        spr, cmat, osb = cut(gate0, 0, g=2, n=KEYS), cut(gate0, 3, g=2, n=P), cut(gate0, 4, b=2, n=2 * P)
        sq = cut(gate0, 0, b=2, n=D)
        ps = [ctx.enter_context(nc.psum_tensor(f"bank{b}", [P, NC], F32)) for b in range(8)]

        caches = {
            "ak": i["cache_a_k"].rearrange("a s (k p) h d -> (a s) p k (h d)", p=P),
            "av": i["cache_a_v"].rearrange("a s (k p) h d -> (a s) p k (h d)", p=P),
            "bk": i["cache_b_k"].rearrange("s (k p) h c d -> s p k (h c d)", p=P),
            "bv": i["cache_b_v"].rearrange("s (k p) h d -> s p k (h d)", p=P),
        }
        out_p = {
            "y": o["y_p"].rearrange("b (t p) n -> p (b t) n", p=P),
            "ak": o["ak_p"].rearrange("a b (t p) h d -> p (a b t) (h d)", p=P),
            "av": o["av_p"].rearrange("a b (t p) h d -> p (a b t) (h d)", p=P),
            "bk": o["bk_p"].rearrange("b (t p) h c d -> p (b t) (h c d)", p=P),
            "bv": o["bv_p"].rearrange("b (t p) h d -> p (b t) (h d)", p=P),
        }
        out_s = {
            "y": o["y_s"].rearrange("s q n -> (s q) n"),
            "ak": o["ak_s"].rearrange("a s q h d -> (a s q) (h d)"),
            "av": o["av_s"].rearrange("a s q h d -> (a s q) (h d)"),
            "bk": o["bk_s"].rearrange("s q h c d -> (s q) (h c d)"),
            "bv": o["bv_s"].rearrange("s q h d -> (s q) (h d)"),
        }
        av_rows = o["av_s"].rearrange("a s q h d -> (a s) q (h d)")
        bv_rows = o["bv_s"].rearrange("s q h d -> s q (h d)")
        o_scratch, x_scratch = i["o_scratch"], i["x_scratch"]

        def piece(w, c, s):
            return w.rearrange("(k p) n -> p k n", p=P)[:, 2 * s:2 * s + 2, NC * c:NC * (c + 1)]

        wa, woa, wkv, wb, wob = (i["w_in_a"][0], i["w_out_a"][0], i["w_kv_b"], i["w_in_b"][0], i["w_out_b"][0])
        gcols = [w.rearrange("(k p) n -> p k n", p=P)[:, :, c0:c0 + D] for w, c0 in ((wa, 3 * D), (wb, D))]

        chunks = [("ak", wa, 2), ("ak", wa, 3), ("av", wa, 4), ("av", wa, 5), ("aq", wa, 0), ("aq", wa, 1),
                  ("ya", woa, 0), ("ya", woa, 1),
                  ("bk", wkv, 0), ("bk", wkv, 1), ("bv", wkv, 2), ("bv", wkv, 3), ("bq", wb, 0), ("bq", wb, 1),
                  ("yb", wob, 0), ("yb", wob, 1)]
        SL = 4
        A0, YA, B0, YB = 0, 6, 8, 14
        dst_of = {"ak": knat, "av": v, "aq": qnat, "bk": kbn, "bv": vb, "bq": qbn}
        freed, count = {}, {"act": 0, "dve": 0}
        for ci, (kind, _, _) in enumerate(chunks):
            for t in range(TT):
                engines = ("act", "dve") if kind[0] == "y" else (("act", "dve")[t % 2],)
                freed[ci, t] = []
                for e in engines:
                    count[e] += 1
                    freed[ci, t].append((e, count[e]))
        mods = [("a", i["mod_w_a"][0], c) for c in range(6)] + [("kv", i["mod_w_kv"], c) for c in range(4)] \
            + [("b", i["mod_w_b"][0], c) for c in range(6)]
        order = [0, 1, 2, 3, 4, 5, 14, 15, 6, 7, 8, 9, 10, 11, 12, 13]
        tasks, task_end = [], []
        for pos, m in enumerate(order):
            tasks += [(pos, r) for r in range(1 if mods[m][2] < 4 else 2)]
            task_end.append(len(tasks))

        def tasks_of(ci):
            return [n for n, (pos, _) in enumerate(tasks) if 0 <= ci < 6 and pos in (4 + 2 * ci, 5 + 2 * ci)]

        s_const, s_mask, s_x, s_c, s_vec = sem("const_in"), sem("mask_in"), sem("x_in"), sem("c_in"), sem("vectors_in")
        s_maskb, s_silu_c, s_cz, s_lam, s_lamx, s_sub = (sem(n) for n in (
            "masks_cast", "silu_c", "c_zeroed", "lambda_dots", "lambda_exp", "subln_scaled"))
        s_gb, s_first = sem("gate_vectors_in"), [sem(f"first_in{n}") for n in range(4)]
        s_w, s_mw = [sem(f"weights_in{b}") for b in range(2)], [sem(f"mod_weights_in{b}") for b in range(2)]
        s_whi, s_wlo, s_wu = sem("w_high"), sem("w_low"), sem("w_slot_used")
        s_mu, s_macc, s_msum, s_mout, s_mdone = (sem(n) for n in (
            "mod_slot_used", "mod_first_summed", "mod_partial_read", "mod_out", "mod_read"))
        s_dve = sem("dve_chain")
        s_ss, s_var, s_sqrt, s_xh = sem("squares_summed"), sem("variance"), sem("sqrt_done"), sem("normed_ready")
        s_tr, s_trA, s_trV = sem("transposed"), sem("transposed_read_act"), sem("transposed_read_dve")
        s_pj, s_pjA, s_pjV = sem("projected"), sem("projected_read_act"), sem("projected_read_dve")
        s_hhi, s_hlo = sem("h_high"), sem("h_low")
        s_stored = {n: sem("stored_" + n) for n in ("ak", "av", "bk", "bv")}
        s_rot = sem("rotated")
        s_yv, s_ysr, s_x2, s_xr, s_xs = (sem(n) for n in (
            "y_variance", "y_sqrt", "x_updated", "x_back", "x_spilled"))
        s_gact, s_gate = sem("gate_silu"), sem("gated")
        s_zero = sem("zeroed")
        s_gw = [[sem(f"g_weights_in{l}{b}") for b in range(2)] for l in "ab"]
        s_ghi, s_glo, s_g, s_gr = ([sem(f"g_{n}_{l}") for l in "ab"] for n in ("w_high", "w_low", "projected", "read"))
        a_qz, a_vst, a_z, a_sig, a_ex, a_mul, a_t, a_at, a_av, a_or = (sem("a_" + n) for n in (
            "q_staged", "v_staged", "z_ready", "sigmoids", "scanned", "a_ready", "t_ready", "at_ready", "o_ready", "o_read"))
        c_kt, c_krA, c_krV, c_q, c_z, c_sig, c_ex, c_mul, c_t, c_at, c_av, c_or = (sem("c_" + n) for n in (
            "k_transposed", "k_read_act", "k_read_dve", "q_staged", "z_ready", "sigmoids", "scanned",
            "a_ready", "t_ready", "at_ready", "o_ready", "o_read"))
        c_k, c_v, c_vn = ([sem(f"c_{n}_in{b}") for b in range(2)] for n in ("k", "v", "vnew"))
        b_qz, b_s, b_mx, b_nb, b_p, b_rc, b_c1, b_w, b_t, b_wt, b_o, b_or = (sem("b_" + n) for n in (
            "q_staged", "s_ready", "max", "neg_max", "p_ready", "reciprocal", "coefficient", "w_ready", "t_ready",
            "wt_ready", "o_ready", "o_read"))
        (d_kt, d_krA, d_krV, d_q, d_s, d_mx, d_nb, d_p, d_rc, d_rs, d_cm, d_wt, d_wtr, d_o, d_or) = (
            sem("d_" + n) for n in ("k_transposed", "k_read_act", "k_read_dve", "q_staged", "s_ready",
                                    "max", "neg_max", "p_ready", "reciprocal", "row_scale", "combiner", "wt_ready",
                                    "wt_read", "o_ready", "o_read"))
        d_k, d_v, d_vn, d_out = ([sem(f"d_{n}{b}") for b in range(2)] for n in ("k_in", "v_in", "vnew_in", "o_out"))
        s_osq, s_oss, s_ov, s_osr, s_og, s_oin, s_out = (sem(n) for n in (
            "o_squares", "o_sums", "o_var", "o_sqrt", "o_scaled", "o_sample_in", "y_stored"))

        def wait_slot_used(eng, n):
            ci, s = divmod(n, SL)
            if s == SL - 1:
                eng.wait_ge(s_pj, TT * (ci + 1))
            else:
                eng.wait_ge(s_wu, (SL - 1) * ci + s + 1)

        def wait_read(eng, ci, t):
            for e, v_ in freed[ci, t]:
                eng.wait_ge({"act": s_pjA, "dve": s_pjV}[e], v_)

        def wait_chunk_read(eng, ci):
            for t in (TT - 2, TT - 1):
                wait_read(eng, ci, t)

        STAGES = ("xa", "ka", "qa", "xb", "kb", "qb", "og")
        GROUPS = [("s", 0), ("s", 1)] + [("p", k) for k in range(KT)]
        tr_of, uses = {}, []
        for st in STAGES:
            tr_of[st] = []
            for g, (kind, k) in enumerate(GROUPS):
                affine = st in ("xa", "xb")
                engines = ["dve"] if (affine and kind == "s") or st == "og" else ["act", "dve"] if st == "xb" \
                    else [("act", "dve")[g % 2]]
                tr_of[st].append((len(uses), engines))
                uses.append(engines)

        def tr_done(n, e):
            return sum(e in u for u in uses[:n + 1])

        def wait_tr_read(eng, n):
            for e in uses[n]:
                eng.wait_ge({"act": s_trA, "dve": s_trV}[e], tr_done(n, e))

        def wait_stage_read(eng, st):
            n = tr_of[st][-1][0]
            for e, s_ in (("act", s_trA), ("dve", s_trV)):
                if tr_done(n, e):
                    eng.wait_ge(s_, tr_done(n, e))

        def tr_dst(dst, g):
            kind, k = GROUPS[g]
            return dst[:, k, 0:SEQ] if kind == "p" else dst[:, 4 * k:4 * k + 4, SEQ:TOK]

        def tr_bank(n, g):
            b = ps[n % 4]
            return b[:, :] if GROUPS[g][0] == "p" else b[:, :].rearrange("p (a n) -> p a n", a=4)

        H_BASE = {"xa": 0, "ya": KT, "kv": 2 * KT, "b": 3 * KT, "yb": 4 * KT}
        h_src = {"xa": h32a, "ya": feat(RB), "kv": hkv32, "b": hb32, "yb": gT}

        def split_ready(eng, name, k):
            if name in ("xa", "kv"):
                st = "xa" if name == "xa" else "xb"
                wait_tr_read(eng, tr_of[st][2 + k][0])
                wait_tr_read(eng, tr_of[st][k // 4][0])
            elif name == "ya":
                eng.wait_ge(s_gate, k + 1)
            elif name == "b":
                wait_slot_used(eng, SL * 11 + k // 2)
            else:
                wait_tr_read(eng, tr_of["og"][2 + k][0])
                wait_tr_read(eng, tr_of["og"][k // 4][0])

        block = ctx.enter_context(nc.Block())

        @block.sync
        def _(sp):
            sp.dma_start(cin, i["cT"]).then_inc(s_c, 16)
            sp.dma_start(const[:, :], i["consts"]).then_inc(s_const, 16)
            sp.dma_start(first[0], i["mod_w_a"][0].rearrange("(k p) n -> p k n", p=P)[:, :, 0:NC]).then_inc(s_first[0], 16)
            sp.dma_start(x[:, 0:NT, :], i["x_prompt"].rearrange("b (t p) n -> p (b t) n", p=P)).then_inc(s_x, 16)
            sp.dma_start(x[:, NT, :], i["x_sample"].rearrange("s q n -> (s q) n")).then_inc(s_x, 16)
            sp.dma_start(lnT[:, :, :], i["lnT"]).then_inc(s_vec, 16)
            sp.dma_start(biasT[:, :, :], i["biasT"]).then_inc(s_vec, 16)
            sp.dma_start(lamv, i["lam"].partition_broadcast(P)).then_inc(s_vec, 16)
            sp.dma_start(subs[:, :], i["subln_b"].rearrange("a (n b) -> (a n) b", b=1)).then_inc(s_vec, 16)
            for n in range(1, 4):
                sp.dma_start(first[n], i["mod_w_a"][0].rearrange("(k p) n -> p k n", p=P)[:, :, NC * n:NC * (n + 1)])\
                    .then_inc(s_first[n], 16)
            sp.dma_start(maskf, i["masks"]).then_inc(s_mask, 16)

            def load(n):
                ci, s = divmod(n, SL)
                if n >= 2:
                    sp.wait_ge(s_wlo, n - 1)
                sp.dma_start(wraw[n % 2].rearrange("p (k n) -> p k n", k=2), piece(chunks[ci][1], chunks[ci][2], s))\
                    .then_inc(s_w[n % 2], 16)

            load(0)
            load(1)
            sp.wait_ge(s_xh, TT)
            for l, (bias, ln) in enumerate(((i["mod_b_a"], i["ln_post_a"]), (i["mod_b_b"], i["ln_post_b"]))):
                sp.dma_start(gvec[l][0], bias[0, 2 * D:3 * D].partition_broadcast(P)).then_inc(s_gb, 16)
                sp.dma_start(gvec[l][1], ln[0].partition_broadcast(P)).then_inc(s_gb, 16)
            sp.wait_ge(s_maskb, 1)
            for n in range(SL * YA):
                ci, s = divmod(n, SL)
                if n >= 1:
                    sp.wait_ge(s_mu, n)
                for b in range(2):
                    m = order[4 + 2 * ci + b]
                    sp.dma_start(mraw[b], piece(mods[m][1], mods[m][2], s)).then_inc(s_mw[b], 16)
                if 2 <= n + 2 < SL * YA:
                    load(n + 2)

            def gates(l, slots):
                def one(p, b):
                    sp.dma_start(wraw[b].rearrange("p (k n) -> p k n", k=KT), gcols[l][:, :, bass.ts(p, P)]).then_inc(s_gw[l][b], 16)
                sp.wait_ge(s_wlo, slots)
                one(0, 0)
                one(1, 1)
                with sp.Fori(0, PAIRS // 2 - 1) as it:
                    for b in range(2):
                        sp.wait_ge(s_glo[l], it * 2 + (HEAD + b + 1))
                        one(it * 2 + (b + 2), b)

            gates(0, SL * YA)
            sp.wait_ge(s_glo[0], HEAD + PAIRS)
            load(SL * YA)
            load(SL * YA + 1)

            sp.wait_ge(a_or, HEAD + PAIRS)
            sp.wait_ge(s_stored["ak"], 32)
            sp.wait_ge(s_stored["av"], 32)
            with sp.Fori(0, NSEQ // 2) as it:
                for b in range(2):
                    s = it * 2 + b
                    sp.wait_ge(c_kt, s * 4 + (HEAD - 4))
                    sp.dma_start(kc[b], caches["ak"][s]).then_inc(c_k[b], 16)
                    sp.wait_ge(c_av, s * 2 + (HEAD - 2))
                    sp.dma_start(vc[b], caches["av"][s]).then_inc(c_v[b], 16)
                    sp.dma_start(vnew[b][0:NEW, :], av_rows[s]).then_inc(c_vn[b], 16)
            sp.wait_ge(c_z, HEAD + 2 * NSEQ)
            sp.dma_start(x[:, 0:NT, :], i["x_prompt"].rearrange("b (t p) n -> p (b t) n", p=P)).then_inc(s_xr, 16)
            sp.dma_start(x[:, NT, :], i["x_sample"].rearrange("s q n -> (s q) n")).then_inc(s_xr, 16)
            for n in range(SL * YA + 2, SL * B0 + 2):
                load(n)
            for t in range(TT):
                sp.wait_ge(s_x2, t + 1)
                sp.dma_start(x_scratch[:, t, :], x[:, t, :]).then_inc(s_xs, 16)
            for n in range(SL * B0 + 2, SL * YB):
                load(n)
            gates(1, SL * YB)
            sp.wait_ge(s_glo[1], HEAD + PAIRS)
            load(SL * YB)
            load(SL * YB + 1)

            sp.wait_ge(b_or, HEAD + NT * PAIRS)
            sp.wait_ge(s_stored["bv"], 32)
            with sp.Fori(0, NSEQ // 2) as it:
                for b in range(2):
                    s = it * 2 + b
                    sp.wait_ge(d_kt, s * 4 + (HEAD - 4))
                    sp.dma_start(kcb[b], caches["bk"][s]).then_inc(d_k[b], 16)
                    sp.wait_ge(d_o, s + (HEAD - 1))
                    for k in range(PK):
                        sp.dma_start(vcb[b][:, k], caches["bv"][s, :, k].rearrange("p (c n) -> p c n", c=2)).then_inc(d_v[b], 16)
                    sp.dma_start(vnewb[b][0:NEW], bv_rows[s].rearrange("q (c n) -> q c n", c=2)).then_inc(d_vn[b], 16)
            for b in range(2):
                sp.wait_ge(d_out[b], HEAD + 16 * 4 * NSEQ // 2)
            sp.dma_start(obuf[:, NT, :].rearrange("p (g j n) -> p g j n", g=2, j=4),
                         o_scratch.rearrange("s q g j n -> (s q) g j n")).then_inc(s_oin, 16)
            sp.wait_ge(s_tr, tr_of["og"][-1][0] + 1)
            sp.dma_start(x[:, :, :], x_scratch).then_inc(s_xr, 16)
            for n in range(SL * YB + 2, SL * len(chunks)):
                load(n)
            for t in range(TT):
                sp.wait_ge(s_x2, TT + t + 1)
                sp.dma_start(out_p["y"][:, t, :] if t < NT else out_s["y"], x[:, t, :]).then_inc(s_out, 16)
            sp.wait_ge(s_out, 16 * TT)
            sp.wait_ge(s_stored["bk"], 32)

        @block.gpsimd
        def _(pool):
            for s in (a_qz, a_vst, c_q, b_qz, d_q):
                pool.sem_inc(s, HEAD)
            zeros = [0]

            def zero(a):
                zeros[0] += 1
                nc.gpsimd.memset(a, 0.0).then_inc(s_zero, 1)
                pool.wait_ge(s_zero, zeros[0])

            def store(name, src, ci):
                wait_chunk_read(pool, ci)
                pool.dma_start(out_p[name], src[:, 0:NT, :]).then_inc(s_stored[name], 16)
                pool.dma_start(out_s[name], src[:, NT, :]).then_inc(s_stored[name], 16)

            def stage_q(p, b, src, done, scores, per):
                pool.wait_ge(scores, p * per + (HEAD - per))
                for h in range(2):
                    rows = slice(HD * h, HD * (h + 1))
                    nc.gpsimd.tensor_copy(qz[rows, b, h, :], src[rows, p, 0:SEQ]).then_inc(done, 1)
                    pool.wait_ge(done, p * 2 + (HEAD + h + 1))

            def stage_new(s, b, kt_src, q_src, kt_dst, q_dst, done, z_done):
                pool.wait_ge(z_done, s * 2 + HEAD)
                new = bass.ds(s * NEW + SEQ, NEW)
                copies = [(kt_dst[b][:, :, PAST:KEYS], kt_src[:, :, new]), (q_dst[0:HD, :, 0:NEW], q_src[0:HD, :, new]),
                          (q_dst[HD:P, :, NEW:32], q_src[HD:P, :, new])]
                for n, (dst, src) in enumerate(copies):
                    nc.gpsimd.tensor_copy(dst, src).then_inc(done, 1)
                    pool.wait_ge(done, s * 3 + (HEAD + n + 1))

            store("ak", knat, 1)
            store("av", v, 3)
            wait_chunk_read(pool, 5)
            wait_stage_read(pool, "qa")
            pool.wait_ge(s_mdone, len(tasks))
            pool.wait_ge(s_stored["ak"], 32)
            for b in range(2):
                zero(qz[HD:P, b, 0, :])
                zero(qz[0:HD, b, 1, :])
            with pool.Fori(0, PAIRS // 2) as it:
                for b in range(2):
                    p = it * 2 + b
                    stage_q(p, b, qT, a_qz, a_z, 8)
                    pool.wait_ge(a_av, p + (HEAD - 1))
                    nc.gpsimd.tensor_copy(vst[:, b], v[:, 0:NT, bass.ts(p, P)]).then_inc(a_vst, 1)
                    pool.wait_ge(a_vst, p + (HEAD + 1))
            pool.wait_ge(a_or, HEAD + PAIRS)
            zero(qb)
            with pool.Fori(0, NSEQ // 2) as it:
                for b in range(2):
                    stage_new(it * 2 + b, b, kT, qT, ktc, qb, c_q, c_z)
            pool.wait_ge(s_rot, 1)
            store("bk", kbn, 9)
            store("bv", vb, 11)
            wait_chunk_read(pool, 13)
            wait_stage_read(pool, "qb")
            pool.wait_ge(s_stored["bk"], 32)
            for b in range(2):
                zero(qz[HD:P, b, 0, :])
                zero(qz[0:HD, b, 1, :])
            with pool.Fori(0, PAIRS // 2) as it:
                for b in range(2):
                    stage_q(it * 2 + b, b, qbT, b_qz, b_s, NT)
            pool.wait_ge(b_or, HEAD + NT * PAIRS)
            zero(qbb)
            zero(swT[:, :, P:WTW])

            with pool.Fori(0, NSEQ // 2) as it:
                for b in range(2):
                    stage_new(it * 2 + b, b, kbT, qbT, ktcb, qbb, d_q, d_s)

        @block.scalar
        def _(act):
            for s in (a_sig, a_at, c_sig, c_krA, c_at, b_p, b_wt, b_or, d_p, d_krA, d_wtr, d_or, *d_out, *s_ghi, *s_gr):
                act.sem_inc(s, HEAD)
            act.wait_ge(s_c, 16)
            act.wait_ge(s_cz, 1)
            nc.scalar.activation(cT[:, :, 0:ROWS], cin, ACT.Silu).then_inc(s_silu_c, 1)
            act.wait_ge(s_lam, 1)
            nc.scalar.activation(small[:, 2:4], small[:, 0:2], ACT.Exp).then_inc(s_lamx, 1)

            def square_sums(stage, dst, ready):
                for t in range(TT):
                    ready(t)
                    nc.scalar.activation(dst[:, t, :], x[:, t, :], ACT.Square,
                                         accum_out=ss[:, TT * stage + t:TT * stage + t + 1]).then_inc(s_ss, 1)
                act.wait_ge(s_var, stage + 1)
                nc.scalar.activation(ss[:, TT * stage:TT * (stage + 1)], ss[:, TT * stage:TT * (stage + 1)],
                                     ACT.Sqrt).then_inc(s_sqrt, 1)

            def w_high(n):
                if n >= SL * len(chunks):
                    return
                act.wait_ge(s_w[n % 2], 16 * (n // 2 + 1))
                if n >= 2:
                    wait_slot_used(act, n - 2)
                nc.scalar.activation(whl[:, n % 2, 0, :], wraw[n % 2], ACT.Copy).then_inc(s_whi, 1)

            def h_high(name, k):
                split_ready(act, name, k)
                nc.scalar.activation(hhi[:, k, :], h_src[name][:, k, :], ACT.Copy).then_inc(s_hhi, 1)

            def read(ci):
                kind, c = chunks[ci][0], chunks[ci][2]
                for t in range(TT):
                    for e, v_ in freed[ci, t]:
                        if e != "act":
                            continue
                        act.wait_ge(s_pj, TT * ci + t + 1)
                        if kind[0] == "y":
                            act.wait_ge(s_pjA, v_ - 1)
                            nc.scalar.activation(junk[t % 2], ps[t][:, :], ACT.Square,
                                                 accum_out=ysq[:, c, t:t + 1]).then_inc(s_pjA, 1)
                        else:
                            nc.scalar.activation(dst_of[kind][:, t, NC * (c % 2):NC * (c % 2 + 1)], ps[t][:, :],
                                                 ACT.Copy).then_inc(s_pjA, 1)

            def stream(c0, c1):
                for n in range(SL * c0, SL * c1):
                    if n + 1 < SL * c1:
                        w_high(n + 1)
                    if n % SL == SL - 1:
                        read(n // SL)
                    if n // SL == 11:
                        for k in range(2 * (n % SL), 2 * (n % SL) + 2):
                            h_high("b", k)

            def read_transposes(stage, dst):
                for g, (n, es) in enumerate(tr_of[stage]):
                    if "act" in es:
                        act.wait_ge(s_tr, n + 1)
                        nc.scalar.activation(tr_dst(dst, g), tr_bank(n, g), ACT.Copy).then_inc(s_trA, 1)

            def affine(dst, k, bank, vs):
                nc.scalar.activation(dst, bank, ACT.Identity, bias=modT[:, vs, k, 0:1], scale=modT[:, vs + 1, k, 0:1])\
                    .then_inc(s_trA, 1)

            act.wait_ge(s_x, 32)
            square_sums(0, xh, lambda t: None)
            w_high(0)
            act.wait_ge(s_mdone, 4)
            for g, (n, es) in enumerate(tr_of["xa"]):
                if "act" in es:
                    act.wait_ge(s_tr, n + 1)
                    affine(h32a[:, GROUPS[g][1], 0:SEQ], GROUPS[g][1], tr_bank(n, g), 0)
            for k in range(KT):
                h_high("xa", k)
            stream(A0, YA)
            act.wait_ge(s_stored["ak"], 32)
            read_transposes("ka", kT)
            read_transposes("qa", qT)

            def g_high(l, p, b):
                act.wait_ge(s_gw[l][b], (p - b) * 8 + 16)
                act.wait_ge(s_g[l], p * 2 + (HEAD - 2))
                nc.scalar.activation(whl[:, b, 0, :], wraw[b], ACT.Copy).then_inc(s_ghi[l], 1)

            def read_g(l, p, half):
                act.wait_ge(s_g[l], p * 2 + (HEAD + half + 1))
                nc.scalar.activation(gT[:, p, 320 * half:320 * (half + 1)], ps[7][:, 0:320], ACT.Copy).then_inc(s_gr[l], 1)

            wait_stage_read(act, "qa")
            wait_chunk_read(act, 5)
            act.wait_ge(s_mdone, len(tasks))

            def sig(p, u):
                w = P * (UNITS[u][1] + 1)
                act.wait_ge(a_z, p * 8 + (HEAD + u + 1))
                act.wait_ge(a_t, p * 8 + (HEAD + u + 1 - 4))
                nc.scalar.activation(beta[:, u % 4, 0:w], ps[u % 4][:, 0:w], ACT.Sigmoid, scale=SCALE)
                nc.scalar.activation(stay[:, u % 4, 0:w], ps[u % 4][:, 0:w], ACT.Sigmoid, scale=-SCALE).then_inc(a_sig, 1)

            def read_at(p, u):
                h, q = UNITS[u]
                act.wait_ge(a_t, p * 8 + (HEAD + u + 1))
                if u == 0:
                    act.wait_ge(a_av, p + HEAD)
                nc.scalar.activation(AT[:, h, 0:q + 1, P * q:P * (q + 1)],
                                     ps[4 + u % 2][:, 0:P * (q + 1)].rearrange("p (j n) -> p j n", j=q + 1),
                                     ACT.Copy).then_inc(a_at, 1)

            def pair_a(p, b, more):
                for u in range(4):
                    sig(p, u + 4)
                    read_at(p, u)
                    if u == 0 and more:
                        g_high(0, p + 1, 1 - b)
                read_g(0, p, 0)
                for u in range(4):
                    if more:
                        sig(p + 1, u)
                    read_at(p, u + 4)
                read_g(0, p, 1)

            g_high(0, 0, 0)
            for u in range(4):
                sig(0, u)
            with act.Fori(0, PAIRS // 2 - 1) as it:
                for b in range(2):
                    pair_a(it * 2 + b, b, True)
            pair_a(PAIRS - 2, 0, True)
            pair_a(PAIRS - 1, 1, False)

            def read_k(ktcs, ready, done, s, b):
                for c in (0, 2):
                    act.wait_ge(ready, s * 4 + (HEAD + c + 1))
                    nc.scalar.activation(ktcs[b][:, 2 * c:2 * c + 2, 0:PAST],
                                         ps[0][:, :].rearrange("p (a n) -> p a n", a=2), ACT.Copy).then_inc(done, 1)

            def sig_s(s):
                for g in range(2):
                    act.wait_ge(c_z, s * 2 + (HEAD + g + 1))
                    act.wait_ge(c_t, s * 2 + (HEAD + g - 1))
                    nc.scalar.activation(sbeta[:, g, :], ps[2 + g][:, 0:KEYS], ACT.Sigmoid, scale=SCALE)
                    nc.scalar.activation(sstay[:, g, :], ps[2 + g][:, 0:KEYS], ACT.Sigmoid, scale=-SCALE).then_inc(c_sig, 1)

            def sample_a(s, b, more):
                if more:
                    read_k(ktc, c_kt, c_krA, s + 1, 1 - b)
                for g in range(2):
                    act.wait_ge(c_t, s * 2 + (HEAD + g + 1))
                    act.wait_ge(c_av, s * 2 + (HEAD + g - 1))
                    nc.scalar.activation(sAT[:, g, 0:2, :], ps[4 + g][:, 0:2 * P].rearrange("p (k n) -> p k n", k=2), ACT.Copy)
                    nc.scalar.activation(sAT[0:NEW, g, 2, :], ps[4 + g][0:NEW, 2 * P:3 * P], ACT.Copy).then_inc(c_at, 1)
                if more:
                    sig_s(s + 1)

            act.wait_ge(a_or, HEAD + PAIRS)
            read_k(ktc, c_kt, c_krA, 0, 0)
            sig_s(0)
            with act.Fori(0, NSEQ // 2 - 1) as it:
                for b in range(2):
                    sample_a(it * 2 + b, b, True)
            sample_a(NSEQ - 2, 0, True)
            sample_a(NSEQ - 1, 1, False)

            w_high(SL * YA)
            act.wait_ge(s_gr[0], HEAD + 2 * PAIRS)
            for k in range(KT):
                nc.scalar.activation(gT[:, k, :], gT[:, k, :], ACT.Silu).then_inc(s_gact, 1)
                if k >= 1:
                    h_high("ya", k - 1)
            h_high("ya", KT - 1)
            stream(YA, B0)

            def y_root(layer):
                act.wait_ge(s_yv, layer + 1)
                nc.scalar.activation(yvar[:, 2, :], yvar[:, 1, :], ACT.Sqrt).then_inc(s_ysr, 1)

            y_root(0)
            square_sums(1, xh2, lambda t: act.wait_ge(s_x2, t + 1))
            w_high(SL * B0)
            for g, (n, es) in enumerate(tr_of["xb"]):
                if "act" in es:
                    act.wait_ge(s_tr, n + 1)
                    affine(hkv32[:, GROUPS[g][1], 0:SEQ], GROUPS[g][1], tr_bank(n, g), 2)
            for k in range(KT):
                h_high("kv", k)
            act.wait_ge(s_xs, 16 * TT)
            stream(B0, YB)
            read_transposes("kb", kbT)
            read_transposes("qb", qbT)

            act.wait_ge(s_stored["bk"], 32)
            wait_stage_read(act, "qb")

            def exps(p, u):
                w = P * (NT - u)
                act.wait_ge(b_nb, p * NT + (HEAD + u + 1))
                act.wait_ge(b_t, p * NT + (HEAD + u - 1))
                for c in range(2):
                    nc.scalar.activation(pr[:, u % 2, c, 0:w], ps[2 * (u % 2) + c][:, 0:w], ACT.Exp,
                                         bias=small[:, 16 + 4 * u + c:17 + 4 * u + c], scale=SCALE,
                                         accum_out=small[:, 32 + 4 * u + c:33 + 4 * u + c]).then_inc(b_p, 1)

            def read_wt(p, u):
                w = P * (NT - u)
                act.wait_ge(b_t, p * NT + (HEAD + u + 1))
                act.wait_ge(b_o, p * NT + (HEAD + u - 1))
                nc.scalar.activation(wT[:, u % 2, 0:w], ps[4 + u % 2][:, 0:w], ACT.Copy).then_inc(b_wt, 1)

            def read_o(p, u):
                act.wait_ge(b_o, p * NT + (HEAD + u + 1))
                nc.scalar.activation(obuf[:, NT - 1 - u, bass.ts(p, P)], ps[6][:, 0:P], ACT.Copy,
                                     scale=small[:, 34 + 4 * u:35 + 4 * u]).then_inc(b_or, 1)

            def pair_b(p, b, more):
                for u in range(NT):
                    if u < NT - 1:
                        exps(p, u + 1)
                    elif more:
                        exps(p + 1, 0)
                    read_wt(p, u)
                    if u:
                        read_o(p, u - 1)
                    if u == 0 and more:
                        g_high(1, p + 1, 1 - b)
                    if u == 1:
                        read_g(1, p, 0)
                read_o(p, NT - 1)
                read_g(1, p, 1)

            g_high(1, 0, 0)
            exps(0, 0)
            with act.Fori(0, PAIRS // 2 - 1) as it:
                for b in range(2):
                    pair_b(it * 2 + b, b, True)
            pair_b(PAIRS - 2, 0, True)
            pair_b(PAIRS - 1, 1, False)

            def exps_s(s):
                for g in range(2):
                    act.wait_ge(d_nb, s * 2 + (HEAD + g + 1))
                    act.wait_ge(d_wt, s + HEAD)
                    nc.scalar.activation(spr[:, g, :], ps[2 + g][:, 0:KEYS], ACT.Exp, bias=small[:, 18 + g:19 + g],
                                         scale=SCALE, accum_out=small[:, 20 + g:21 + g]).then_inc(d_p, 1)

            def sample_b(s, b, more):
                if more:
                    read_k(ktcb, d_kt, d_krA, s + 1, 1 - b)
                act.wait_ge(d_wt, s + (HEAD + 1))
                act.wait_ge(d_o, s + HEAD)
                nc.scalar.activation(swT[:, 0:2, 0:P], ps[4][:, 0:2 * P].rearrange("p (k n) -> p k n", k=2), ACT.Copy)
                nc.scalar.activation(swT[0:NEW, 2, 0:P], ps[4][0:NEW, 2 * P:3 * P], ACT.Copy).then_inc(d_wtr, 1)
                if more:
                    exps_s(s + 1)
                act.wait_ge(d_o, s + (HEAD + 1))
                act.wait_ge(d_out[b], (s - b) * 32 + HEAD)
                nc.scalar.activation(osb[:, b], ps[5][:, 0:2 * P], ACT.Copy).then_inc(d_or, 1)
                act.wait_ge(d_or, s + (HEAD + 1))
                for j in range(4):
                    act.dma_start(o_scratch[s][:, :, j, :],
                                  osb[32 * j:32 * j + NEW, b].rearrange("p (g n) -> p g n", g=2)).then_inc(d_out[b], 16)

            act.wait_ge(b_or, HEAD + NT * PAIRS)
            act.wait_ge(b_w, HEAD + NT * PAIRS)
            read_k(ktcb, d_kt, d_krA, 0, 0)
            exps_s(0)
            with act.Fori(0, NSEQ // 2 - 1) as it:
                for b in range(2):
                    sample_b(it * 2 + b, b, True)
            sample_b(NSEQ - 2, 0, True)
            sample_b(NSEQ - 1, 1, False)

            act.wait_ge(s_gr[1], HEAD + 2 * PAIRS)
            w_high(SL * YB)
            for b in range(2):
                act.wait_ge(d_out[b], HEAD + 16 * 4 * NSEQ // 2)
            act.wait_ge(d_wt, HEAD + NSEQ)
            for t in range(TT):
                if t == NT:
                    act.wait_ge(s_oin, 16)
                if t >= 2:
                    act.wait_ge(s_oss, t - 1)
                nc.scalar.activation(sq[:, t % 2, :], obuf[:, t, :], ACT.Square).then_inc(s_osq, 1)
            act.wait_ge(s_ov, 1)
            nc.scalar.activation(small[:, 0:40], small[:, 0:40], ACT.Sqrt).then_inc(s_osr, 1)
            for k in range(KT):
                nc.scalar.activation(gT[:, k, :], gT[:, k, :], ACT.Silu).then_inc(s_gact, 1)
            for k in range(KT):
                h_high("yb", k)
            stream(YB, len(chunks))
            y_root(1)

        @block.vector
        def _(dve):
            chain = [0]

            def link(ins):
                chain[0] += 1
                ins.then_inc(s_dve, 1)
                dve.wait_ge(s_dve, chain[0])

            for s in (a_ex, a_mul, a_or, c_ex, c_mul, c_or, c_krV, b_mx, b_nb, b_rc, b_c1, b_w, d_mx, d_nb, d_rc, d_rs,
                      d_cm, d_krV, *s_glo):
                dve.sem_inc(s, HEAD)
            nc.vector.memset(cT[:, :, ROWS:32], 0.0).then_inc(s_cz, 1)

            def norm(stage, dst):
                a, b = TT * stage, TT * (stage + 1)
                dve.wait_ge(s_ss, b)
                nc.vector.tensor_scalar(ss[:, a:b], ss[:, a:b], 1.0 / D, EPS, ALU.mult, ALU.add).then_inc(s_var, 1)
                dve.wait_ge(s_sqrt, stage + 1)
                link(nc.vector.reciprocal(rstd[:, a:b], ss[:, a:b]))
                for t in range(TT):
                    nc.vector.tensor_scalar(dst[:, t, :], x[:, t, :], rstd[:, a + t:a + t + 1], None, ALU.mult)\
                        .then_inc(s_xh, 1)

            def read_partial(pos):
                if pos >= 2:
                    dve.wait_ge(s_mout, task_end[pos - 2])
                if pos < 4:
                    dve.wait_ge(s_macc, pos + 1)
                else:
                    dve.wait_ge(s_mu, SL * ((pos - 4) // 2 + 1))
                nc.vector.tensor_copy(msum(pos), ps[5 + pos % 2][:, :]).then_inc(s_msum, 1)

            def finish_task(n):
                pos, r = tasks[n]
                group, _, c = mods[order[pos]]
                dve.wait_ge(s_mout, n + 1)
                if c < 4:
                    vi = {"a": 0, "kv": 2, "b": 4}[group] + c // 2
                    k = slice(4 * (c % 2), 4 * (c % 2) + 4)
                    dst = modT[:, vi, k, :]
                    bias = biasT[:, vi, k].unsqueeze(2).to_broadcast([P, 4, ROWS])
                    src = ps[7][:, 0:4 * ROWS].rearrange("p (k r) -> p k r", k=4)
                    if vi % 2 == 0:
                        nc.vector.tensor_tensor(dst, src, bias, ALU.add).then_inc(s_mdone, 1)
                    else:
                        link(nc.vector.tensor_tensor(dst, src, bias, ALU.add))
                        ln = lnT[:, vi // 2, k].unsqueeze(2).to_broadcast([P, 4, ROWS])
                        link(nc.vector.tensor_scalar(dst, dst, 1.0, None, ALU.add))
                        nc.vector.tensor_tensor(dst, dst, ln, ALU.mult).then_inc(s_mdone, 1)
                else:
                    layer = 0 if group == "a" else 1
                    half = slice(NC * (c - 4), NC * (c - 3))
                    dve.wait_ge(s_gb, 64)
                    dst = G[layer][:, r, half]
                    link(nc.vector.tensor_tensor(dst, ps[7][:, :], gvec[layer][0][:, half], ALU.add))
                    nc.vector.tensor_tensor(dst, dst, gvec[layer][1][:, half], ALU.mult).then_inc(s_mdone, 1)

            def w_low(n):
                if n >= SL * len(chunks):
                    return
                dve.wait_ge(s_whi, n + 1)
                nc.vector.tensor_tensor(whl[:, n % 2, 1, :], wraw[n % 2], whl[:, n % 2, 0, :].bitcast(F32), ALU.subtract)\
                    .then_inc(s_wlo, 1)

            def h_low(name, k):
                dve.wait_ge(s_hhi, H_BASE[name] + k + 1)
                nc.vector.tensor_tensor(hlo[:, k, :], h_src[name][:, k, :], hhi[:, k, :].bitcast(F32), ALU.subtract)\
                    .then_inc(s_hlo, 1)

            def read(ci):
                kind, c = chunks[ci][0], chunks[ci][2]
                for t in range(TT):
                    for e, v_ in freed[ci, t]:
                        if e != "dve":
                            continue
                        dve.wait_ge(s_pj, TT * ci + t + 1)
                        if kind[0] == "y":
                            dst = ysb[:, t, NC * c:NC * (c + 1)]
                            dve.wait_ge(s_pjA, freed[ci, t][0][1])
                        else:
                            dst = dst_of[kind][:, t, NC * (c % 2):NC * (c % 2 + 1)]
                        if kind[0] == "y":
                            gate = G[int(ci >= YB)][:, int(t == NT), NC * c:NC * (c + 1)]
                            nc.vector.tensor_tensor(dst, ps[t][:, :], gate, ALU.mult).then_inc(s_pjV, 1)
                        else:
                            nc.vector.tensor_copy(dst, ps[t][:, :]).then_inc(s_pjV, 1)

            def stream(c0, c1):
                for n in range(SL * c0, SL * c1):
                    ci, s = divmod(n, SL)
                    if n + 1 < SL * c1:
                        w_low(n + 1)
                    todo = tasks_of(ci - 1) if ci < YA else []
                    if s < len(todo):
                        finish_task(todo[s])
                    if s == SL - 1:
                        if ci < YA:
                            read_partial(4 + 2 * ci)
                            read_partial(5 + 2 * ci)
                        read(ci)
                    if ci == 11:
                        h_low("b", 2 * s)
                        h_low("b", 2 * s + 1)
                    if n == SL * 10 - 1:
                        wait_chunk_read(dve, 9)
                        rotate(kbn, WR[:, 8 * KB:16 * KB])

            dve.wait_ge(s_vec, 64)
            link(nc.vector.tensor_tensor(lamv[:, 0:3:2, :], lamv[:, 0:3:2, :], lamv[:, 1:4:2, :], ALU.mult))
            nc.vector.tensor_reduce(small[:, 0:2], lamv[:, 0:3:2, :], AX.X, ALU.add).then_inc(s_lam, 1)
            dve.wait_ge(s_lamx, 1)
            link(nc.vector.tensor_tensor(small[:, 10:11], small[:, 3:4], small[:, 2:3], ALU.subtract))
            link(nc.vector.tensor_scalar(neglam[:, :], small[:, 10:11], -LAMBDA_INIT, None, ALU.add))
            dve.wait_ge(s_const, 16)
            link(nc.vector.scalar_tensor_tensor(sgn[:, :], const[:, C_M1:C_M1 + 1], neglam[:, 0:1],
                                                const[:, C_M0:C_M0 + 1], ALU.mult, ALU.add))
            link(nc.vector.tensor_scalar(subs[:, :], subs[:, :], 1.0 - LAMBDA_INIT, None, ALU.mult))
            read_partial(0)
            finish_task(0)
            dve.wait_ge(s_x, 32)
            norm(0, xh)
            for n in range(1, 4):
                read_partial(n)
                finish_task(n)
            dve.wait_ge(s_mask, 16)
            nc.vector.tensor_copy(maskb[:, :], maskf).then_inc(s_maskb, 1)

            def sample_affine(dst, n, g, vs):
                j = GROUPS[g][1]
                k = slice(4 * j, 4 * j + 4)
                d = dst[:, k, SEQ:TOK].rearrange("p k (s q) -> p k s q", s=NSEQ)
                src = ps[n % 4][:, :].rearrange("p (k s q) -> p k s q", k=4, q=NEW)
                sc, sh = (modT[:, vs + a, k, 1:ROWS].unsqueeze(3).to_broadcast([P, 4, NSEQ, NEW]) for a in (1, 0))
                link(nc.vector.tensor_tensor(d, src, sc, ALU.mult))
                return nc.vector.tensor_tensor(d, d, sh, ALU.add)

            def prompt_affine(dst, n, g, vs):
                k = GROUPS[g][1]
                return nc.vector.tensor_scalar(dst[:, k, 0:SEQ], tr_bank(n, g), modT[:, vs + 1, k, 0:1],
                                               modT[:, vs, k, 0:1], ALU.mult, ALU.add)

            w_low(0)
            for g, (n, es) in enumerate(tr_of["xa"]):
                if "dve" in es:
                    dve.wait_ge(s_tr, n + 1)
                    (prompt_affine if GROUPS[g][0] == "p" else sample_affine)(h32a, n, g, 0).then_inc(s_trV, 1)
            for k in range(KT):
                h_low("xa", k)

            def read_transposes(stage, dst):
                for g, (n, es) in enumerate(tr_of[stage]):
                    if "dve" in es:
                        dve.wait_ge(s_tr, n + 1)
                        nc.vector.tensor_copy(tr_dst(dst, g), tr_bank(n, g)).then_inc(s_trV, 1)

            def rotate(a, tmp):
                h4 = a.rearrange("p t (k d) -> p t k d", d=HD)
                x1, x2 = h4[:, :, :, 0:HALF], h4[:, :, :, HALF:ROT]
                cs, sn = (const[:, c0:c0 + TT * HALF].rearrange("p (t d) -> p t d", t=TT).unsqueeze(2)
                          .to_broadcast([P, TT, 2 * PAIRS, HALF]) for c0 in (C_COS, C_SIN))
                tm = [tmp[:, TT * P * n_:TT * P * (n_ + 1)].rearrange("p (t k d) -> p t k d", t=TT, k=2 * PAIRS)
                      for n_ in range(3)]
                nc.vector.tensor_tensor(tm[0], x1, cs, ALU.mult)
                nc.vector.tensor_tensor(tm[1], x2, sn, ALU.mult)
                link(nc.vector.tensor_tensor(tm[2], x1, sn, ALU.mult))
                link(nc.vector.tensor_tensor(x1, tm[0], tm[1], ALU.subtract))
                link(nc.vector.tensor_tensor(tm[0], x2, cs, ALU.mult))
                nc.vector.tensor_tensor(x2, tm[2], tm[0], ALU.add).then_inc(s_rot, 1)

            stream(A0, YA)
            for n in tasks_of(YA - 1):
                finish_task(n)
            read_transposes("ka", kT)
            read_transposes("qa", qT)
            dve.wait_ge(s_stored["ak"], 32)

            def g_low(l, p, b):
                dve.wait_ge(s_ghi[l], p + (HEAD + 1))
                nc.vector.tensor_tensor(whl[:, b, 1, :], wraw[b], whl[:, b, 0, :].bitcast(F32), ALU.subtract)\
                    .then_inc(s_glo[l], 1)

            def scan(p, u):
                w = P * (UNITS[u][1] + 1)
                dve.wait_ge(a_sig, p * 8 + (HEAD + u + 1))
                dve.wait_ge(a_mul, p * 8 + (HEAD + u - 1))
                st = stay[:, u % 4, w - 1:0:-1]
                nc.vector.tensor_tensor_scan(ex[:, u % 2, 0:w - 1][:, ::-1], st, st, 1.0, ALU.mult, ALU.bypass)\
                    .then_inc(a_ex, 1)

            def mul(p, u):
                w = P * (UNITS[u][1] + 1)
                dve.wait_ge(a_ex, p * 8 + (HEAD + u + 1))
                b = beta[:, u % 4, 0:w - 1]
                nc.vector.tensor_tensor(b, b, ex[:, u % 2, 0:w - 1], ALU.mult).then_inc(a_mul, 1)

            def pair_a(p, b, more):
                mul(p, 3)
                for u in range(4):
                    scan(p, u + 4)
                    mul(p, u + 4)
                    if u == 1 and more:
                        g_low(0, p + 1, 1 - b)
                for u in range(4):
                    if more:
                        scan(p + 1, u)
                        if u < 3:
                            mul(p + 1, u)
                dve.wait_ge(a_av, p + (HEAD + 1))
                nc.vector.tensor_copy(qT[:, p, 0:SEQ], ps[6][:, :]).then_inc(a_or, 1)

            g_low(0, 0, 0)
            for u in range(4):
                scan(0, u)
                if u < 3:
                    mul(0, u)
            with dve.Fori(0, PAIRS // 2 - 1) as it:
                for b in range(2):
                    pair_a(it * 2 + b, b, True)
            pair_a(PAIRS - 2, 0, True)
            pair_a(PAIRS - 1, 1, False)

            def read_k(ktcs, ready, done, s, b):
                for c in (1, 3):
                    dve.wait_ge(ready, s * 4 + (HEAD + c + 1))
                    nc.vector.tensor_copy(ktcs[b][:, 2 * c:2 * c + 2, 0:PAST],
                                          ps[1][:, :].rearrange("p (a n) -> p a n", a=2)).then_inc(done, 1)

            def diag(bank, rows, off):
                a = bank[rows, 0:NC].rearrange("p (a n) -> p a n", a=4)[:, :, off:off + NEW]
                ap = [list(x_) for x_ in a.ap]
                ap[-2][0] = P + 32
                return bass.AP(a.tensor, a.offset, ap)

            def scans_s(s):
                for g in range(2):
                    dve.wait_ge(c_sig, s * 2 + (HEAD + g + 1))
                    dve.wait_ge(c_mul, s * 2 + (HEAD + g - 1))
                    st = sstay[:, g, KEYS - 1:0:-1]
                    nc.vector.tensor_tensor_scan(sex[:, g, 0:KEYS - 1][:, ::-1], st, st, 1.0, ALU.mult, ALU.bypass)\
                        .then_inc(c_ex, 1)
                for g in range(2):
                    dve.wait_ge(c_ex, s * 2 + (HEAD + g + 1))
                    bt = sbeta[:, g, 0:KEYS - 1]
                    nc.vector.tensor_tensor(bt, bt, sex[:, g, 0:KEYS - 1], ALU.mult).then_inc(c_mul, 1)

            def sample_a(s, b, more):
                if more:
                    read_k(ktc, c_kt, c_krV, s + 1, 1 - b)
                    scans_s(s + 1)
                for g in range(2):
                    dve.wait_ge(c_av, s * 2 + (HEAD + g + 1))
                    for h in range(2):
                        rows = slice(HD * h, HD * (h + 1))
                        ins = nc.vector.tensor_copy(qT[rows, 4 * g:4 * g + 4, bass.ds(s * NEW + SEQ, NEW)],
                                                    diag(ps[6 + g], rows, NEW * h))
                    ins.then_inc(c_or, 1)

            read_k(ktc, c_kt, c_krV, 0, 0)
            scans_s(0)
            with dve.Fori(0, NSEQ // 2 - 1) as it:
                for b in range(2):
                    sample_a(it * 2 + b, b, True)
            sample_a(NSEQ - 2, 0, True)
            sample_a(NSEQ - 1, 1, False)

            w_low(SL * YA)
            dve.wait_ge(c_or, HEAD + 2 * NSEQ)
            for k in range(KT):
                dve.wait_ge(s_gact, k + 1)
                nc.vector.tensor_tensor(qT[:, k, :], qT[:, k, :], gT[:, k, :], ALU.mult).then_inc(s_gate, 1)
                if k >= 1:
                    h_low("ya", k - 1)
            h_low("ya", KT - 1)
            stream(YA, B0)

            def residual(layer):
                dve.wait_ge(s_pjA, freed[(YA, YB)[layer] + 1, TT - 1][0][1])
                link(nc.vector.tensor_tensor(yvar[:, 0, :], ysq[:, 0, :], ysq[:, 1, :], ALU.add))
                nc.vector.tensor_scalar(yvar[:, 1, :], yvar[:, 0, :], 1.0 / D, EPS, ALU.mult, ALU.add).then_inc(s_yv, 1)
                dve.wait_ge(s_ysr, layer + 1)
                link(nc.vector.reciprocal(yvar[:, 0, :], yvar[:, 2, :]))
                dve.wait_ge(s_xr, 32 + 16 * layer)
                dve.wait_ge(s_pjV, freed[(YA, YB)[layer] + 1, TT - 1][1][1])
                for t in range(TT):
                    nc.vector.scalar_tensor_tensor(x[:, t, :], ysb[:, t, :], yvar[:, 0, t:t + 1], x[:, t, :],
                                                   ALU.mult, ALU.add).then_inc(s_x2, 1)

            residual(0)
            norm(1, xh2)
            w_low(SL * B0)
            for g, (n, es) in enumerate(tr_of["xb"]):
                dve.wait_ge(s_tr, n + 1)
                if GROUPS[g][0] == "p":
                    dve.wait_ge(s_trA, tr_done(n, "act"))
                    prompt_affine(hb32, n, g, 4).then_inc(s_trV, 1)
                else:
                    sample_affine(hkv32, n, g, 2)
                    sample_affine(hb32, n, g, 4).then_inc(s_trV, 1)
            for k in range(KT):
                h_low("kv", k)
            dve.wait_ge(s_xs, 16 * TT)
            stream(B0, YB)
            wait_chunk_read(dve, 13)
            rotate(qbn, WR[:, 8 * KB:16 * KB])
            read_transposes("kb", kbT)
            read_transposes("qb", qbT)

            dve.wait_ge(s_stored["bk"], 32)

            def maxes(p, u):
                w = P * (NT - u)
                mx, nb = small[:, 12:14], small[:, 16 + 4 * u:18 + 4 * u]
                dve.wait_ge(b_s, p * NT + (HEAD + u + 1))
                dve.wait_ge(b_nb, p * NT + (HEAD + u))
                for c in range(2):
                    ins = nc.vector.tensor_reduce(small[:, 12 + c:13 + c], ps[2 * (u % 2) + c][:, 0:w], AX.X, ALU.max)
                ins.then_inc(b_mx, 1)
                dve.wait_ge(b_mx, p * NT + (HEAD + u + 1))
                nc.vector.tensor_scalar(nb, mx, -SCALE, None, ALU.mult).then_inc(b_nb, 1)

            def combine(p, u):
                w = P * (NT - u)
                l, r, c1 = 32 + 4 * u, 34 + 4 * u, 48 + u
                dve.wait_ge(b_p, p * (2 * NT) + (HEAD + 2 * u + 2))
                dve.wait_ge(b_or, p * NT + (HEAD + u + 1 - NT))
                nc.vector.reciprocal(small[:, r:r + 2], small[:, l:l + 2]).then_inc(b_rc, 1)
                dve.wait_ge(b_rc, p * NT + (HEAD + u + 1))
                nc.vector.scalar_tensor_tensor(small[:, c1:c1 + 1], small[:, l:l + 1], small[:, r + 1:r + 2], neglam[:, :],
                                               ALU.mult, ALU.mult).then_inc(b_c1, 1)
                dve.wait_ge(b_c1, p * NT + (HEAD + u + 1))
                nc.vector.scalar_tensor_tensor(pr[:, u % 2, 0, 0:w], pr[:, u % 2, 1, 0:w], small[:, c1:c1 + 1],
                                               pr[:, u % 2, 0, 0:w], ALU.mult, ALU.add).then_inc(b_w, 1)

            def pair_b(p, b, more):
                for u in range(NT):
                    combine(p, u)
                    if u < 2:
                        maxes(p, u + 2)
                    elif more:
                        maxes(p + 1, u - 2)
                    if u == 0 and more:
                        g_low(1, p + 1, 1 - b)

            g_low(1, 0, 0)
            maxes(0, 0)
            maxes(0, 1)
            with dve.Fori(0, PAIRS // 2 - 1) as it:
                for b in range(2):
                    pair_b(it * 2 + b, b, True)
            pair_b(PAIRS - 2, 0, True)
            pair_b(PAIRS - 1, 1, False)

            def soft_s(s):
                for g in range(2):
                    dve.wait_ge(d_s, s * 2 + (HEAD + g + 1))
                    nc.vector.tensor_reduce(small[:, 16 + g:17 + g], ps[2 + g][:, 0:KEYS], AX.X, ALU.max).then_inc(d_mx, 1)
                    dve.wait_ge(d_mx, s * 2 + (HEAD + g + 1))
                    nc.vector.tensor_scalar(small[:, 18 + g:19 + g], small[:, 16 + g:17 + g], -SCALE, None, ALU.mult)\
                        .then_inc(d_nb, 1)
                for g in range(2):
                    dve.wait_ge(d_p, s * 2 + (HEAD + g + 1))
                    nc.vector.reciprocal(small[:, 22 + g:23 + g], small[:, 20 + g:21 + g]).then_inc(d_rc, 1)
                    dve.wait_ge(d_rc, s * 2 + (HEAD + g + 1))
                    nc.vector.tensor_tensor(small[:, 24 + g:25 + g], small[:, 22 + g:23 + g], sgn[:, :], ALU.mult).then_inc(d_rs, 1)
                    dve.wait_ge(d_rs, s * 2 + (HEAD + g + 1))
                    nc.vector.tensor_scalar(cmat[:, g, :], const[:, C_PAIR + P * g:C_PAIR + P * (g + 1)],
                                            small[:, 24 + g:25 + g], None, ALU.mult).then_inc(d_cm, 1)

            dve.wait_ge(b_or, HEAD + NT * PAIRS)
            read_k(ktcb, d_kt, d_krV, 0, 0)
            soft_s(0)
            with dve.Fori(0, NSEQ // 2 - 1) as it:
                for b in range(2):
                    read_k(ktcb, d_kt, d_krV, it * 2 + (b + 1), 1 - b)
                    soft_s(it * 2 + (b + 1))
            read_k(ktcb, d_kt, d_krV, NSEQ - 1, 1)
            soft_s(NSEQ - 1)

            w_low(SL * YB)
            for t in range(TT):
                dve.wait_ge(s_osq, t + 1)
                nc.vector.tensor_reduce(small[:, 8 * t:8 * t + 8], sq[:, t % 2, :].rearrange("p (h e) -> p h e", h=PAIRS),
                                        AX.X, ALU.add).then_inc(s_oss, 1)
            dve.wait_ge(s_oss, TT)
            nc.vector.tensor_scalar(small[:, 0:40], small[:, 0:40], 1.0 / P, EPS, ALU.mult, ALU.add).then_inc(s_ov, 1)
            dve.wait_ge(s_osr, 1)
            link(nc.vector.reciprocal(small[:, 0:40], small[:, 0:40]))
            for t in reversed(range(TT)):
                o3 = obuf[:, t, :].rearrange("p (h e) -> p h e", h=PAIRS)
                nc.vector.tensor_tensor(o3, o3, small[:, 8 * t:8 * t + 8].unsqueeze(2).to_broadcast([P, PAIRS, P]), ALU.mult)\
                    .then_inc(s_og, 1)
            for g, (n, es) in enumerate(tr_of["og"]):
                dve.wait_ge(s_tr, n + 1)
                dve.wait_ge(s_gact, KT + (KT if g < 2 else GROUPS[g][1] + 1))
                nc.vector.scalar_tensor_tensor(tr_dst(gT, g), tr_bank(n, g), subs[:, 0:1], tr_dst(gT, g), ALU.mult, ALU.mult)\
                    .then_inc(s_trV, 1)
            for k in range(KT):
                h_low("yb", k)
            stream(YB, len(chunks))
            residual(1)

        @block.tensor
        def _(pe):
            for s in (a_z, a_t, a_av, c_kt, c_z, c_t, c_av, b_s, b_t, b_o, d_kt, d_s, d_wt, d_o, *s_g):
                pe.sem_inc(s, HEAD)
            mm, tp = nc.tensor.matmul, nc.tensor.transpose

            def parts(out, a, w, start, stop):
                (ah, al), (wh, wl) = a, w
                mm(out, ah, wh, start=start, stop=False)
                mm(out, ah, wl, start=False, stop=False)
                return mm(out, al, wh, start=False, stop=stop)

            def second(n):
                pos, r = tasks[n]
                pe.wait_ge(s_msum, pos + 1)
                if n:
                    pe.wait_ge(s_mdone, n)
                m, c = msum(pos), mods[order[pos]][2]
                if c < 4:
                    for f in range(4):
                        last = mm(ps[7][:, ROWS * f:ROWS * (f + 1)], m[:, P * f:P * (f + 1)],
                                  const[:, C_SEL:C_SEL + ROWS], start=True, stop=True)
                else:
                    c0 = (C_EXP, C_EXS)[r]
                    last = mm(ps[7][:, :], const[:, c0:c0 + P], m, start=True, stop=True)
                last.then_inc(s_mout, 1)

            def first_mod(n):
                pe.wait_ge(s_first[n], 16)
                if n >= 2:
                    pe.wait_ge(s_msum, n - 1)
                for kk in range(2):
                    for j in range(4):
                        last = mm(ps[5 + n % 2][32 * j:32 * j + 32, :], cT[:, 4 * kk + j, :], first[n][:, 4 * kk + j, :],
                                  start=kk == 0, stop=kk == 1)
                last.then_inc(s_macc, 1)

            def side_mods(ci, s):
                n = SL * ci + s
                if s == 0:
                    pe.wait_ge(s_msum, 4 + 2 * ci)
                for b in range(2):
                    pe.wait_ge(s_mw[b], 16 * (n + 1))
                    for kk in range(2):
                        k = 2 * s + kk
                        j = (k + 2 * b) % 4
                        last = mm(ps[5 + b][32 * j:32 * j + 32, :], cT[:, k, :], mraw[b][:, kk, :],
                                  start=k < 4, stop=k >= 4, skip_group_check=True)
                last.then_inc(s_mu, 1)

            def transposes(stage, src, ready=None, after=None):
                for g, (n, es) in enumerate(tr_of[stage]):
                    if after is not None and g < 4:
                        wait_read(pe, after, n % 4)
                    if n >= 4:
                        wait_tr_read(pe, n - 4)
                    kind, k = GROUPS[g]
                    for b in range(4):
                        t, f = (b, k) if kind == "p" else (NT, 4 * k + b)
                        if ready is not None:
                            ready(t)
                        last = tp(ps[n % 4][:, P * b:P * (b + 1)], src[:, t, P * f:P * (f + 1)], ident)
                    last.then_inc(s_tr, 1)

            def project(ci, name):
                for s in range(SL):
                    n = SL * ci + s
                    pe.wait_ge(s_wlo, n + 1)
                    w = [whl[:, n % 2, a, :].rearrange("p (k n) -> p k n", k=2) for a in range(2)]
                    for kk in range(2):
                        k = 2 * s + kk
                        pe.wait_ge(s_hlo, H_BASE[name] + k + 1)
                        for t in range(TT):
                            if k == 0 and ci:
                                wait_read(pe, ci - 1, t)
                            tt = slice(P * t, P * (t + 1))
                            last = parts(ps[t][:, :], (hhi[:, k, tt], hlo[:, k, tt]), (w[0][:, kk, :], w[1][:, kk, :]),
                                         k == 0, k == KT - 1)
                            if k == KT - 1:
                                last.then_inc(s_pj, 1)
                    if s < SL - 1:
                        last.then_inc(s_wu, 1)
                    if ci < YA:
                        side_mods(ci, s)
                    todo = tasks_of(ci - 1) if ci < YA else []
                    if s < len(todo):
                        second(todo[s])

            pe.wait_ge(s_silu_c, 1)
            pe.wait_ge(s_const, 16)
            for n in range(4):
                first_mod(n)
                second(n)
            transposes("xa", xh, lambda t: pe.wait_ge(s_xh, t + 1))
            wait_stage_read(pe, "xa")
            for ci in range(A0, YA):
                project(ci, "xa")
            for n in tasks_of(YA - 1):
                second(n)
            transposes("ka", knat, after=5)
            wait_chunk_read(pe, 5)
            transposes("qa", qnat)

            def gate(l, p, b, n):
                half, kq = divmod(n, 4)
                if n == 0:
                    pe.wait_ge(s_glo[l], p + (HEAD + 1))
                if kq == 0:
                    pe.wait_ge(s_gr[l], p * 2 + (HEAD + half))
                w = [whl[:, b, a, :].rearrange("p (k n) -> p k n", k=KT) for a in range(2)]
                for k in (2 * kq, 2 * kq + 1):
                    tt = slice(320 * half, 320 * (half + 1))
                    last = parts(ps[7][:, 0:320], (w[0][:, k, :], w[1][:, k, :]), (hhi[:, k, tt], hlo[:, k, tt]),
                                 k == 0, k == KT - 1)
                if kq == 3:
                    last.then_inc(s_g[l], 1)

            pe.wait_ge(s_mdone, len(tasks))
            pe.wait_ge(s_maskb, 1)
            wait_stage_read(pe, "qa")
            pe.wait_ge(s_zero, 4)

            def scores_a(p, b, u):
                h, q = UNITS[u]
                w = P * (q + 1)
                if u < 2:
                    pe.wait_ge(a_qz, p * 2 + (HEAD + u + 1))
                pe.wait_ge(a_sig, p * 8 + (HEAD + u - 3))
                mm(ps[u % 4][:, 0:w], qz[:, b, h, P * q:P * (q + 1)], kT[:, p, 0:w], start=True, stop=True)
                mm(ps[u % 4][:, P * q:w], identb, mask_sb, start=False, stop=True, skip_group_check=True).then_inc(a_z, 1)

            def turn_a(p, u):
                h, q = UNITS[u]
                pe.wait_ge(a_mul, p * 8 + (HEAD + u + 1))
                pe.wait_ge(a_at, p * 8 + (HEAD + u - 1))
                for j in range(q + 1):
                    last = tp(ps[4 + u % 2][:, P * j:P * (j + 1)], beta[:, u % 4, P * j:P * (j + 1)], ident)
                last.then_inc(a_t, 1)

            def values_a(p, b):
                pe.wait_ge(a_at, p * 8 + (HEAD + 8))
                pe.wait_ge(a_vst, p + (HEAD + 1))
                pe.wait_ge(a_or, p + HEAD)
                for j in range(NT):
                    for h in range(2):
                        last = mm(ps[6][HD * h:HD * (h + 1), P * j:SEQ], vst[:, b, j, HD * h:HD * (h + 1)],
                                  AT[:, h, j, P * j:SEQ], start=j == 0, stop=True, skip_group_check=True)
                last.then_inc(a_av, 1)

            def pair_a(p, b, more):
                for u in range(4):
                    scores_a(p, b, u + 4)
                    turn_a(p, u)
                    gate(0, p, b, u)
                for u in range(4):
                    if more:
                        scores_a(p + 1, 1 - b, u)
                    turn_a(p, u + 4)
                    gate(0, p, b, u + 4)
                values_a(p, b)

            for u in range(4):
                scores_a(0, 0, u)
            with pe.Fori(0, PAIRS // 2 - 1) as it:
                for b in range(2):
                    pair_a(it * 2 + b, b, True)
            pair_a(PAIRS - 2, 0, True)
            pair_a(PAIRS - 1, 1, False)

            def turn_k(kcs, k_in, ready, done, s, b):
                pe.wait_ge(k_in[b], (s - b) * 8 + 16)
                for c in range(4):
                    pe.wait_ge(done[c % 2], s * 2 + (HEAD + c // 2))
                    for a in range(2):
                        for k in range(PK):
                            last = tp(ps[c % 2][:, PAST * a + P * k:PAST * a + P * (k + 1)],
                                      kcs[b][:, k, P * (2 * c + a):P * (2 * c + a + 1)], ident)
                    last.then_inc(ready, 1)

            def scores_s(s, ktcs, b, q, k_read, staged, ready, free, add_mask):
                for k_r in k_read:
                    pe.wait_ge(k_r, s * 2 + (HEAD + 2))
                pe.wait_ge(staged, s * 3 + (HEAD + 3))
                for g in range(2):
                    pe.wait_ge(free, s * 2 + (HEAD + g - 1))
                    for j in range(4):
                        last = mm(ps[2 + g][32 * j:32 * j + 32, 0:KEYS], q[:, 4 * g + j, :], ktcs[b][:, 4 * g + j, :],
                                  start=True, stop=True, skip_group_check=True)
                    if add_mask:
                        last = mm(ps[2 + g][:, PAST:KEYS], identb, mask_new, start=False, stop=True, skip_group_check=True)
                    last.then_inc(ready, 1)

            def sample_a(s, b, more):
                if more:
                    turn_k(kc, c_k, c_kt, (c_krA, c_krV), s + 1, 1 - b)
                for g in range(2):
                    pe.wait_ge(c_mul, s * 2 + (HEAD + g + 1))
                    pe.wait_ge(c_at, s * 2 + (HEAD + g - 1))
                    for k in range(3):
                        w = P if k < 2 else NEW
                        last = tp(ps[4 + g][0:w, P * k:P * (k + 1)], sbeta[:, g, P * k:P * k + w], ident)
                    last.then_inc(c_t, 1)
                if more:
                    scores_s(s + 1, ktc, 1 - b, qb, (c_krA, c_krV), c_q, c_z, c_sig, True)
                pe.wait_ge(c_v[b], (s - b) * 8 + 16)
                pe.wait_ge(c_vn[b], (s - b) * 8 + 16)
                for g in range(2):
                    pe.wait_ge(c_at, s * 2 + (HEAD + g + 1))
                    pe.wait_ge(c_or, s * 2 + (HEAD + g - 1))
                    for a in range(4):
                        pair = slice(P * (4 * g + a), P * (4 * g + a + 1))
                        out = ps[6 + g][:, P * a:P * (a + 1)]
                        for k in range(PK):
                            mm(out, vc[b][:, k, pair], sAT[:, g, k, :], start=k == 0, stop=False)
                        last = mm(out, vnew[b][0:NEW, pair], sAT[0:NEW, g, 2, :], start=False, stop=True)
                    last.then_inc(c_av, 1)

            pe.wait_ge(s_gr[0], HEAD + 2 * PAIRS)
            pe.wait_ge(a_or, HEAD + PAIRS)
            turn_k(kc, c_k, c_kt, (c_krA, c_krV), 0, 0)
            scores_s(0, ktc, 0, qb, (c_krA, c_krV), c_q, c_z, c_sig, True)
            with pe.Fori(0, NSEQ // 2 - 1) as it:
                for b in range(2):
                    sample_a(it * 2 + b, b, True)
            sample_a(NSEQ - 2, 0, True)
            sample_a(NSEQ - 1, 1, False)

            pe.wait_ge(c_at, HEAD + 2 * NSEQ)
            pe.wait_ge(c_krA, HEAD + 2 * NSEQ)
            pe.wait_ge(c_krV, HEAD + 2 * NSEQ)
            for ci in range(YA, B0):
                project(ci, "ya")
            transposes("xb", xh2, lambda t: pe.wait_ge(s_xh, TT + t + 1), after=B0 - 1)
            wait_stage_read(pe, "xb")
            for ci in range(B0, YB):
                project(ci, "kv" if ci < B0 + 4 else "b")
            pe.wait_ge(s_rot, 1)
            transposes("kb", kbn, after=YB - 1)
            pe.wait_ge(s_rot, 2)
            transposes("qb", qbn)

            wait_stage_read(pe, "qb")
            pe.wait_ge(s_zero, 9)

            def scores_b(p, b, u):
                q = NT - 1 - u
                w = P * (q + 1)
                if u == 0:
                    pe.wait_ge(b_qz, p * 2 + (HEAD + 2))
                pe.wait_ge(b_p, p * (2 * NT) + (HEAD + 2 * u - 2))
                for c in range(2):
                    mm(ps[2 * (u % 2) + c][:, 0:w], qz[:, b, c, P * q:P * (q + 1)], kbT[:, p, 0:w], start=True, stop=True)
                    last = mm(ps[2 * (u % 2) + c][:, P * q:w], identb, mask_da, start=False, stop=True, skip_group_check=True)
                last.then_inc(b_s, 1)

            def turn_b(p, u):
                pe.wait_ge(b_w, p * NT + (HEAD + u + 1))
                pe.wait_ge(b_wt, p * NT + (HEAD + u - 1))
                for j in range(NT - u):
                    last = tp(ps[4 + u % 2][:, P * j:P * (j + 1)], pr[:, u % 2, 0, P * j:P * (j + 1)], ident)
                last.then_inc(b_t, 1)

            def values_b(p, u):
                pe.wait_ge(b_wt, p * NT + (HEAD + u + 1))
                pe.wait_ge(b_or, p * NT + (HEAD + u))
                for j in range(NT - u):
                    last = mm(ps[6][:, 0:P], wT[:, u % 2, P * j:P * (j + 1)], vb[:, j, bass.ts(p, P)],
                              start=j == 0, stop=j == NT - 1 - u)
                last.then_inc(b_o, 1)

            def pair_b(p, b, more):
                for u in range(NT):
                    if u < 2:
                        scores_b(p, b, u + 2)
                    elif more:
                        scores_b(p + 1, 1 - b, u - 2)
                    gate(1, p, b, 2 * u)
                    turn_b(p, u)
                    if u:
                        values_b(p, u - 1)
                    gate(1, p, b, 2 * u + 1)
                values_b(p, NT - 1)

            scores_b(0, 0, 0)
            scores_b(0, 0, 1)
            with pe.Fori(0, PAIRS // 2 - 1) as it:
                for b in range(2):
                    pair_b(it * 2 + b, b, True)
            pair_b(PAIRS - 2, 0, True)
            pair_b(PAIRS - 1, 1, False)

            def sample_b(s, b, more):
                if more:
                    turn_k(kcb, d_k, d_kt, (d_krA, d_krV), s + 1, 1 - b)
                pe.wait_ge(d_cm, s * 2 + (HEAD + 2))
                pe.wait_ge(d_wtr, s + HEAD)
                for k in range(3):
                    w = P if k < 2 else NEW
                    for g in range(2):
                        last = mm(ps[4][0:w, P * k:P * (k + 1)], spr[:, g, P * k:P * k + w], cmat[:, g, :],
                                  start=g == 0, stop=g == 1)
                last.then_inc(d_wt, 1)
                if more:
                    scores_s(s + 1, ktcb, 1 - b, qbb, (d_krA, d_krV), d_q, d_s, d_p, False)
                pe.wait_ge(d_v[b], (s - b) * 16 + 32)
                pe.wait_ge(d_vn[b], (s - b) * 8 + 16)
                pe.wait_ge(d_wtr, s + (HEAD + 1))
                pe.wait_ge(d_or, s + HEAD)
                for g in range(2):
                    for k in range(3):
                        w = P if k < 2 else NEW
                        for j in range(4):
                            hh = 4 * g + j
                            v_ = vcb[b][:, k, g, P * j:P * (j + 1)] if k < 2 else vnewb[b][0:NEW, g, P * j:P * (j + 1)]
                            last = mm(ps[5][32 * j:32 * j + 32, P * g:P * (g + 1)], swT[0:w, k, NEW * hh:NEW * hh + 32], v_,
                                      start=k == 0, stop=k == 2, skip_group_check=True)
                last.then_inc(d_o, 1)

            pe.wait_ge(s_zero, 11)
            pe.wait_ge(b_or, HEAD + NT * PAIRS)
            turn_k(kcb, d_k, d_kt, (d_krA, d_krV), 0, 0)
            scores_s(0, ktcb, 0, qbb, (d_krA, d_krV), d_q, d_s, d_p, False)
            with pe.Fori(0, NSEQ // 2 - 1) as it:
                for b in range(2):
                    sample_b(it * 2 + b, b, True)
            sample_b(NSEQ - 2, 0, True)
            sample_b(NSEQ - 1, 1, False)
            pe.wait_ge(d_or, HEAD + NSEQ)
            transposes("og", obuf, lambda t: pe.wait_ge(s_og, TT - t))
            wait_stage_read(pe, "og")
            for ci in range(YB, len(chunks)):
                project(ci, "yb")


_OUTS = [("y_p", (1, SEQ, D)), ("y_s", (NSEQ, NEW, D)), ("ak_p", (1, 1, SEQ, 16, HD)), ("av_p", (1, 1, SEQ, 16, HD)),
         ("bk_p", (1, SEQ, 8, 2, HD)), ("bv_p", (1, SEQ, 8, P)), ("ak_s", (1, NSEQ, NEW, 16, HD)),
         ("av_s", (1, NSEQ, NEW, 16, HD)), ("bk_s", (NSEQ, NEW, 8, 2, HD)), ("bv_s", (NSEQ, NEW, 8, P))]


def kernel(**inputs):
    import concourse.bacc as _bacc
    from concourse.bass_utils import run_bass_kernel_spmd as _run

    a = {k: np.ascontiguousarray(x) for k, x in inputs.items()}

    def columns(rows):
        return np.ascontiguousarray(rows.reshape(-1, KT, P).transpose(2, 0, 1))

    direct = ["x_prompt", "x_sample", "cache_a_k", "cache_a_v", "cache_b_k", "cache_b_v", "mod_w_a", "mod_b_a", "w_in_a",
              "w_out_a", "ln_post_a", "mod_w_kv", "w_kv_b", "ln_post_b", "mod_w_b", "mod_b_b", "w_in_b", "w_out_b", "subln_b"]
    arrays = {n: a[n] for n in direct}
    arrays["cT"] = np.ascontiguousarray(columns(np.concatenate([a["c_prompt"], a["c_sample"]])).transpose(0, 2, 1))
    arrays["lnT"] = columns(np.concatenate([a["ln_pre_a"], a["ln_kv"][None], a["ln_pre_b"]]))
    arrays["biasT"] = columns(np.concatenate([a["mod_b_a"][0, :2 * D], a["mod_b_kv"], a["mod_b_b"][0, :2 * D]]))
    arrays["lam"] = np.concatenate([a["lambda_q1"], a["lambda_k1"], a["lambda_q2"], a["lambda_k2"]])
    arrays["consts"] = constant_table()
    arrays["masks"] = mask_table()
    nc = _bacc.Bacc("TRN2", target_bir_lowering=False, num_devices=1,
                    dynamic_dma_scratch_size=4096)
    ins = {n: nc.dram_tensor(f"in_{n}", x.shape, F32, kind="ExternalInput").ap() for n, x in arrays.items()}
    outs = {n: nc.dram_tensor(f"out_{n}", shape, F32, kind="ExternalOutput").ap() for n, shape in _OUTS}
    ins["x_scratch"] = nc.dram_tensor("x_scratch", (P, TT, D), F32, kind="Internal").ap()
    ins["o_scratch"] = nc.dram_tensor("o_scratch", (NSEQ, NEW, 2, 4, P), F32, kind="Internal").ap()
    build(nc, ins, outs)
    r = _run(nc, [{f"in_{n}": x for n, x in arrays.items()}], core_ids=[0])
    return tuple(r.results[0][f"out_{n}"] for n, _ in _OUTS)
```

```python
import math
from contextlib import ExitStack

import numpy as np
import concourse.bass as bass
from concourse import mybir
from concourse.alu_op_type import AluOpType as ALU

F32 = mybir.dt.float32
BF16 = mybir.dt.bfloat16
F32R = mybir.dt.float32r
ACT = mybir.ActivationFunctionType
AX = mybir.AxisListType

P = 128
D = 1024
KT = D // P
SEQ = 512
NT = SEQ // P
NSEQ = 8
NEW = 16
TT = NT + 1
TOK = TT * P
PAST = 256
PK = PAST // P
KEYS = PAST + NEW
PAIRS = 8
HD = 64
NC = 512
ROWS = 1 + NSEQ
SCALE = HD ** -0.5
EPS = 1e-6
NEG = -1e30
ROT = HD // 4
HALF = ROT // 2
LAMBDA_INIT = 0.8 - 0.6 * math.exp(-0.3)
HEAD = 8
UNITS = [(h, i) for i in (3, 2, 1, 0) for h in (0, 1)]
KB = 256

C_ID, C_SEL, C_EXP, C_EXS, C_COS, C_SIN, C_M0, C_M1 = 0, 128, 137, 265, 393, 433, 473, 474
C_PAIR = 475
C_N = C_PAIR + 2 * P


def constant_table():
    t = np.zeros((P, C_N), np.float32)
    p = np.arange(P)
    t[p, C_ID + p] = 1.0
    for r in range(ROWS):
        t[p % 32 == r, C_SEL + r] = 1.0
    t[p % 32 == 0, C_EXP:C_EXP + P] = 1.0
    for s in range(NSEQ):
        t[p % 32 == 1 + s, C_EXS + NEW * s:C_EXS + NEW * (s + 1)] = 1.0
    inv = np.float32(500000.0) ** (-np.arange(0, ROT, 2, dtype=np.float32) / np.float32(ROT))
    for i in range(TT):
        pos = (P * i + p) if i < NT else PAST + p % NEW
        ang = pos.astype(np.float32)[:, None] * inv[None, :].astype(np.float32)
        t[:, C_COS + HALF * i:C_COS + HALF * (i + 1)] = np.cos(ang)
        t[:, C_SIN + HALF * i:C_SIN + HALF * (i + 1)] = np.sin(ang)
    comp = (p // NEW) % 2
    t[:, C_M0] = comp == 0
    t[:, C_M1] = comp == 1
    for g in range(2):
        t[p, C_PAIR + P * g + NEW * (4 * g + p // 32) + p % NEW] = 1.0
    return t


def mask_table():
    q, k = np.arange(P)[:, None], np.arange(P)[None, :]
    return np.concatenate([
        np.where(k < q, 0.0, NEG), np.where(k // HD <= q // HD, 0.0, NEG),
        np.where(np.arange(NEW)[None, :] < q % NEW, 0.0, NEG), np.eye(P)], axis=1).astype(np.float32)


def build(nc, i, o):
    ctx = ExitStack()
    with ctx:
        def sb(name, shape, dt=F32):
            return ctx.enter_context(nc.sbuf_tensor(name, shape, dt))

        def sem(name):
            return ctx.enter_context(nc.semaphore(name))

        arena = sb("arena", [P, 141 * KB])
        at = [0]

        def region(kb):
            a = arena[:, at[0] * KB:(at[0] + kb) * KB]
            at[0] += kb
            return a

        X, RA, RB, RC, RD, KN = (region(20) for _ in range(6))
        WR, RH = region(16), region(5)

        def tok(r):
            return r.rearrange("p (t n) -> p t n", t=TT)

        def feat(r):
            return r.rearrange("p (k n) -> p k n", k=KT)

        def sub(r, a, n):
            return r[:, int(a * KB):int(a * KB) + n]

        def cut(r, a, /, **dims):
            names = " ".join(dims)
            return sub(r, a, math.prod(dims.values())).rearrange(f"p ({names}) -> p {names}", **dims)

        hhl = sb("h_parts", [P, 2, KT, TOK], F32R)
        whl = sb("w_parts", [P, 2, 2, 2 * NC], F32R)
        hhi, hlo = hhl[:, 0], hhl[:, 1]

        x = tok(X)
        wraw = [sub(WR, 4 * b, 2 * NC) for b in range(2)]
        mraw = [cut(WR, 8 + 4 * b, k=2, n=NC) for b in range(2)]
        G = [sb(f"gate_{l}", [P, 2, D]) for l in "ab"]
        modT = sb("modT", [P, 6, KT, ROWS])
        const = sb("const", [P, C_N])
        ident = const[:, C_ID:C_ID + P]
        maskf = cut(WR, 12, n=3 * P + NEW)
        maskb = sb("maskb", [P, 2 * P + NEW + P], BF16)
        mask_sb, mask_da = maskb[:, 0:P], maskb[:, P:2 * P]
        mask_new, identb = maskb[:, 2 * P:2 * P + NEW], maskb[:, 2 * P + NEW:]
        lnT = sb("lnT", [P, 3, KT])
        biasT = sb("biasT", [P, 6, KT])
        ss = sb("ss", [P, 2 * TT])
        rstd = sb("rstd", [P, 2 * TT])
        small = sb("small", [P, 64])
        ysq = sb("ysq", [P, 2, TT])
        yvar = sb("yvar", [P, 3, TT])
        neglam = sb("neglam", [P, 1])
        sgn = sb("sgn", [P, 1])
        osum = sb("osum", [P, TT * PAIRS])
        subs = sb("subs", [P, 1])
        first = [cut(r, 0, k=KT, n=NC) for r in (RA, RB, RC, RD)]
        cT, cin = cut(RH, 0, k=KT, r=32), cut(RH, 1, k=KT, r=ROWS)
        lamv = cut(RH, 1.5, a=4, d=HD)
        gvec = [[sub(X, 8 * l + 4 * b, D) for b in range(2)] for l in range(2)]

        def msum(m):
            return sub(RH, 3, NC) if m % 2 == 0 else sub(RC, 16, NC) if m < 4 else sub(X, 16, NC)

        xh, h32a = tok(KN), feat(RB)
        kT, qT, gT, v, knat, qnat = feat(RA), feat(RB), feat(RC), tok(RD), tok(KN), tok(RC)
        xh2, hkv32, hb32 = tok(RC), feat(RD), feat(RB)
        kbT, qbT, vb, kbn, qbn, obuf = feat(RA), feat(RB), tok(RD), tok(KN), tok(X), tok(X)
        ysb = tok(KN)
        junk = [sub(RH, 2 * b, NC) for b in range(2)]
        qz = cut(WR, 8, b=2, h=2, n=NC)
        AT = cut(KN, 0, h=2, j=NT, q=NC)
        vst = cut(KN, 16, b=2, j=NT, n=P)
        beta, stay, ex = cut(X, 0, b=4, n=NC), cut(X, 8, b=4, n=NC), cut(X, 16, b=2, n=NC)
        pr, wT = cut(KN, 0, b=2, c=2, n=NC), cut(KN, 8, b=2, n=NC)
        kc = [cut(RD, 8 * b, k=PK, n=D) for b in range(2)]
        vc = [cut(KN, 8 * b, k=PK, n=D) for b in range(2)]
        vnew = [sub(KN, 16, D), sub(RD, 16, D)]
        ktc = [cut(X, 8.5 * b, k=PAIRS, n=KEYS) for b in range(2)]
        qb = cut(X, 17, k=PAIRS, n=32)
        so = cut(RH, 3, b=2, n=2 * P)
        sbeta, sstay, sex = (cut(WR, 8 + 2.25 * b, g=2, n=KEYS) for b in range(3))
        sAT = cut(RH, 0, g=2, k=3, n=P)
        kcb = [cut(WR, 0, k=PK, n=D), cut(RD, 0, k=PK, n=D)]
        vcb = [kbT[:, 4 * b:4 * b + 4, 0:SEQ].rearrange("p (k c) n -> p k c n", c=2) for b in range(2)]
        vnewb = [qbT[:, 2 * b:2 * b + 2, 0:SEQ] for b in range(2)]
        ktcb = [cut(KN, 8.5 * b, k=PAIRS, n=KEYS) for b in range(2)]
        qbb = cut(KN, 17, k=PAIRS, n=32)
        WTW = P + NEW
        swT = cut(KN, 18, k=3, n=WTW)
        gate0 = G[0][:, :, :].rearrange("p a n -> p (a n)")
        spr, cmat, osb = cut(gate0, 0, g=2, n=KEYS), cut(gate0, 3, g=2, n=P), cut(gate0, 4, b=2, n=2 * P)
        osq = qbT[:, 4:6, 0:SEQ]
        ps = [ctx.enter_context(nc.psum_tensor(f"bank{b}", [P, NC], F32)) for b in range(8)]

        caches = {
            "ak": i["cache_a_k"].rearrange("a s (k p) h d -> (a s) p k (h d)", p=P),
            "av": i["cache_a_v"].rearrange("a s (k p) h d -> (a s) p k (h d)", p=P),
            "bk": i["cache_b_k"].rearrange("s (k p) h c d -> s p k (h c d)", p=P),
            "bv": i["cache_b_v"].rearrange("s (k p) h d -> s p k (h d)", p=P),
        }
        out_p = {
            "y": o["y_p"].rearrange("b (t p) n -> p (b t) n", p=P),
            "ak": o["ak_p"].rearrange("a b (t p) h d -> p (a b t) (h d)", p=P),
            "av": o["av_p"].rearrange("a b (t p) h d -> p (a b t) (h d)", p=P),
            "bk": o["bk_p"].rearrange("b (t p) h c d -> p (b t) (h c d)", p=P),
            "bv": o["bv_p"].rearrange("b (t p) h d -> p (b t) (h d)", p=P),
        }
        out_s = {
            "y": o["y_s"].rearrange("s q n -> (s q) n"),
            "ak": o["ak_s"].rearrange("a s q h d -> (a s q) (h d)"),
            "av": o["av_s"].rearrange("a s q h d -> (a s q) (h d)"),
            "bk": o["bk_s"].rearrange("s q h c d -> (s q) (h c d)"),
            "bv": o["bv_s"].rearrange("s q h d -> (s q) (h d)"),
        }
        av_rows = o["av_s"].rearrange("a s q h d -> (a s) q (h d)")
        bv_rows = o["bv_s"].rearrange("s q h d -> s q (h d)")
        o_scratch, x_scratch = i["o_scratch"], i["x_scratch"]

        def piece(w, c, s):
            return w.rearrange("(k p) n -> p k n", p=P)[:, 2 * s:2 * s + 2, NC * c:NC * (c + 1)]

        wa, woa, wkv, wb, wob = (i["w_in_a"][0], i["w_out_a"][0], i["w_kv_b"], i["w_in_b"][0], i["w_out_b"][0])
        gcols = [w.rearrange("(k p) n -> p k n", p=P)[:, :, c0:c0 + D] for w, c0 in ((wa, 3 * D), (wb, D))]

        chunks = [("ak", wa, 2), ("ak", wa, 3), ("av", wa, 4), ("av", wa, 5), ("aq", wa, 0), ("aq", wa, 1),
                  ("ya", woa, 0), ("ya", woa, 1),
                  ("bk", wkv, 0), ("bk", wkv, 1), ("bv", wkv, 2), ("bv", wkv, 3), ("bq", wb, 0), ("bq", wb, 1),
                  ("yb", wob, 0), ("yb", wob, 1)]
        SL = 4
        A0, YA, B0, YB = 0, 6, 8, 14
        dst_of = {"ak": knat, "av": v, "aq": qnat, "bk": kbn, "bv": vb, "bq": qbn}
        freed, count = {}, {"act": 0, "dve": 0}
        for ci, (kind, _, _) in enumerate(chunks):
            for t in range(TT):
                engines = ("act", "dve") if kind[0] == "y" else (("act", "dve")[t % 2],)
                freed[ci, t] = []
                for e in engines:
                    count[e] += 1
                    freed[ci, t].append((e, count[e]))
        mods = [("a", i["mod_w_a"][0], c) for c in range(6)] + [("kv", i["mod_w_kv"], c) for c in range(4)] \
            + [("b", i["mod_w_b"][0], c) for c in range(6)]
        order = [0, 2, 1, 3, 4, 5, 14, 15, 6, 7, 8, 9, 10, 11, 12, 13]
        tasks, task_end = [], []
        for pos, m in enumerate(order):
            tasks += [(pos, r) for r in range(1 if mods[m][2] < 4 else 2)]
            task_end.append(len(tasks))

        def sum_of(pos):
            return pos if pos < 4 else 4 + (pos - 4) // 2

        def mod_bank(n):
            return ps[7] if n >= 2 else ps[2 + n]

        def sum_bank(m):
            return ps[m] if m < 2 else ps[7] if m < 4 else ps[5]

        def tasks_of(ci):
            return [n for n, (pos, _) in enumerate(tasks) if 0 <= ci < 6 and pos in (4 + 2 * ci, 5 + 2 * ci)]

        s_const, s_mask, s_x, s_c, s_vec = sem("const_in"), sem("mask_in"), sem("x_in"), sem("c_in"), sem("vectors_in")
        s_maskb, s_silu_c, s_cz, s_lam, s_lamx = (sem(n) for n in (
            "masks_cast", "silu_c", "c_zeroed", "lambda_dots", "lambda_exp"))
        s_gb, s_first = sem("gate_vectors_in"), [sem(f"first_in{n}") for n in range(4)]
        s_w, s_mw = [sem(f"weights_in{b}") for b in range(2)], [sem(f"mod_weights_in{b}") for b in range(2)]
        s_whi, s_wlo, s_wu = sem("w_high"), sem("w_low"), sem("w_slot_used")
        s_mu, s_macc, s_msum, s_mout, s_mdone = (sem(n) for n in (
            "mod_slot_used", "mod_first_summed", "mod_partial_read", "mod_out", "mod_read"))
        s_dve = sem("dve_chain")
        s_ss, s_var, s_sqrt, s_rstd, s_xh, s_xhA = (sem(n) for n in (
            "squares_summed", "variance", "sqrt_done", "rstd_ready", "normed_dve", "normed_act"))
        NORM_DVE, NORM_ACT = (4, 0, 2), (1, 3)
        s_tr, s_trA, s_trV = sem("transposed"), sem("transposed_read_act"), sem("transposed_read_dve")
        s_pj, s_pjA, s_pjV = sem("projected"), sem("projected_read_act"), sem("projected_read_dve")
        s_hhi, s_hlo, s_hhs, s_hls = sem("h_high"), sem("h_low"), sem("h_high_samples"), sem("h_low_samples")
        s_stored = {n: sem("stored_" + n) for n in ("ak", "av", "bk", "bv")}
        s_rot = sem("rotated")
        s_yv, s_ysr, s_yr, s_ys, s_x2, s_x2p, s_xr, s_xs = (sem(n) for n in (
            "y_variance", "y_sqrt", "y_rstd", "y_scaled", "x_updated_dve", "x_updated_pool", "x_back", "x_spilled"))
        s_gact, s_gate = sem("gate_silu"), sem("gated")
        s_zero = sem("zeroed")
        s_gw = [[sem(f"g_weights_in{l}{b}") for b in range(2)] for l in "ab"]
        s_ghi, s_glo, s_g, s_gr = ([sem(f"g_{n}_{l}") for l in "ab"] for n in ("w_high", "w_low", "projected", "read"))
        a_qz, a_vst, a_z, a_sig, a_ex, a_mul, a_t, a_at, a_av, a_or = (sem("a_" + n) for n in (
            "q_staged", "v_staged", "z_ready", "sigmoids", "scanned", "a_ready", "t_ready", "at_ready", "o_ready", "o_read"))
        c_kt, c_krA, c_krV, c_q, c_z, c_sig, c_ex, c_mul, c_t, c_at, c_av, c_or, c_ot, c_od = (sem("c_" + n) for n in (
            "k_transposed", "k_read_act", "k_read_dve", "q_staged", "z_ready", "sigmoids", "scanned",
            "a_ready", "t_ready", "at_ready", "o_ready", "o_read", "o_transposed", "o_done"))
        c_k, c_v, c_vn = ([sem(f"c_{n}_in{b}") for b in range(2)] for n in ("k", "v", "vnew"))
        b_qz, b_s, b_mx, b_nb, b_p, b_rc, b_c1, b_w, b_t, b_wt, b_o, b_or = (sem("b_" + n) for n in (
            "q_staged", "s_ready", "max", "neg_max", "p_ready", "reciprocal", "coefficient", "w_ready", "t_ready",
            "wt_ready", "o_ready", "o_read"))
        (d_kt, d_krA, d_krV, d_q, d_s, d_mx, d_nb, d_p, d_rc, d_rs, d_cm, d_wt, d_wtr, d_o, d_or) = (
            sem("d_" + n) for n in ("k_transposed", "k_read_act", "k_read_dve", "q_staged", "s_ready",
                                    "max", "neg_max", "p_ready", "reciprocal", "row_scale", "combiner", "wt_ready",
                                    "wt_read", "o_ready", "o_read"))
        d_k, d_v, d_vn, d_out = ([sem(f"d_{n}{b}") for b in range(2)] for n in ("k_in", "v_in", "vnew_in", "o_out"))
        s_osq, s_oss, s_ov, s_osr, s_og, s_oin, s_out = (sem(n) for n in (
            "o_squares", "o_sums", "o_var", "o_sqrt", "o_scaled", "o_sample_in", "y_stored"))

        def wait_slot_used(eng, n):
            ci, s = divmod(n, SL)
            if s == SL - 1:
                eng.wait_ge(s_pj, TT * (ci + 1))
            else:
                eng.wait_ge(s_wu, (SL - 1) * ci + s + 1)

        def wait_read(eng, ci, t):
            for e, v_ in freed[ci, t]:
                eng.wait_ge({"act": s_pjA, "dve": s_pjV}[e], v_)

        def wait_chunk_read(eng, ci):
            for t in (TT - 2, TT - 1):
                wait_read(eng, ci, t)

        ALL = [("s", 0), ("s", 1)] + [("p", k) for k in range(KT)]
        MIXED = [("s", 0)] + [("p", k) for k in range(4)] + [("s", 1)] + [("p", k) for k in range(4, KT)]
        HALVES = [[("s", j)] + [("p", 4 * j + k) for k in range(4)] for j in range(2)]
        STAGES = [("xa", MIXED, (6, 7, 6, 7, 6, 6, 7, 6, 7, 6)), ("ka", ALL, (6,)),
                  ("q1a", HALVES[0], (6,)), ("q2a", HALVES[1], (4, 5, 6)),
                  ("xb", MIXED, (5, 6, 7)), ("kb", ALL, (5, 6, 7)),
                  ("q1b", HALVES[0], (5, 6, 7)), ("q2b", HALVES[1], (4, 5, 6, 7)),
                  ("og", ALL[2:] + ALL[:2], (5, 6, 7))]
        tr_of, uses = {}, []
        for st, groups, banks in STAGES:
            tr_of[st] = []
            for g, grp in enumerate(groups):
                affine = st in ("xa", "xb")
                engines = ["dve"] if (affine and grp[0] == "s") or st == "og" else ["act", "dve"] if st == "xb" \
                    else [("act", "dve")[g % 2]]
                tr_of[st].append((len(uses), grp))
                uses.append((engines, banks[g % len(banks)]))

        def tr_done(n, e):
            return sum(e in u for u, _ in uses[:n + 1])

        def wait_tr_read(eng, n):
            for e in uses[n][0]:
                eng.wait_ge({"act": s_trA, "dve": s_trV}[e], tr_done(n, e))

        def wait_group_read(eng, st, grp):
            wait_tr_read(eng, next(n for n, g in tr_of[st] if g == grp))

        def wait_stage_read(eng, st):
            n = tr_of[st][-1][0]
            for e, s_ in (("act", s_trA), ("dve", s_trV)):
                if tr_done(n, e):
                    eng.wait_ge(s_, tr_done(n, e))

        def tr_dst(dst, grp):
            kind, k = grp
            return dst[:, k, 0:SEQ] if kind == "p" else dst[:, 4 * k:4 * k + 4, SEQ:TOK]

        def tr_bank(n, grp):
            b = ps[uses[n][1]]
            return b[:, :] if grp[0] == "p" else b[:, :].rearrange("p (a n) -> p a n", a=4)

        beside = {}
        for k, idx in ((0, 4), (1, 5), (4, 7), (4, 8), (5, 9)):
            beside.setdefault((A0, k), []).append(("xa", idx))
        for k, idx in ((0, 5), (0, 6), (1, 7), (2, 8), (2, 9)):
            beside.setdefault((B0, k), []).append(("xb", idx))
        for k, idx in ((0, 4), (0, 5), (1, 6), (1, 7), (3, 8), (3, 9)):
            beside.setdefault((YB, k), []).append(("og", idx))
        for idx in range(len(ALL)):
            beside.setdefault((A0 + 2, idx + 1) if idx < 7 else (A0 + 3, idx - 6), []).append(("ka", idx))
            beside.setdefault((YB - 2, idx // 2), []).append(("kb", idx))
        for idx in range(len(HALVES[0])):
            beside.setdefault((YA - 1, idx + 1), []).append(("q1a", idx))
            beside.setdefault((YB - 1, idx + 3), []).append(("q1b", idx))

        H_BASE = {"xa": 0, "ya": KT, "kv": 2 * KT, "b": 3 * KT, "yb": 4 * KT}
        h_src = {"xa": h32a, "ya": feat(RB), "kv": hkv32, "b": hb32, "yb": gT}

        def split_ready(eng, name, k):
            if name in ("xa", "kv"):
                st = "xa" if name == "xa" else "xb"
                wait_group_read(eng, st, ("p", k))
                wait_group_read(eng, st, ("s", k // 4))
            elif name == "ya":
                eng.wait_ge(s_gate, k + 1)
            elif name == "b":
                wait_slot_used(eng, SL * 11 + k // 2)
            else:
                wait_group_read(eng, "og", ("p", k))

        def h_columns(name):
            return slice(0, SEQ if name == "yb" else TOK)

        def split_behind(stage, idx):
            if stage == "xa":
                return {2: (0,), 3: (1,), 4: (2, 3), 6: (4,), 7: (5,), 8: (6,), 9: (7,)}.get(idx, ())
            return {2: (0,), 3: (1,), 4: (2,), 5: (3,), 7: (4,), 8: (5,), 9: (6, 7)}.get(idx, ())

        tr_out = {"ka": kT, "q1a": qT, "kb": kbT, "q1b": qbT}

        def beside_slot(n):
            return [g for k in (2 * (n % SL), 2 * (n % SL) + 1) for g in beside.get((n // SL, k), []) if g[0] in tr_out]

        block = ctx.enter_context(nc.Block())

        @block.sync
        def _(sp):
            sp.dma_start(cin, i["cT"]).then_inc(s_c, 16)
            sp.dma_start(const[:, :], i["consts"]).then_inc(s_const, 16)
            sp.dma_start(first[0], i["mod_w_a"][0].rearrange("(k p) n -> p k n", p=P)[:, :, 0:NC]).then_inc(s_first[0], 16)
            sp.dma_start(x[:, 0:NT, :], i["x_prompt"].rearrange("b (t p) n -> p (b t) n", p=P)).then_inc(s_x, 16)
            sp.dma_start(x[:, NT, :], i["x_sample"].rearrange("s q n -> (s q) n")).then_inc(s_x, 16)
            sp.dma_start(maskf, i["masks"]).then_inc(s_mask, 16)
            sp.dma_start(lnT[:, :, :], i["lnT"]).then_inc(s_vec, 16)
            sp.dma_start(biasT[:, :, :], i["biasT"]).then_inc(s_vec, 16)
            sp.dma_start(lamv, i["lam"].partition_broadcast(P)).then_inc(s_vec, 16)
            sp.dma_start(subs[:, :], i["subln_b"].rearrange("a (n b) -> (a n) b", b=1)).then_inc(s_vec, 16)

            def load_first(n):
                cols = slice(NC * order[n], NC * (order[n] + 1))
                sp.dma_start(first[n], i["mod_w_a"][0].rearrange("(k p) n -> p k n", p=P)[:, :, cols]).then_inc(s_first[n], 16)

            def load(n):
                ci, s = divmod(n, SL)
                if n >= 2:
                    sp.wait_ge(s_wlo, n - 1)
                sp.dma_start(wraw[n % 2].rearrange("p (k n) -> p k n", k=2), piece(chunks[ci][1], chunks[ci][2], s))\
                    .then_inc(s_w[n % 2], 16)

            load_first(1)
            load(0)
            load(1)
            load_first(2)
            load_first(3)
            sp.wait_ge(s_xhA, len(NORM_ACT))
            sp.wait_ge(s_xh, len(NORM_DVE))
            for l, (bias, ln) in enumerate(((i["mod_b_a"], i["ln_post_a"]), (i["mod_b_b"], i["ln_post_b"]))):
                sp.dma_start(gvec[l][0], bias[0, 2 * D:3 * D].partition_broadcast(P)).then_inc(s_gb, 16)
                sp.dma_start(gvec[l][1], ln[0].partition_broadcast(P)).then_inc(s_gb, 16)
            sp.wait_ge(s_maskb, 1)
            for n in range(SL * YA):
                ci, s = divmod(n, SL)
                if n >= 1:
                    sp.wait_ge(s_mu, n)
                for b in range(2):
                    m = order[4 + 2 * ci + b]
                    sp.dma_start(mraw[b], piece(mods[m][1], mods[m][2], s)).then_inc(s_mw[b], 16)
                if 2 <= n + 2 < SL * YA:
                    load(n + 2)

            def gates(l, slots):
                def one(p, b):
                    sp.dma_start(wraw[b].rearrange("p (k n) -> p k n", k=KT), gcols[l][:, :, bass.ts(p, P)])\
                        .then_inc(s_gw[l][b], 16)
                sp.wait_ge(s_wlo, slots)
                one(0, 0)
                one(1, 1)
                with sp.Fori(0, PAIRS // 2 - 1) as it:
                    for b in range(2):
                        sp.wait_ge(s_glo[l], it * 2 + (HEAD + b + 1))
                        one(it * 2 + (b + 2), b)

            gates(0, SL * YA)
            def load_k(s, b):
                sp.dma_start(kc[b], caches["ak"][s]).then_inc(c_k[b], 16)

            def next_k(s, b):
                sp.wait_ge(c_kt, s * 4 + (HEAD - 4))
                load_k(s, b)

            def load_v(s, b):
                sp.wait_ge(c_av, s + (HEAD - 1))
                sp.dma_start(vc[b], caches["av"][s]).then_inc(c_v[b], 16)
                sp.dma_start(vnew[b][0:NEW, :], av_rows[s]).then_inc(c_vn[b], 16)

            sp.wait_ge(s_stored["av"], 32)
            sp.wait_ge(a_vst, HEAD + PAIRS)
            load_k(0, 0)
            load_k(1, 1)
            sp.wait_ge(s_glo[0], HEAD + PAIRS)
            load(SL * YA)
            load(SL * YA + 1)
            sp.wait_ge(a_or, HEAD + PAIRS)
            sp.wait_ge(s_stored["ak"], 32)
            load_v(0, 0)
            load_v(1, 1)
            next_k(2, 0)
            with sp.Fori(1, NSEQ // 2 - 1) as it:
                for b in range(2):
                    next_k(it * 2 + (b + 1), 1 - b)
                    load_v(it * 2 + b, b)
            next_k(NSEQ - 1, 1)
            load_v(NSEQ - 2, 0)
            load_v(NSEQ - 1, 1)
            sp.wait_ge(c_z, HEAD + 2 * NSEQ)
            sp.dma_start(x[:, 0:NT, :], i["x_prompt"].rearrange("b (t p) n -> p (b t) n", p=P)).then_inc(s_xr, 16)
            sp.dma_start(x[:, NT, :], i["x_sample"].rearrange("s q n -> (s q) n")).then_inc(s_xr, 16)
            for n in range(SL * YA + 2, SL * B0 + 2):
                load(n)
            for t in range(TT):
                sp.wait_ge(s_x2, t + 1)
                sp.wait_ge(s_x2p, t + 1)
                sp.dma_start(x_scratch[:, t, :], x[:, t, :]).then_inc(s_xs, 16)
            for n in range(SL * B0 + 2, SL * YB):
                load(n)
            gates(1, SL * YB)
            sp.wait_ge(s_glo[1], HEAD + PAIRS)
            sp.dma_start(kcb[0], caches["bk"][0]).then_inc(d_k[0], 16)

            sp.wait_ge(b_or, HEAD + NT * PAIRS)
            sp.wait_ge(s_stored["bv"], 32)

            def rows_out(s, b):
                sp.wait_ge(d_or, s + (HEAD + 1))
                for j in range(4):
                    sp.dma_start(o_scratch[s][:, :, j, :],
                                 osb[32 * j:32 * j + NEW, b].rearrange("p (g n) -> p g n", g=2)).then_inc(d_out[b], 16)

            def load_kb(s, b):
                sp.wait_ge(d_kt, s * 4 + (HEAD - 4))
                sp.dma_start(kcb[b], caches["bk"][s]).then_inc(d_k[b], 16)

            def load_vb(s, b):
                sp.wait_ge(d_o, s + (HEAD - 1))
                for k in range(PK):
                    sp.dma_start(vcb[b][:, k], caches["bv"][s, :, k].rearrange("p (c n) -> p c n", c=2)).then_inc(d_v[b], 16)
                sp.dma_start(vnewb[b][0:NEW], bv_rows[s].rearrange("q (c n) -> q c n", c=2)).then_inc(d_vn[b], 16)

            load_kb(1, 1)
            load_vb(0, 0)
            load_vb(1, 1)
            load_kb(2, 0)
            with sp.Fori(1, NSEQ // 2 - 1) as it:
                for b in range(2):
                    load_kb(it * 2 + (b + 1), 1 - b)
                    load_vb(it * 2 + b, b)
                    rows_out(it * 2 + (b - 2), b)
            load_kb(NSEQ - 1, 1)
            for b in range(2):
                load_vb(NSEQ - 2 + b, b)
                rows_out(NSEQ - 4 + b, b)
            sp.wait_ge(d_kt, HEAD + 4 * (NSEQ - 1))
            load(SL * YB)
            load(SL * YB + 1)
            rows_out(NSEQ - 2, 0)
            rows_out(NSEQ - 1, 1)
            for b in range(2):
                sp.wait_ge(d_out[b], HEAD + 16 * 4 * NSEQ // 2)
            sp.dma_start(obuf[:, NT, :].rearrange("p (g j n) -> p g j n", g=2, j=4),
                         o_scratch.rearrange("s q g j n -> (s q) g j n")).then_inc(s_oin, 16)
            load(SL * YB + 2)
            load(SL * YB + 3)
            sp.wait_ge(s_tr, tr_of["og"][-1][0] + 1)
            sp.dma_start(x[:, :, :], x_scratch).then_inc(s_xr, 16)
            for n in range(SL * YB + 4, SL * len(chunks)):
                load(n)
            for t in range(TT):
                sp.wait_ge(s_x2, TT + t + 1)
                sp.wait_ge(s_x2p, TT + t + 1)
                sp.dma_start(out_p["y"][:, t, :] if t < NT else out_s["y"], x[:, t, :]).then_inc(s_out, 16)
            sp.wait_ge(s_out, 16 * TT)
            sp.wait_ge(s_stored["bk"], 32)

        @block.gpsimd
        def _(pool):
            for s in (a_qz, a_vst, c_q, b_qz, d_q):
                pool.sem_inc(s, HEAD)
            zeros = [0]

            def zero(a):
                zeros[0] += 1
                nc.gpsimd.memset(a, 0.0).then_inc(s_zero, 1)
                pool.wait_ge(s_zero, zeros[0])

            def store(name, src, ci):
                wait_chunk_read(pool, ci)
                pool.dma_start(out_p[name], src[:, 0:NT, :]).then_inc(s_stored[name], 16)
                pool.dma_start(out_s[name], src[:, NT, :]).then_inc(s_stored[name], 16)

            def stage_q(p, b, src, done, scores, per):
                pool.wait_ge(scores, p * per + (HEAD - per))
                for h in range(2):
                    rows = slice(HD * h, HD * (h + 1))
                    nc.gpsimd.tensor_copy(qz[rows, b, h, :], src[rows, p, 0:SEQ]).then_inc(done, 1)
                    pool.wait_ge(done, p * 2 + (HEAD + h + 1))

            def stage_new(s, b, kt_src, q_src, kt_dst, q_dst, done, z_done):
                pool.wait_ge(z_done, s * 2 + HEAD)
                new = bass.ds(s * NEW + SEQ, NEW)
                copies = [(kt_dst[b][:, :, PAST:KEYS], kt_src[:, :, new]), (q_dst[0:HD, :, 0:NEW], q_src[0:HD, :, new]),
                          (q_dst[HD:P, :, NEW:32], q_src[HD:P, :, new])]
                for n, (dst, src) in enumerate(copies):
                    nc.gpsimd.tensor_copy(dst, src).then_inc(done, 1)
                    pool.wait_ge(done, s * 3 + (HEAD + n + 1))

            store("ak", knat, 1)
            store("av", v, 3)
            pool.wait_ge(s_mu, SL * YA)
            for b in range(2):
                zero(qz[HD:P, b, 0, :])
                zero(qz[0:HD, b, 1, :])
            wait_stage_read(pool, "q1a")
            pool.wait_ge(s_stored["ak"], 32)
            with pool.Fori(0, PAIRS // 2) as it:
                for b in range(2):
                    p = it * 2 + b
                    stage_q(p, b, qT, a_qz, a_z, 8)
                    pool.wait_ge(a_av, p + (HEAD - 1))
                    nc.gpsimd.tensor_copy(vst[:, b], v[:, 0:NT, bass.ts(p, P)]).then_inc(a_vst, 1)
                    pool.wait_ge(a_vst, p + (HEAD + 1))
            pool.wait_ge(a_or, HEAD + PAIRS)
            zero(qb)
            with pool.Fori(0, NSEQ // 2) as it:
                for b in range(2):
                    stage_new(it * 2 + b, b, kT, qT, ktc, qb, c_q, c_z)
            def residual(layer):
                pool.wait_ge(s_xr, 32 + 16 * layer)
                for t in range(TT):
                    pool.wait_ge(s_ys, layer * TT + t + 1)
                    nc.gpsimd.tensor_tensor(x[:, t, 0:NC], x[:, t, 0:NC], ysb[:, t, 0:NC], ALU.add).then_inc(s_x2p, 1)
                pool.wait_ge(s_x2p, (layer + 1) * TT)

            residual(0)
            pool.wait_ge(c_t, HEAD + 2 * NSEQ)
            for b in range(2):
                zero(qz[HD:P, b, 0, :])
                zero(qz[0:HD, b, 1, :])
            pool.wait_ge(s_rot, 1)
            store("bk", kbn, 9)
            store("bv", vb, 11)
            wait_stage_read(pool, "q1b")
            pool.wait_ge(s_stored["bk"], 32)
            with pool.Fori(0, PAIRS // 2) as it:
                for b in range(2):
                    stage_q(it * 2 + b, b, qbT, b_qz, b_s, NT)
            pool.wait_ge(b_or, HEAD + NT * PAIRS)
            zero(qbb)
            zero(swT[:, :, P:WTW])

            with pool.Fori(0, NSEQ // 2) as it:
                for b in range(2):
                    stage_new(it * 2 + b, b, kbT, qbT, ktcb, qbb, d_q, d_s)
            residual(1)

        @block.scalar
        def _(act):
            for s in (a_sig, a_at, c_sig, c_krA, c_at, c_or, b_p, b_wt, b_or, d_p, d_krA, d_wtr, d_or, s_osq,
                      *d_out, *s_ghi, *s_gr):
                act.sem_inc(s, HEAD)
            act.wait_ge(s_c, 16)
            act.wait_ge(s_cz, 1)
            nc.scalar.activation(cT[:, :, 0:ROWS], cin, ACT.Silu).then_inc(s_silu_c, 1)
            act.wait_ge(s_lam, 1)
            nc.scalar.activation(small[:, 2:4], small[:, 0:2], ACT.Exp).then_inc(s_lamx, 1)

            def square_sums(stage, dst, ready):
                for t in range(TT):
                    ready(t)
                    nc.scalar.activation(dst[:, t, :], x[:, t, :], ACT.Square,
                                         accum_out=ss[:, TT * stage + t:TT * stage + t + 1]).then_inc(s_ss, 1)
                act.wait_ge(s_var, stage + 1)
                nc.scalar.activation(ss[:, TT * stage:TT * (stage + 1)], ss[:, TT * stage:TT * (stage + 1)],
                                     ACT.Sqrt).then_inc(s_sqrt, 1)
                act.wait_ge(s_rstd, stage + 1)
                for t in NORM_ACT:
                    nc.scalar.activation(dst[:, t, :], x[:, t, :], ACT.Copy, scale=rstd[:, TT * stage + t:TT * stage + t + 1])\
                        .then_inc(s_xhA, 1)

            def w_high(n):
                if n >= SL * len(chunks):
                    return
                act.wait_ge(s_w[n % 2], 16 * (n // 2 + 1))
                if n >= 2:
                    wait_slot_used(act, n - 2)
                nc.scalar.activation(whl[:, n % 2, 0, :], wraw[n % 2], ACT.Copy).then_inc(s_whi, 1)

            def h_high(name, k):
                split_ready(act, name, k)
                n = h_columns(name)
                nc.scalar.activation(hhi[:, k, n], h_src[name][:, k, n], ACT.Copy).then_inc(s_hhi, 1)

            def y_root(layer, t):
                act.wait_ge(s_yv, layer * TT + t + 1)
                nc.scalar.activation(yvar[:, 2, t:t + 1], yvar[:, 1, t:t + 1], ACT.Sqrt).then_inc(s_ysr, 1)

            def y_scale(layer, t):
                act.wait_ge(s_yr, layer * TT + t + 1)
                act.wait_ge(s_pjV, freed[(YA, YB)[layer], t][1][1])
                nc.scalar.activation(ysb[:, t, 0:NC], ysb[:, t, 0:NC], ACT.Copy, scale=yvar[:, 0, t:t + 1]).then_inc(s_ys, 1)

            def read(ci):
                kind, c = chunks[ci][0], chunks[ci][2]
                for t in range(TT):
                    for e, v_ in freed[ci, t]:
                        if e != "act":
                            continue
                        act.wait_ge(s_pj, TT * ci + t + 1)
                        if kind[0] == "y":
                            act.wait_ge(s_pjA, v_ - 1)
                            nc.scalar.activation(junk[t % 2], ps[t][:, :], ACT.Square, scale=D ** -0.5,
                                                 accum_out=ysq[:, c, t:t + 1]).then_inc(s_pjA, 1)
                            if c == 1 and t:
                                y_root(int(ci >= YB), t - 1)
                                if t > 1:
                                    y_scale(int(ci >= YB), t - 2)
                        else:
                            nc.scalar.activation(dst_of[kind][:, t, NC * (c % 2):NC * (c % 2 + 1)], ps[t][:, :],
                                                 ACT.Copy).then_inc(s_pjA, 1)

            def read_group(stage, idx, dst):
                n, grp = tr_of[stage][idx]
                if "act" in uses[n][0]:
                    act.wait_ge(s_tr, n + 1)
                    nc.scalar.activation(tr_dst(dst, grp), tr_bank(n, grp), ACT.Copy).then_inc(s_trA, 1)

            def stream(c0, c1, split=1, ahead=0):
                for n in range(SL * c0, SL * c1):
                    if SL * c0 + split <= n + 1 < SL * c1 + ahead:
                        w_high(n + 1)
                    for stage, idx in beside_slot(n):
                        read_group(stage, idx, tr_out[stage])
                    if n % SL == SL - 1:
                        read(n // SL)
                    if n // SL == 11:
                        for k in range(2 * (n % SL), 2 * (n % SL) + 2):
                            h_high("b", k)

            def affine(dst, k, bank, vs):
                nc.scalar.activation(dst, bank, ACT.Identity, bias=modT[:, vs, k, 0:1], scale=modT[:, vs + 1, k, 0:1])\
                    .then_inc(s_trA, 1)

            act.wait_ge(s_x, 32)
            square_sums(0, xh, lambda t: None)
            w_high(0)
            w_high(1)

            def modulate(stage, name, dst, vs):
                for idx, (n, (kind, k)) in enumerate(tr_of[stage]):
                    if stage == "xa" and idx in (0, 5):
                        act.wait_ge(s_mdone, 2 if idx == 0 else 4)
                    if "act" in uses[n][0]:
                        act.wait_ge(s_tr, n + 1)
                        affine(dst[:, k, 0:SEQ], k, tr_bank(n, (kind, k)), vs)
                    for k_ in split_behind(stage, idx):
                        h_high(name, k_)
                    if stage == "xa" and idx == 4:
                        w_high(2)

            modulate("xa", "xa", h32a, 0)
            stream(A0, YA, 3)
            act.wait_ge(s_stored["ak"], 32)

            def g_high(l, p, b):
                act.wait_ge(s_gw[l][b], (p - b) * 8 + 16)
                act.wait_ge(s_g[l], p * 2 + (HEAD - 2))
                nc.scalar.activation(whl[:, b, 0, :], wraw[b], ACT.Copy).then_inc(s_ghi[l], 1)

            def read_g(l, p, half):
                act.wait_ge(s_g[l], p * 2 + (HEAD + half + 1))
                nc.scalar.activation(gT[:, p, 320 * half:320 * (half + 1)], ps[7][:, 0:320], ACT.Copy).then_inc(s_gr[l], 1)

            wait_chunk_read(act, 5)
            act.wait_ge(s_mdone, len(tasks))

            def sig(p, u):
                w = P * (UNITS[u][1] + 1)
                act.wait_ge(a_z, p * 8 + (HEAD + u + 1))
                act.wait_ge(a_t, p * 8 + (HEAD + u + 1 - 4))
                nc.scalar.activation(beta[:, u % 4, 0:w], ps[u % 4][:, 0:w], ACT.Sigmoid, scale=SCALE)
                nc.scalar.activation(stay[:, u % 4, 0:w], ps[u % 4][:, 0:w], ACT.Sigmoid, scale=-SCALE).then_inc(a_sig, 1)

            def read_at(p, u):
                h, q = UNITS[u]
                act.wait_ge(a_t, p * 8 + (HEAD + u + 1))
                if u == 0:
                    act.wait_ge(a_av, p + HEAD)
                nc.scalar.activation(AT[:, h, 0:q + 1, P * q:P * (q + 1)],
                                     ps[4 + u % 2][:, 0:P * (q + 1)].rearrange("p (j n) -> p j n", j=q + 1),
                                     ACT.Copy).then_inc(a_at, 1)

            def pair_a(p, b, more):
                for u in range(4):
                    sig(p, u + 4)
                    read_at(p, u)
                    if u == 0 and more:
                        g_high(0, p + 1, 1 - b)
                read_g(0, p, 0)
                for u in range(4):
                    if more:
                        sig(p + 1, u)
                    read_at(p, u + 4)
                read_g(0, p, 1)

            g_high(0, 0, 0)
            for u in range(4):
                sig(0, u)
            for idx in range(len(HALVES[1])):
                read_group("q2a", idx, qT)
            with act.Fori(0, PAIRS // 2 - 1) as it:
                for b in range(2):
                    pair_a(it * 2 + b, b, True)
            pair_a(PAIRS - 2, 0, True)
            pair_a(PAIRS - 1, 1, False)

            def read_k(ktcs, ready, done, s, b):
                for c in (0, 2):
                    act.wait_ge(ready, s * 4 + (HEAD + c + 1))
                    nc.scalar.activation(ktcs[b][:, 2 * c:2 * c + 2, 0:PAST],
                                         ps[0][:, :].rearrange("p (a n) -> p a n", a=2), ACT.Copy).then_inc(done, 1)

            def sig_s(s):
                for g in range(2):
                    act.wait_ge(c_z, s * 2 + (HEAD + g + 1))
                    act.wait_ge(c_t, s * 2 + (HEAD + g - 1))
                    nc.scalar.activation(sbeta[:, g, :], ps[2 + g][:, 0:KEYS], ACT.Sigmoid, scale=SCALE)
                    nc.scalar.activation(sstay[:, g, :], ps[2 + g][:, 0:KEYS], ACT.Sigmoid, scale=-SCALE).then_inc(c_sig, 1)

            def silu(k):
                nc.scalar.activation(gT[:, k, :], gT[:, k, :], ACT.Silu).then_inc(s_gact, 1)

            def sample_a(s, b, more, silus=()):
                if more:
                    read_k(ktc, c_kt, c_krA, s + 1, 1 - b)
                for g in range(2):
                    act.wait_ge(c_t, s * 2 + (HEAD + g + 1))
                    act.wait_ge(c_av, s + HEAD)
                    nc.scalar.activation(sAT[:, g, 0:2, :], ps[4 + g][:, 0:2 * P].rearrange("p (k n) -> p k n", k=2), ACT.Copy)
                    nc.scalar.activation(sAT[0:NEW, g, 2, :], ps[4 + g][0:NEW, 2 * P:3 * P], ACT.Copy).then_inc(c_at, 1)
                for k in silus:
                    silu(k)
                if more:
                    sig_s(s + 1)
                act.wait_ge(c_av, s + (HEAD + 1))
                act.wait_ge(c_ot, s + (HEAD - 1))
                nc.scalar.activation(so[:, b], ps[6][:, 0:2 * P], ACT.Copy).then_inc(c_or, 1)

            act.wait_ge(a_or, HEAD + PAIRS)
            read_k(ktc, c_kt, c_krA, 0, 0)
            sig_s(0)
            with act.Fori(0, NSEQ // 2 - 1) as it:
                for b in range(2):
                    sample_a(it * 2 + b, b, True)
            sample_a(NSEQ - 2, 0, True)
            act.wait_ge(s_gr[0], HEAD + 2 * PAIRS)
            w_high(SL * YA)
            sample_a(NSEQ - 1, 1, False, silus=(0, 1))
            h_high("ya", 0)
            w_high(SL * YA + 1)
            for k in range(2, KT):
                silu(k)
                h_high("ya", k - 1)
            h_high("ya", KT - 1)
            stream(YA, B0, split=2, ahead=1)

            y_root(0, NT)
            y_scale(0, NT - 1)
            y_scale(0, NT)
            square_sums(1, xh2, lambda t: (act.wait_ge(s_x2, t + 1), act.wait_ge(s_x2p, t + 1)))
            w_high(SL * B0 + 1)
            modulate("xb", "kv", hkv32, 2)
            act.wait_ge(s_xs, 16 * TT)
            stream(B0, YB, 2)

            act.wait_ge(s_stored["bk"], 32)

            def exps(p, u):
                w = P * (NT - u)
                act.wait_ge(b_nb, p * NT + (HEAD + u + 1))
                act.wait_ge(b_t, p * NT + (HEAD + u - 1))
                for c in range(2):
                    nc.scalar.activation(pr[:, u % 2, c, 0:w], ps[2 * (u % 2) + c][:, 0:w], ACT.Exp,
                                         bias=small[:, 16 + 4 * u + c:17 + 4 * u + c], scale=SCALE,
                                         accum_out=small[:, 32 + 4 * u + c:33 + 4 * u + c]).then_inc(b_p, 1)

            def read_wt(p, u):
                w = P * (NT - u)
                act.wait_ge(b_t, p * NT + (HEAD + u + 1))
                act.wait_ge(b_o, p * NT + (HEAD + u - 1))
                nc.scalar.activation(wT[:, u % 2, 0:w], ps[4 + u % 2][:, 0:w], ACT.Copy).then_inc(b_wt, 1)

            def read_o(p, u):
                act.wait_ge(b_o, p * NT + (HEAD + u + 1))
                nc.scalar.activation(obuf[:, NT - 1 - u, bass.ts(p, P)], ps[6][:, 0:P], ACT.Copy,
                                     scale=small[:, 34 + 4 * u:35 + 4 * u]).then_inc(b_or, 1)

            def pair_b(p, b, more):
                for u in range(NT):
                    if u < NT - 1:
                        exps(p, u + 1)
                    elif more:
                        exps(p + 1, 0)
                    read_wt(p, u)
                    if u:
                        read_o(p, u - 1)
                    if u == 1:
                        read_g(1, p, 0)
                        if more:
                            g_high(1, p + 1, 1 - b)
                read_o(p, NT - 1)
                read_g(1, p, 1)

            g_high(1, 0, 0)
            exps(0, 0)
            for idx in range(len(HALVES[1])):
                read_group("q2b", idx, qbT)
            with act.Fori(0, PAIRS // 2 - 1) as it:
                for b in range(2):
                    pair_b(it * 2 + b, b, True)
            pair_b(PAIRS - 2, 0, True)
            pair_b(PAIRS - 1, 1, False)

            def exps_s(s):
                for g in range(2):
                    act.wait_ge(d_nb, s * 2 + (HEAD + g + 1))
                    act.wait_ge(d_wt, s + HEAD)
                    nc.scalar.activation(spr[:, g, :], ps[2 + g][:, 0:KEYS], ACT.Exp, bias=small[:, 18 + g:19 + g],
                                         scale=SCALE, accum_out=small[:, 20 + g:21 + g]).then_inc(d_p, 1)

            def squares(t):
                act.wait_ge(s_oss, t + HEAD)
                nc.scalar.activation(osq, obuf[:, t, :].rearrange("p (c n) -> p c n", c=2), ACT.Square).then_inc(s_osq, 1)

            def sample_b(s, b, more, tile=None, silus=()):
                if more:
                    read_k(ktcb, d_kt, d_krA, s + 1, 1 - b)
                act.wait_ge(d_wt, s + (HEAD + 1))
                act.wait_ge(d_o, s + HEAD)
                nc.scalar.activation(swT[:, 0:2, 0:P], ps[4][:, 0:2 * P].rearrange("p (k n) -> p k n", k=2), ACT.Copy)
                nc.scalar.activation(swT[0:NEW, 2, 0:P], ps[4][0:NEW, 2 * P:3 * P], ACT.Copy).then_inc(d_wtr, 1)
                for k in silus:
                    silu(k)
                if more:
                    exps_s(s + 1)
                if tile is not None:
                    squares(tile)
                act.wait_ge(d_o, s + (HEAD + 1))
                act.wait_ge(d_out[b], (s - b) * 32 + HEAD)
                nc.scalar.activation(osb[:, b], ps[5][:, 0:2 * P], ACT.Copy).then_inc(d_or, 1)

            act.wait_ge(b_or, HEAD + NT * PAIRS)
            act.wait_ge(b_w, HEAD + NT * PAIRS)
            read_k(ktcb, d_kt, d_krA, 0, 0)
            exps_s(0)
            with act.Fori(0, NSEQ // 2 - 1) as it:
                for b in range(2):
                    sample_b(it * 2 + b, b, True, it * 1 if b == 0 else None)
            sample_b(NSEQ - 2, 0, True, NT - 1)

            def head_root(columns, n):
                act.wait_ge(s_ov, n)
                nc.scalar.activation(osum[:, columns], osum[:, columns], ACT.Sqrt).then_inc(s_osr, 1)

            head_root(slice(0, NT * PAIRS), 1)
            act.wait_ge(s_gr[1], HEAD + 2 * PAIRS)
            w_high(SL * YB)
            sample_b(NSEQ - 1, 1, False, silus=(0, 1))
            silu(2)
            w_high(SL * YB + 1)
            silu(3)
            h_high("yb", 0)
            silu(4)
            h_high("yb", 1)
            for k in (5, 6, 7):
                silu(k)
            h_high("yb", 2)
            act.wait_ge(s_oin, 16)
            squares(NT)
            h_high("yb", 3)
            h_high("yb", 4)
            head_root(slice(NT * PAIRS, TT * PAIRS), 2)
            for k in (5, 6, 7):
                h_high("yb", k)
            for j in range(2):
                wait_group_read(act, "og", ("s", j))
                part = (slice(None), slice(4 * j, 4 * j + 4), slice(SEQ, TOK))
                nc.scalar.activation(hhi[part], gT[part], ACT.Copy).then_inc(s_hhs, 1)
            stream(YB, len(chunks), 2)
            y_root(1, NT)
            y_scale(1, NT - 1)
            y_scale(1, NT)

        @block.vector
        def _(dve):
            chain = [0]

            def link(ins):
                chain[0] += 1
                ins.then_inc(s_dve, 1)
                dve.wait_ge(s_dve, chain[0])

            for s in (a_ex, a_mul, a_or, c_ex, c_mul, c_od, c_krV, b_mx, b_nb, b_rc, b_c1, b_w, d_mx, d_nb, d_rc, d_rs,
                      d_cm, d_krV, s_oss, *s_glo):
                dve.sem_inc(s, HEAD)
            nc.vector.memset(cT[:, :, ROWS:32], 0.0).then_inc(s_cz, 1)

            def norm(stage, dst):
                a, b = TT * stage, TT * (stage + 1)
                dve.wait_ge(s_ss, b)
                nc.vector.tensor_scalar(ss[:, a:b], ss[:, a:b], 1.0 / D, EPS, ALU.mult, ALU.add).then_inc(s_var, 1)
                dve.wait_ge(s_sqrt, stage + 1)
                nc.vector.reciprocal(rstd[:, a:b], ss[:, a:b]).then_inc(s_rstd, 1)
                dve.wait_ge(s_rstd, stage + 1)
                for t in NORM_DVE:
                    nc.vector.tensor_scalar(dst[:, t, :], x[:, t, :], rstd[:, a + t:a + t + 1], None, ALU.mult)\
                        .then_inc(s_xh, 1)

            def read_partial(m):
                if m >= 2:
                    dve.wait_ge(s_mout, task_end[m - 2 if m < 6 else 2 * m - 7])
                if m < 4:
                    dve.wait_ge(s_macc, m + 1)
                else:
                    dve.wait_ge(s_mu, SL * (m - 3))
                nc.vector.tensor_copy(msum(m), sum_bank(m)[:, :]).then_inc(s_msum, 1)

            def finish_task(n):
                pos, r = tasks[n]
                group, _, c = mods[order[pos]]
                dve.wait_ge(s_mout, n + 1)
                if c < 4:
                    vi = {"a": 0, "kv": 2, "b": 4}[group] + c // 2
                    k = slice(4 * (c % 2), 4 * (c % 2) + 4)
                    dst = modT[:, vi, k, :]
                    bias = biasT[:, vi, k].unsqueeze(2).to_broadcast([P, 4, ROWS])
                    src = mod_bank(n)[:, 0:4 * ROWS].rearrange("p (k r) -> p k r", k=4)
                    if vi % 2 == 0:
                        nc.vector.tensor_tensor(dst, src, bias, ALU.add).then_inc(s_mdone, 1)
                    else:
                        link(nc.vector.tensor_tensor(dst, src, bias, ALU.add))
                        ln = lnT[:, vi // 2, k].unsqueeze(2).to_broadcast([P, 4, ROWS])
                        link(nc.vector.tensor_scalar(dst, dst, 1.0, None, ALU.add))
                        nc.vector.tensor_tensor(dst, dst, ln, ALU.mult).then_inc(s_mdone, 1)
                else:
                    layer = 0 if group == "a" else 1
                    half = slice(NC * (c - 4), NC * (c - 3))
                    dve.wait_ge(s_gb, 64)
                    dst = G[layer][:, r, half]
                    link(nc.vector.tensor_tensor(dst, ps[7][:, :], gvec[layer][0][:, half], ALU.add))
                    nc.vector.tensor_tensor(dst, dst, gvec[layer][1][:, half], ALU.mult).then_inc(s_mdone, 1)

            def w_low(n):
                if n >= SL * len(chunks):
                    return
                dve.wait_ge(s_whi, n + 1)
                nc.vector.tensor_tensor(whl[:, n % 2, 1, :], wraw[n % 2], whl[:, n % 2, 0, :].bitcast(F32), ALU.subtract)\
                    .then_inc(s_wlo, 1)

            def h_low(name, k):
                dve.wait_ge(s_hhi, H_BASE[name] + k + 1)
                n = h_columns(name)
                nc.vector.tensor_tensor(hlo[:, k, n], h_src[name][:, k, n], hhi[:, k, n].bitcast(F32), ALU.subtract)\
                    .then_inc(s_hlo, 1)

            def y_variance(layer, t):
                nc.vector.tensor_scalar(yvar[:, 1, t:t + 1], ysq[:, 0, t:t + 1], ysq[:, 1, t:t + 1], EPS, ALU.add, ALU.add)\
                    .then_inc(s_yv, 1)

            def residual(layer, t):
                dve.wait_ge(s_ysr, layer * TT + t + 1)
                nc.vector.reciprocal(yvar[:, 0, t:t + 1], yvar[:, 2, t:t + 1]).then_inc(s_yr, 1)
                dve.wait_ge(s_yr, layer * TT + t + 1)
                dve.wait_ge(s_xr, 32 + 16 * layer)
                dve.wait_ge(s_pjV, freed[(YA, YB)[layer] + 1, t][1][1])
                nc.vector.scalar_tensor_tensor(x[:, t, NC:D], ysb[:, t, NC:D], yvar[:, 0, t:t + 1], x[:, t, NC:D],
                                               ALU.mult, ALU.add).then_inc(s_x2, 1)

            def read(ci):
                kind, c = chunks[ci][0], chunks[ci][2]
                for t in range(TT):
                    for e, v_ in freed[ci, t]:
                        if e != "dve":
                            continue
                        dve.wait_ge(s_pj, TT * ci + t + 1)
                        if kind[0] == "y":
                            dst = ysb[:, t, NC * c:NC * (c + 1)]
                            dve.wait_ge(s_pjA, freed[ci, t][0][1])
                        else:
                            dst = dst_of[kind][:, t, NC * (c % 2):NC * (c % 2 + 1)]
                        if kind[0] == "y" and c == 1:
                            y_variance(int(ci >= YB), t)
                        if kind[0] == "y":
                            gate = G[int(ci >= YB)][:, int(t == NT), NC * c:NC * (c + 1)]
                            nc.vector.tensor_tensor(dst, ps[t][:, :], gate, ALU.mult).then_inc(s_pjV, 1)
                        else:
                            nc.vector.tensor_copy(dst, ps[t][:, :]).then_inc(s_pjV, 1)
                        if kind[0] == "y" and c == 1 and t:
                            residual(int(ci >= YB), t - 1)

            def read_group(stage, idx, dst):
                n, grp = tr_of[stage][idx]
                if "dve" in uses[n][0]:
                    dve.wait_ge(s_tr, n + 1)
                    nc.vector.tensor_copy(tr_dst(dst, grp), tr_bank(n, grp)).then_inc(s_trV, 1)

            def stream(c0, c1, split=1, ahead=0):
                for n in range(SL * c0, SL * c1):
                    ci, s = divmod(n, SL)
                    if SL * c0 + split <= n + 1 < SL * c1 + ahead:
                        w_low(n + 1)
                    if n == SL * (YB - 1):
                        wait_chunk_read(dve, YB - 2)
                        rotate(qbn, gate0, 0, PAIRS)
                    for stage, idx in beside_slot(n):
                        read_group(stage, idx, tr_out[stage])
                    todo = tasks_of(ci - 1) if ci < YA else []
                    if s < len(todo):
                        finish_task(todo[s])
                    if s == SL - 1:
                        read(ci)
                        if ci < YA:
                            read_partial(4 + ci)
                    if ci == 11:
                        h_low("b", 2 * s)
                        h_low("b", 2 * s + 1)
                    if n == SL * 10 - 1:
                        wait_chunk_read(dve, 9)
                        rotate(kbn, gate0, 0, 2 * PAIRS)

            dve.wait_ge(s_vec, 64)
            link(nc.vector.tensor_tensor(lamv[:, 0:3:2, :], lamv[:, 0:3:2, :], lamv[:, 1:4:2, :], ALU.mult))
            nc.vector.tensor_reduce(small[:, 0:2], lamv[:, 0:3:2, :], AX.X, ALU.add).then_inc(s_lam, 1)
            dve.wait_ge(s_lamx, 1)
            link(nc.vector.tensor_tensor(small[:, 10:11], small[:, 3:4], small[:, 2:3], ALU.subtract))
            link(nc.vector.tensor_scalar(neglam[:, :], small[:, 10:11], -LAMBDA_INIT, None, ALU.add))
            dve.wait_ge(s_const, 16)
            link(nc.vector.scalar_tensor_tensor(sgn[:, :], const[:, C_M1:C_M1 + 1], neglam[:, 0:1],
                                                const[:, C_M0:C_M0 + 1], ALU.mult, ALU.add))
            link(nc.vector.tensor_scalar(subs[:, :], subs[:, :], 1.0 - LAMBDA_INIT, None, ALU.mult))
            read_partial(0)
            finish_task(0)
            dve.wait_ge(s_x, 32)
            norm(0, xh)
            dve.wait_ge(s_mask, 16)
            nc.vector.tensor_copy(maskb[:, :], maskf).then_inc(s_maskb, 1)
            read_partial(1)
            finish_task(1)

            def sample_affine(dst, n, j, vs):
                k = slice(4 * j, 4 * j + 4)
                d = dst[:, k, SEQ:TOK].rearrange("p k (s q) -> p k s q", s=NSEQ)
                src = ps[uses[n][1]][:, :].rearrange("p (k s q) -> p k s q", k=4, q=NEW)
                sc, sh = (modT[:, vs + a, k, 1:ROWS].unsqueeze(3).to_broadcast([P, 4, NSEQ, NEW]) for a in (1, 0))
                link(nc.vector.tensor_tensor(d, src, sc, ALU.mult))
                return nc.vector.tensor_tensor(d, d, sh, ALU.add)

            def prompt_affine(dst, n, k, vs):
                return nc.vector.tensor_scalar(dst[:, k, 0:SEQ], ps[uses[n][1]][:, :], modT[:, vs + 1, k, 0:1],
                                               modT[:, vs, k, 0:1], ALU.mult, ALU.add)

            for idx, (n, (kind, k)) in enumerate(tr_of["xa"]):
                if idx in (0, 5):
                    dve.wait_ge(s_mdone, 2 if idx == 0 else 4)
                if "dve" in uses[n][0]:
                    dve.wait_ge(s_tr, n + 1)
                    (prompt_affine if kind == "p" else sample_affine)(h32a, n, k, 0).then_inc(s_trV, 1)
                if idx == 1:
                    w_low(0)
                for k_ in split_behind("xa", idx):
                    h_low("xa", k_)
                if idx == 3:
                    w_low(1)
                if idx == 4:
                    read_partial(2)
                    w_low(2)
                    finish_task(2)
                    read_partial(3)
                    finish_task(3)

            def rotate(a, tmp, c0, c1):
                c = c1 - c0
                h4 = a[:, :, HD * c0:HD * c1].rearrange("p t (k d) -> p t k d", d=HD)
                x1, x2 = h4[:, :, :, 0:HALF], h4[:, :, :, HALF:ROT]
                cs, sn = (const[:, c_:c_ + TT * HALF].rearrange("p (t d) -> p t d", t=TT).unsqueeze(2)
                          .to_broadcast([P, TT, c, HALF]) for c_ in (C_COS, C_SIN))
                size = TT * c * HALF
                tm = [tmp[:, size * n_:size * (n_ + 1)].rearrange("p (t k d) -> p t k d", t=TT, k=c) for n_ in range(3)]
                nc.vector.tensor_tensor(tm[0], x1, cs, ALU.mult)
                nc.vector.tensor_tensor(tm[1], x2, sn, ALU.mult)
                link(nc.vector.tensor_tensor(tm[2], x1, sn, ALU.mult))
                link(nc.vector.tensor_tensor(x1, tm[0], tm[1], ALU.subtract))
                link(nc.vector.tensor_tensor(tm[0], x2, cs, ALU.mult))
                nc.vector.tensor_tensor(x2, tm[2], tm[0], ALU.add).then_inc(s_rot, 1)

            stream(A0, YA, 3)
            for n in tasks_of(YA - 1):
                finish_task(n)
            dve.wait_ge(s_stored["ak"], 32)

            def g_low(l, p, b):
                dve.wait_ge(s_ghi[l], p + (HEAD + 1))
                nc.vector.tensor_tensor(whl[:, b, 1, :], wraw[b], whl[:, b, 0, :].bitcast(F32), ALU.subtract)\
                    .then_inc(s_glo[l], 1)

            def scan(p, u):
                w = P * (UNITS[u][1] + 1)
                dve.wait_ge(a_sig, p * 8 + (HEAD + u + 1))
                dve.wait_ge(a_mul, p * 8 + (HEAD + u - 1))
                st = stay[:, u % 4, w - 1:0:-1]
                nc.vector.tensor_tensor_scan(ex[:, u % 2, 0:w - 1][:, ::-1], st, st, 1.0, ALU.mult, ALU.bypass)\
                    .then_inc(a_ex, 1)

            def mul(p, u):
                w = P * (UNITS[u][1] + 1)
                dve.wait_ge(a_ex, p * 8 + (HEAD + u + 1))
                b = beta[:, u % 4, 0:w - 1]
                nc.vector.tensor_tensor(b, b, ex[:, u % 2, 0:w - 1], ALU.mult).then_inc(a_mul, 1)

            def pair_a(p, b, more):
                mul(p, 3)
                for u in range(4):
                    scan(p, u + 4)
                    mul(p, u + 4)
                    if u == 1 and more:
                        g_low(0, p + 1, 1 - b)
                for u in range(4):
                    if more:
                        scan(p + 1, u)
                        if u < 3:
                            mul(p + 1, u)
                dve.wait_ge(a_av, p + (HEAD + 1))
                nc.vector.tensor_copy(qT[:, p, 0:SEQ], ps[6][:, :]).then_inc(a_or, 1)

            g_low(0, 0, 0)
            for u in range(4):
                scan(0, u)
                if u < 3:
                    mul(0, u)
                if u == 1:
                    for idx in range(len(HALVES[1])):
                        read_group("q2a", idx, qT)
            with dve.Fori(0, PAIRS // 2 - 1) as it:
                for b in range(2):
                    pair_a(it * 2 + b, b, True)
            pair_a(PAIRS - 2, 0, True)
            pair_a(PAIRS - 1, 1, False)

            def read_k(ktcs, ready, done, s, b):
                for c in (1, 3):
                    dve.wait_ge(ready, s * 4 + (HEAD + c + 1))
                    nc.vector.tensor_copy(ktcs[b][:, 2 * c:2 * c + 2, 0:PAST],
                                          ps[1][:, :].rearrange("p (a n) -> p a n", a=2)).then_inc(done, 1)

            def scans_s(s):
                for g in range(2):
                    dve.wait_ge(c_sig, s * 2 + (HEAD + g + 1))
                    dve.wait_ge(c_mul, s * 2 + (HEAD + g - 1))
                    st = sstay[:, g, KEYS - 1:0:-1]
                    nc.vector.tensor_tensor_scan(sex[:, g, 0:KEYS - 1][:, ::-1], st, st, 1.0, ALU.mult, ALU.bypass)\
                        .then_inc(c_ex, 1)
                for g in range(2):
                    dve.wait_ge(c_ex, s * 2 + (HEAD + g + 1))
                    bt = sbeta[:, g, 0:KEYS - 1]
                    nc.vector.tensor_tensor(bt, bt, sex[:, g, 0:KEYS - 1], ALU.mult).then_inc(c_mul, 1)

            def take_o(s):
                dve.wait_ge(c_ot, s + (HEAD + 1))
                for h in range(2):
                    rows = slice(HD * h, HD * (h + 1))
                    own = ps[7][rows, 0:2 * P].rearrange("p (a n) -> p a n", a=PAIRS)[:, :, NEW * h:NEW * (h + 1)]
                    ins = nc.vector.tensor_copy(qT[rows, :, bass.ds(s * NEW + SEQ, NEW)], own)
                ins.then_inc(c_od, 1)

            def sample_a(s, b, first=False):
                read_k(ktc, c_kt, c_krV, s + 1, 1 - b)
                if not first:
                    take_o(s - 1)
                scans_s(s + 1)

            read_k(ktc, c_kt, c_krV, 0, 0)
            scans_s(0)
            sample_a(0, 0, True)
            sample_a(1, 1)
            with dve.Fori(1, NSEQ // 2 - 1) as it:
                for b in range(2):
                    sample_a(it * 2 + b, b)
            sample_a(NSEQ - 2, 0)
            take_o(NSEQ - 2)
            w_low(SL * YA)
            take_o(NSEQ - 1)
            dve.wait_ge(c_od, HEAD + NSEQ)
            for k in range(KT):
                dve.wait_ge(s_gact, k + 1)
                nc.vector.tensor_tensor(qT[:, k, :], qT[:, k, :], gT[:, k, :], ALU.mult).then_inc(s_gate, 1)
                if k >= 2:
                    h_low("ya", k - 1)
                if k == 0:
                    h_low("ya", 0)
                if k == 1:
                    w_low(SL * YA + 1)
            h_low("ya", KT - 1)
            stream(YA, B0, split=2, ahead=1)

            residual(0, NT)
            norm(1, xh2)
            for idx, (n, (kind, k)) in enumerate(tr_of["xb"]):
                if idx == 5:
                    w_low(SL * B0 + 1)
                dve.wait_ge(s_tr, n + 1)
                if kind == "p":
                    dve.wait_ge(s_trA, tr_done(n, "act"))
                    prompt_affine(hb32, n, k, 4).then_inc(s_trV, 1)
                else:
                    sample_affine(hkv32, n, k, 2)
                    sample_affine(hb32, n, k, 4).then_inc(s_trV, 1)
                for k_ in split_behind("xb", idx):
                    h_low("kv", k_)
            dve.wait_ge(s_xs, 16 * TT)
            stream(B0, YB, 2)
            wait_chunk_read(dve, YB - 1)
            rotate(qbn, gate0, PAIRS, 2 * PAIRS)

            dve.wait_ge(s_stored["bk"], 32)

            def maxes(p, u):
                w = P * (NT - u)
                mx, nb = small[:, 12:14], small[:, 16 + 4 * u:18 + 4 * u]
                dve.wait_ge(b_s, p * NT + (HEAD + u + 1))
                dve.wait_ge(b_nb, p * NT + (HEAD + u))
                for c in range(2):
                    ins = nc.vector.tensor_reduce(small[:, 12 + c:13 + c], ps[2 * (u % 2) + c][:, 0:w], AX.X, ALU.max)
                ins.then_inc(b_mx, 1)
                dve.wait_ge(b_mx, p * NT + (HEAD + u + 1))
                nc.vector.tensor_scalar(nb, mx, -SCALE, None, ALU.mult).then_inc(b_nb, 1)

            def combine(p, u):
                w = P * (NT - u)
                l, r, c1 = 32 + 4 * u, 34 + 4 * u, 48 + u
                dve.wait_ge(b_p, p * (2 * NT) + (HEAD + 2 * u + 2))
                dve.wait_ge(b_or, p * NT + (HEAD + u + 1 - NT))
                nc.vector.reciprocal(small[:, r:r + 2], small[:, l:l + 2]).then_inc(b_rc, 1)
                dve.wait_ge(b_rc, p * NT + (HEAD + u + 1))
                nc.vector.scalar_tensor_tensor(small[:, c1:c1 + 1], small[:, l:l + 1], small[:, r + 1:r + 2], neglam[:, :],
                                               ALU.mult, ALU.mult).then_inc(b_c1, 1)
                dve.wait_ge(b_c1, p * NT + (HEAD + u + 1))
                nc.vector.scalar_tensor_tensor(pr[:, u % 2, 0, 0:w], pr[:, u % 2, 1, 0:w], small[:, c1:c1 + 1],
                                               pr[:, u % 2, 0, 0:w], ALU.mult, ALU.add).then_inc(b_w, 1)

            def pair_b(p, b, more):
                for u in range(NT):
                    combine(p, u)
                    if u == 2 and more:
                        g_low(1, p + 1, 1 - b)
                    if u < 2:
                        maxes(p, u + 2)
                    elif more:
                        maxes(p + 1, u - 2)

            maxes(0, 0)
            g_low(1, 0, 0)
            for idx in range(len(HALVES[1])):
                read_group("q2b", idx, qbT)
            maxes(0, 1)
            with dve.Fori(0, PAIRS // 2 - 1) as it:
                for b in range(2):
                    pair_b(it * 2 + b, b, True)
            pair_b(PAIRS - 2, 0, True)
            pair_b(PAIRS - 1, 1, False)

            def soft_s(s):
                for g in range(2):
                    dve.wait_ge(d_s, s * 2 + (HEAD + g + 1))
                    nc.vector.tensor_reduce(small[:, 16 + g:17 + g], ps[2 + g][:, 0:KEYS], AX.X, ALU.max).then_inc(d_mx, 1)
                    dve.wait_ge(d_mx, s * 2 + (HEAD + g + 1))
                    nc.vector.tensor_scalar(small[:, 18 + g:19 + g], small[:, 16 + g:17 + g], -SCALE, None, ALU.mult)\
                        .then_inc(d_nb, 1)
                for g in range(2):
                    dve.wait_ge(d_p, s * 2 + (HEAD + g + 1))
                    nc.vector.reciprocal(small[:, 22 + g:23 + g], small[:, 20 + g:21 + g]).then_inc(d_rc, 1)
                    dve.wait_ge(d_rc, s * 2 + (HEAD + g + 1))
                    nc.vector.tensor_tensor(small[:, 24 + g:25 + g], small[:, 22 + g:23 + g], sgn[:, :], ALU.mult)\
                        .then_inc(d_rs, 1)
                    dve.wait_ge(d_rs, s * 2 + (HEAD + g + 1))
                    nc.vector.tensor_scalar(cmat[:, g, :], const[:, C_PAIR + P * g:C_PAIR + P * (g + 1)],
                                            small[:, 24 + g:25 + g], None, ALU.mult).then_inc(d_cm, 1)

            def head_sums(t):
                dve.wait_ge(s_osq, t + (HEAD + 1))
                out = osum[:, bass.ts(t, PAIRS)]
                nc.vector.tensor_reduce(out, osq.rearrange("p c (h e) -> p c h e", e=P), AX.X, ALU.add).then_inc(s_oss, 1)

            dve.wait_ge(b_or, HEAD + NT * PAIRS)
            read_k(ktcb, d_kt, d_krV, 0, 0)
            soft_s(0)
            with dve.Fori(0, NSEQ // 2 - 1) as it:
                for b in range(2):
                    read_k(ktcb, d_kt, d_krV, it * 2 + (b + 1), 1 - b)
                    soft_s(it * 2 + (b + 1))
                    if b == 0:
                        head_sums(it)
            read_k(ktcb, d_kt, d_krV, NSEQ - 1, 1)
            soft_s(NSEQ - 1)
            head_sums(NT - 1)

            def head_variance(c0, c1):
                dve.wait_ge(s_oss, HEAD + c1)
                c = slice(PAIRS * c0, PAIRS * c1)
                nc.vector.tensor_scalar(osum[:, c], osum[:, c], 1.0 / P, EPS, ALU.mult, ALU.add).then_inc(s_ov, 1)

            def head_norm(n, c0, c1):
                c = slice(PAIRS * c0, PAIRS * c1)
                dve.wait_ge(s_osr, n)
                link(nc.vector.reciprocal(osum[:, c], osum[:, c]))
                for t in range(c0, c1):
                    o3 = obuf[:, t, :].rearrange("p (h e) -> p h e", h=PAIRS)
                    rms = osum[:, PAIRS * t:PAIRS * (t + 1)].unsqueeze(2).to_broadcast([P, PAIRS, P])
                    nc.vector.tensor_tensor(o3, o3, rms, ALU.mult).then_inc(s_og, 1)

            def gate_groups(groups):
                for n, grp in groups:
                    dve.wait_ge(s_tr, n + 1)
                    dve.wait_ge(s_gact, KT + (KT if grp[0] == "s" else grp[1] + 1))
                    nc.vector.scalar_tensor_tensor(tr_dst(gT, grp), tr_bank(n, grp), subs[:, 0:1], tr_dst(gT, grp),
                                                   ALU.mult, ALU.mult).then_inc(s_trV, 1)

            head_variance(0, NT)
            head_norm(1, 0, NT)
            w_low(SL * YB)
            og = tr_of["og"]
            gate_groups(og[0:2])
            h_low("yb", 0)
            gate_groups(og[2:3])
            h_low("yb", 1)
            w_low(SL * YB + 1)
            gate_groups(og[3:4])
            h_low("yb", 2)
            gate_groups(og[4:6])
            head_sums(NT)
            head_variance(NT, TT)
            h_low("yb", 3)
            gate_groups(og[6:8])
            h_low("yb", 4)
            head_norm(2, NT, TT)
            gate_groups(og[8:10])
            for j in range(2):
                dve.wait_ge(s_hhs, j + 1)
                part = (slice(None), slice(4 * j, 4 * j + 4), slice(SEQ, TOK))
                nc.vector.tensor_tensor(hlo[part], gT[part], hhi[part].bitcast(F32), ALU.subtract).then_inc(s_hls, 1)
            for k in (5, 6, 7):
                h_low("yb", k)
            stream(YB, len(chunks), 2)
            residual(1, NT)

        @block.tensor
        def _(pe):
            for s in (a_z, a_t, a_av, c_kt, c_z, c_t, c_av, c_ot, b_s, b_t, b_o, d_kt, d_s, d_wt, d_o, *s_g):
                pe.sem_inc(s, HEAD)
            mm, tp = nc.tensor.matmul, nc.tensor.transpose

            def parts(out, a, w, start, stop):
                (ah, al), (wh, wl) = a, w
                mm(out, ah, wh, start=start, stop=False)
                mm(out, ah, wl, start=False, stop=False)
                return mm(out, al, wh, start=False, stop=stop)

            def second(n):
                pos, r = tasks[n]
                pe.wait_ge(s_msum, sum_of(pos) + 1)
                if n:
                    pe.wait_ge(s_mdone, n)
                m, c, bank = msum(sum_of(pos)), mods[order[pos]][2], mod_bank(n)
                rows = slice(0, P) if pos < 4 else slice(HD * (pos % 2), HD * (pos % 2) + HD)
                if c < 4:
                    for f in range(4):
                        last = mm(bank[:, ROWS * f:ROWS * (f + 1)], m[rows, P * f:P * (f + 1)],
                                  const[rows, C_SEL:C_SEL + ROWS], start=True, stop=True)
                else:
                    c0 = (C_EXP, C_EXS)[r]
                    last = mm(bank[:, :], const[rows, c0:c0 + P], m[rows], start=True, stop=True)
                last.then_inc(s_mout, 1)

            def first_mod(n):
                pe.wait_ge(s_first[n], 16)
                if n == 3:
                    pe.wait_ge(s_mdone, 3)
                for kk in range(2):
                    for j in range(4):
                        last = mm(sum_bank(n)[32 * j:32 * j + 32, :], cT[:, 4 * kk + j, :], first[n][:, 4 * kk + j, :],
                                  start=kk == 0, stop=kk == 1)
                last.then_inc(s_macc, 1)

            def side_mods(ci, s):
                n = SL * ci + s
                if s == 0 and ci:
                    pe.wait_ge(s_msum, 4 + ci)
                for b in range(2):
                    pe.wait_ge(s_mw[b], 16 * (n + 1))
                    for kk in range(2):
                        j = 2 * b + kk
                        last = mm(ps[5][32 * j:32 * j + 32, :], cT[:, 2 * s + kk, :], mraw[b][:, kk, :],
                                  start=s == 0, stop=s == SL - 1, skip_group_check=True)
                last.then_inc(s_mu, 1)

            def turn(stage, idx):
                src = tr_src[stage]
                n, (kind, k) = tr_of[stage][idx]
                same = [m for m in range(n) if uses[m][1] == uses[n][1]]
                if same:
                    wait_tr_read(pe, same[-1])
                if stage == "og":
                    pe.wait_ge(s_og, NT if kind == "p" else TT)
                for b in range(4):
                    t, f = (b, k) if kind == "p" else (NT, 4 * k + b)
                    if stage in ("xa", "xb"):
                        ready, mine = (s_xh, NORM_DVE) if t in NORM_DVE else (s_xhA, NORM_ACT)
                        pe.wait_ge(ready, len(mine) * int(stage == "xb") + mine.index(t) + 1)
                    last = tp(ps[uses[n][1]][:, P * b:P * (b + 1)], src[:, t, P * f:P * (f + 1)], ident)
                last.then_inc(s_tr, 1)

            tr_src = {"xa": xh, "ka": knat, "q1a": qnat, "q2a": qnat, "xb": xh2, "kb": kbn, "q1b": qbn, "q2b": qbn, "og": obuf}
            natural_ready = {"ka": lambda: wait_chunk_read(pe, A0 + 1), "q1a": lambda: wait_chunk_read(pe, YA - 2),
                             "kb": lambda: pe.wait_ge(s_rot, 1), "q1b": lambda: pe.wait_ge(s_rot, 2)}

            def project(ci, name):
                steps = [(k, t) for k in range(KT) for t in range(TT)]
                if ci >= YA:
                    steps[-2 * TT:] = [(k, t) for t in range(TT) for k in (KT - 2, KT - 1)]
                if ci == YB:
                    late = [(k, NT) for k in range(KT // 2)]
                    early = [(k, t) for k in range(KT // 2) for t in range(NT)]
                    steps = early + late + steps[TT * KT // 2:]
                for k, t in steps:
                    s, kk = divmod(k, 2)
                    n = SL * ci + s
                    if t == 0:
                        if kk == 0:
                            pe.wait_ge(s_wlo, n + 1)
                        for stage, idx in beside.get((ci, k), []):
                            if idx == 0:
                                natural_ready[stage]()
                            turn(stage, idx)
                        pe.wait_ge(s_hlo, H_BASE[name] + k + 1)
                    if ci == A0:
                        if (k, t) == (1, 0):
                            wait_tr_read(pe, tr_of["xa"][3][0])
                            first_mod(2)
                        elif (k, t) == (2, 0):
                            second(2)
                        elif (k, t) == (2, 3):
                            first_mod(3)
                        elif (k, t) == (3, 1):
                            second(3)
                        elif (k, t) == (3, 4):
                            pe.wait_ge(s_mdone, 4)
                            turn("xa", 6)
                    if t == NT and name == "yb":
                        pe.wait_ge(s_hls, k // 4 + 1)
                    if k == 0 and ci:
                        wait_read(pe, ci - 1, t)
                    w = [whl[:, n % 2, a, :].rearrange("p (k n) -> p k n", k=2)[:, kk, :] for a in range(2)]
                    tt = slice(P * t, P * (t + 1))
                    last = parts(ps[t][:, :], (hhi[:, k, tt], hlo[:, k, tt]), w, k == 0, k == KT - 1)
                    if k == KT - 1:
                        last.then_inc(s_pj, 1)
                    if kk == 0 or t < NT:
                        continue
                    if s < SL - 1:
                        last.then_inc(s_wu, 1)
                    if ci < YA:
                        side_mods(ci, s)
                    todo = tasks_of(ci - 1) if ci < YA else []
                    if s < len(todo):
                        if todo[s] == 4:
                            wait_stage_read(pe, "xa")
                        second(todo[s])

            pe.wait_ge(s_silu_c, 1)
            pe.wait_ge(s_const, 16)
            first_mod(0)
            second(0)
            first_mod(1)
            turn("xa", 0)
            turn("xa", 1)
            second(1)
            turn("xa", 2)
            turn("xa", 3)
            for ci in range(A0, YA):
                project(ci, "xa")
            for n in tasks_of(YA - 1):
                second(n)

            def gate(l, p, b, n):
                half, kq = divmod(n, 4)
                if n == 0:
                    pe.wait_ge(s_glo[l], p + (HEAD + 1))
                if kq == 0:
                    pe.wait_ge(s_gr[l], p * 2 + (HEAD + half))
                w = [whl[:, b, a, :].rearrange("p (k n) -> p k n", k=KT) for a in range(2)]
                for k in (2 * kq, 2 * kq + 1):
                    tt = slice(320 * half, 320 * (half + 1))
                    last = parts(ps[7][:, 0:320], (w[0][:, k, :], w[1][:, k, :]), (hhi[:, k, tt], hlo[:, k, tt]),
                                 k == 0, k == KT - 1)
                if kq == 3:
                    last.then_inc(s_g[l], 1)

            pe.wait_ge(s_mdone, len(tasks))
            pe.wait_ge(s_maskb, 1)
            wait_chunk_read(pe, YA - 1)
            wait_stage_read(pe, "q1a")
            pe.wait_ge(s_zero, 4)

            def scores_a(p, b, u):
                h, q = UNITS[u]
                w = P * (q + 1)
                if u < 2:
                    pe.wait_ge(a_qz, p * 2 + (HEAD + u + 1))
                pe.wait_ge(a_sig, p * 8 + (HEAD + u - 3))
                mm(ps[u % 4][:, 0:w], qz[:, b, h, P * q:P * (q + 1)], kT[:, p, 0:w], start=True, stop=True)
                mm(ps[u % 4][:, P * q:w], identb, mask_sb, start=False, stop=True, skip_group_check=True).then_inc(a_z, 1)

            def turn_a(p, u):
                h, q = UNITS[u]
                pe.wait_ge(a_mul, p * 8 + (HEAD + u + 1))
                pe.wait_ge(a_at, p * 8 + (HEAD + u - 1))
                for j in range(q + 1):
                    last = tp(ps[4 + u % 2][:, P * j:P * (j + 1)], beta[:, u % 4, P * j:P * (j + 1)], ident)
                last.then_inc(a_t, 1)

            def values_a(p, b):
                pe.wait_ge(a_at, p * 8 + (HEAD + 8))
                pe.wait_ge(a_vst, p + (HEAD + 1))
                pe.wait_ge(a_or, p + HEAD)
                for j in range(NT):
                    for h in range(2):
                        last = mm(ps[6][HD * h:HD * (h + 1), P * j:SEQ], vst[:, b, j, HD * h:HD * (h + 1)],
                                  AT[:, h, j, P * j:SEQ], start=j == 0, stop=True, skip_group_check=True)
                last.then_inc(a_av, 1)

            def pair_a(p, b, more):
                for u in range(4):
                    scores_a(p, b, u + 4)
                    turn_a(p, u)
                    gate(0, p, b, u)
                for u in range(4):
                    if more:
                        scores_a(p + 1, 1 - b, u)
                    turn_a(p, u + 4)
                    gate(0, p, b, u + 4)
                values_a(p, b)

            for u in range(4):
                scores_a(0, 0, u)
            for idx in range(len(HALVES[1])):
                turn("q2a", idx)
            wait_stage_read(pe, "q2a")
            with pe.Fori(0, PAIRS // 2 - 1) as it:
                for b in range(2):
                    pair_a(it * 2 + b, b, True)
            pair_a(PAIRS - 2, 0, True)
            pair_a(PAIRS - 1, 1, False)

            def turn_k(kcs, k_in, ready, done, s, b):
                pe.wait_ge(k_in[b], (s - b) * 8 + 16)
                for c in range(4):
                    pe.wait_ge(done[c % 2], s * 2 + (HEAD + c // 2))
                    for a in range(2):
                        for k in range(PK):
                            last = tp(ps[c % 2][:, PAST * a + P * k:PAST * a + P * (k + 1)],
                                      kcs[b][:, k, P * (2 * c + a):P * (2 * c + a + 1)], ident)
                    last.then_inc(ready, 1)

            def scores_s(s, ktcs, b, q, k_read, staged, ready, free, add_mask):
                for k_r in k_read:
                    pe.wait_ge(k_r, s * 2 + (HEAD + 2))
                pe.wait_ge(staged, s * 3 + (HEAD + 3))
                for g in range(2):
                    pe.wait_ge(free, s * 2 + (HEAD + g - 1))
                    for j in range(4):
                        last = mm(ps[2 + g][32 * j:32 * j + 32, 0:KEYS], q[:, 4 * g + j, :], ktcs[b][:, 4 * g + j, :],
                                  start=True, stop=True, skip_group_check=True)
                    if add_mask:
                        last = mm(ps[2 + g][:, PAST:KEYS], identb, mask_new, start=False, stop=True, skip_group_check=True)
                    last.then_inc(ready, 1)

            def turn_o(s, b):
                pe.wait_ge(c_or, s + (HEAD + 1))
                pe.wait_ge(c_od, s + HEAD)
                for g in range(2):
                    last = tp(ps[7][:, P * g:P * (g + 1)], so[:, b, P * g:P * (g + 1)], ident)
                last.then_inc(c_ot, 1)

            def sample_a(s, b, more, first=False):
                if more:
                    turn_k(kc, c_k, c_kt, (c_krA, c_krV), s + 1, 1 - b)
                if not first:
                    turn_o(s - 1, 1 - b)
                for g in range(2):
                    pe.wait_ge(c_mul, s * 2 + (HEAD + g + 1))
                    pe.wait_ge(c_at, s * 2 + (HEAD + g - 1))
                    for k in range(3):
                        w = P if k < 2 else NEW
                        last = tp(ps[4 + g][0:w, P * k:P * (k + 1)], sbeta[:, g, P * k:P * k + w], ident)
                    last.then_inc(c_t, 1)
                if more:
                    scores_s(s + 1, ktc, 1 - b, qb, (c_krA, c_krV), c_q, c_z, c_sig, True)
                pe.wait_ge(c_v[b], (s - b) * 8 + 16)
                pe.wait_ge(c_vn[b], (s - b) * 8 + 16)
                pe.wait_ge(c_or, s + HEAD)
                for g in range(2):
                    pe.wait_ge(c_at, s * 2 + (HEAD + g + 1))
                    for k in range(3):
                        w = P if k < 2 else NEW
                        for j in range(4):
                            pair = slice(P * (4 * g + j), P * (4 * g + j + 1))
                            v_ = vc[b][:, k, pair] if k < 2 else vnew[b][0:NEW, pair]
                            last = mm(ps[6][32 * j:32 * j + 32, P * g:P * (g + 1)], sAT[0:w, g, k, 32 * j:32 * j + 32], v_,
                                      start=k == 0, stop=k == 2, skip_group_check=True)
                last.then_inc(c_av, 1)

            pe.wait_ge(s_gr[0], HEAD + 2 * PAIRS)
            pe.wait_ge(a_or, HEAD + PAIRS)
            turn_k(kc, c_k, c_kt, (c_krA, c_krV), 0, 0)
            scores_s(0, ktc, 0, qb, (c_krA, c_krV), c_q, c_z, c_sig, True)
            sample_a(0, 0, True, first=True)
            sample_a(1, 1, True)
            with pe.Fori(1, NSEQ // 2 - 1) as it:
                for b in range(2):
                    sample_a(it * 2 + b, b, True)
            sample_a(NSEQ - 2, 0, True)
            sample_a(NSEQ - 1, 1, False)
            turn_o(NSEQ - 1, 1)

            pe.wait_ge(c_at, HEAD + 2 * NSEQ)
            pe.wait_ge(c_krA, HEAD + 2 * NSEQ)
            pe.wait_ge(c_krV, HEAD + 2 * NSEQ)
            for ci in range(YA, B0):
                project(ci, "ya")
            for idx in range(5):
                turn("xb", idx)
            for ci in range(B0, YB):
                project(ci, "kv" if ci < B0 + 4 else "b")
            wait_chunk_read(pe, YB - 1)

            wait_stage_read(pe, "q1b")
            pe.wait_ge(s_zero, 9)

            def scores_b(p, b, u):
                q = NT - 1 - u
                w = P * (q + 1)
                if u == 0:
                    pe.wait_ge(b_qz, p * 2 + (HEAD + 2))
                pe.wait_ge(b_p, p * (2 * NT) + (HEAD + 2 * u - 2))
                for c in range(2):
                    mm(ps[2 * (u % 2) + c][:, 0:w], qz[:, b, c, P * q:P * (q + 1)], kbT[:, p, 0:w], start=True, stop=True)
                    last = mm(ps[2 * (u % 2) + c][:, P * q:w], identb, mask_da, start=False, stop=True, skip_group_check=True)
                last.then_inc(b_s, 1)

            def turn_b(p, u):
                pe.wait_ge(b_w, p * NT + (HEAD + u + 1))
                pe.wait_ge(b_wt, p * NT + (HEAD + u - 1))
                for j in range(NT - u):
                    last = tp(ps[4 + u % 2][:, P * j:P * (j + 1)], pr[:, u % 2, 0, P * j:P * (j + 1)], ident)
                last.then_inc(b_t, 1)

            def values_b(p, u):
                pe.wait_ge(b_wt, p * NT + (HEAD + u + 1))
                pe.wait_ge(b_or, p * NT + (HEAD + u))
                for j in range(NT - u):
                    last = mm(ps[6][:, 0:P], wT[:, u % 2, P * j:P * (j + 1)], vb[:, j, bass.ts(p, P)],
                              start=j == 0, stop=j == NT - 1 - u)
                last.then_inc(b_o, 1)

            def pair_b(p, b, more):
                for u in range(NT):
                    if u < 2:
                        scores_b(p, b, u + 2)
                    elif more:
                        scores_b(p + 1, 1 - b, u - 2)
                    gate(1, p, b, 2 * u)
                    turn_b(p, u)
                    if u:
                        values_b(p, u - 1)
                    gate(1, p, b, 2 * u + 1)
                values_b(p, NT - 1)

            scores_b(0, 0, 0)
            scores_b(0, 0, 1)
            pe.wait_ge(s_rot, 3)
            for idx in range(len(HALVES[1])):
                turn("q2b", idx)
            wait_stage_read(pe, "q2b")
            with pe.Fori(0, PAIRS // 2 - 1) as it:
                for b in range(2):
                    pair_b(it * 2 + b, b, True)
            pair_b(PAIRS - 2, 0, True)
            pair_b(PAIRS - 1, 1, False)

            def sample_b(s, b, more):
                if more:
                    turn_k(kcb, d_k, d_kt, (d_krA, d_krV), s + 1, 1 - b)
                pe.wait_ge(d_cm, s * 2 + (HEAD + 2))
                pe.wait_ge(d_wtr, s + HEAD)
                for k in range(3):
                    w = P if k < 2 else NEW
                    for g in range(2):
                        last = mm(ps[4][0:w, P * k:P * (k + 1)], spr[:, g, P * k:P * k + w], cmat[:, g, :],
                                  start=g == 0, stop=g == 1)
                last.then_inc(d_wt, 1)
                if more:
                    scores_s(s + 1, ktcb, 1 - b, qbb, (d_krA, d_krV), d_q, d_s, d_p, False)
                pe.wait_ge(d_v[b], (s - b) * 16 + 32)
                pe.wait_ge(d_vn[b], (s - b) * 8 + 16)
                pe.wait_ge(d_wtr, s + (HEAD + 1))
                pe.wait_ge(d_or, s + HEAD)
                for g in range(2):
                    for k in range(3):
                        w = P if k < 2 else NEW
                        for j in range(4):
                            hh = 4 * g + j
                            v_ = vcb[b][:, k, g, P * j:P * (j + 1)] if k < 2 else vnewb[b][0:NEW, g, P * j:P * (j + 1)]
                            last = mm(ps[5][32 * j:32 * j + 32, P * g:P * (g + 1)], swT[0:w, k, NEW * hh:NEW * hh + 32], v_,
                                      start=k == 0, stop=k == 2, skip_group_check=True)
                last.then_inc(d_o, 1)

            pe.wait_ge(s_zero, 11)
            pe.wait_ge(b_or, HEAD + NT * PAIRS)
            turn_k(kcb, d_k, d_kt, (d_krA, d_krV), 0, 0)
            scores_s(0, ktcb, 0, qbb, (d_krA, d_krV), d_q, d_s, d_p, False)
            with pe.Fori(0, NSEQ // 2 - 1) as it:
                for b in range(2):
                    sample_b(it * 2 + b, b, True)
            sample_b(NSEQ - 2, 0, True)
            sample_b(NSEQ - 1, 1, False)
            pe.wait_ge(d_or, HEAD + NSEQ)
            pe.wait_ge(s_gr[1], HEAD + 2 * PAIRS)
            for idx in range(4):
                turn("og", idx)
            for ci in range(YB, len(chunks)):
                project(ci, "yb")


_OUTS = [("y_p", (1, SEQ, D)), ("y_s", (NSEQ, NEW, D)), ("ak_p", (1, 1, SEQ, 16, HD)), ("av_p", (1, 1, SEQ, 16, HD)),
         ("bk_p", (1, SEQ, 8, 2, HD)), ("bv_p", (1, SEQ, 8, P)), ("ak_s", (1, NSEQ, NEW, 16, HD)),
         ("av_s", (1, NSEQ, NEW, 16, HD)), ("bk_s", (NSEQ, NEW, 8, 2, HD)), ("bv_s", (NSEQ, NEW, 8, P))]


def kernel(**inputs):
    import concourse.bacc as _bacc
    from concourse.bass_utils import run_bass_kernel_spmd as _run

    a = {k: np.ascontiguousarray(x) for k, x in inputs.items()}

    def columns(rows):
        return np.ascontiguousarray(rows.reshape(-1, KT, P).transpose(2, 0, 1))

    direct = ["x_prompt", "x_sample", "cache_a_k", "cache_a_v", "cache_b_k", "cache_b_v", "mod_w_a", "mod_b_a", "w_in_a",
              "w_out_a", "ln_post_a", "mod_w_kv", "w_kv_b", "ln_post_b", "mod_w_b", "mod_b_b", "w_in_b", "w_out_b", "subln_b"]
    arrays = {n: a[n] for n in direct}
    arrays["cT"] = np.ascontiguousarray(columns(np.concatenate([a["c_prompt"], a["c_sample"]])).transpose(0, 2, 1))
    arrays["lnT"] = columns(np.concatenate([a["ln_pre_a"], a["ln_kv"][None], a["ln_pre_b"]]))
    arrays["biasT"] = columns(np.concatenate([a["mod_b_a"][0, :2 * D], a["mod_b_kv"], a["mod_b_b"][0, :2 * D]]))
    arrays["lam"] = np.concatenate([a["lambda_q1"], a["lambda_k1"], a["lambda_q2"], a["lambda_k2"]])
    arrays["consts"] = constant_table()
    arrays["masks"] = mask_table()
    nc = _bacc.Bacc("TRN2", target_bir_lowering=False, num_devices=1,
                    dynamic_dma_scratch_size=4096)
    ins = {n: nc.dram_tensor(f"in_{n}", x.shape, F32, kind="ExternalInput").ap() for n, x in arrays.items()}
    outs = {n: nc.dram_tensor(f"out_{n}", shape, F32, kind="ExternalOutput").ap() for n, shape in _OUTS}
    ins["x_scratch"] = nc.dram_tensor("x_scratch", (P, TT, D), F32, kind="Internal").ap()
    ins["o_scratch"] = nc.dram_tensor("o_scratch", (NSEQ, NEW, 2, 4, P), F32, kind="Internal").ap()
    build(nc, ins, outs)
    r = _run(nc, [{f"in_{n}": x for n, x in arrays.items()}], core_ids=[0])
    return tuple(r.results[0][f"out_{n}"] for n, _ in _OUTS)
```
